# Optimizing a Trainium2 kernel written in Bass

```python
import jax, jax.numpy as jnp
from jax import lax
import numpy as np

D_MODEL = 1024
BATCH = 1
SEQ = 1024
DEPTH = 1

CHUNK = 64
EPS = 1e-6

SSD_HEADS = 16
SSD_HEAD_DIM = 64
SSD_INNER = SSD_HEADS * SSD_HEAD_DIM
SSD_GROUPS = 4
SSD_HPG = SSD_HEADS // SSD_GROUPS
SSD_STATE = 128
SSD_CONV = 4
SSD_CONV_CH = SSD_INNER + 2 * SSD_GROUPS * SSD_STATE

HG_HEADS = 8
HG_KDIM = 128
HG_VDIM = 128
HG_K = HG_HEADS * HG_KDIM
HG_V = HG_HEADS * HG_VDIM

MIX_WIDTH = SSD_INNER + HG_V
IN_SIZES = (SSD_INNER, SSD_CONV_CH, SSD_HEADS, HG_K, HG_K, HG_V, HG_V)
IN_COLS = SSD_INNER + SSD_CONV_CH + SSD_HEADS + 2 * HG_K + 2 * HG_V

PEER_HEADS = 8
PEER_KEYS = 128
PEER_EXPERTS = PEER_KEYS * PEER_KEYS
PEER_TOPK = 16
PEER_QDIM = 256
PEER_HALF = PEER_QDIM // 2
PEER_BLOCK = 128

kernel_name = "hymba_ssd_hgrn2_peer_block"

def rmsnorm(x, w):
    xf = x.astype(jnp.float32)
    r = xf * lax.rsqrt(jnp.mean(xf * xf, axis=-1, keepdims=True) + EPS)
    return (r * w.astype(jnp.float32)).astype(x.dtype)

def causal_dwconv(x, w, b):
    k, c = w.shape
    y = lax.conv_general_dilated(x, w[:, None, :].astype(x.dtype), window_strides=(1,),
                                 padding=[(k - 1, 0)], dimension_numbers=('NWC', 'WIO', 'NWC'),
                                 feature_group_count=c)
    return y + b.astype(x.dtype)

def segsum_exp(a):
    n = a.shape[-1]
    cs = jnp.cumsum(a, axis=-1)
    diff = cs[..., :, None] - cs[..., None, :]
    mask = jnp.tril(jnp.ones((n, n), dtype=bool))
    return jnp.where(mask, jnp.exp(jnp.where(mask, diff, 0.0)), 0.0)

def ssd_mixer(z, xbc, dt_raw, conv_w, conv_b, dt_bias, a_log, d_skip, norm_w):
    bsz, seqlen, _ = z.shape
    nc = seqlen // CHUNK
    g, r, p, n = SSD_GROUPS, SSD_HPG, SSD_HEAD_DIM, SSD_STATE
    xbc = jax.nn.silu(causal_dwconv(xbc, conv_w, conv_b))
    xs = xbc[..., :SSD_INNER].reshape(bsz, nc, CHUNK, g, r, p)
    bm = xbc[..., SSD_INNER:SSD_INNER + g * n].reshape(bsz, nc, CHUNK, g, n)
    cm = xbc[..., SSD_INNER + g * n:].reshape(bsz, nc, CHUNK, g, n)
    dt = jax.nn.softplus(dt_raw.astype(jnp.float32) + dt_bias.astype(jnp.float32))
    a_head = -jnp.exp(a_log.astype(jnp.float32))
    dt = dt.reshape(bsz, nc, CHUNK, g, r)
    a = jnp.moveaxis(dt * a_head.reshape(g, r), 2, -1)
    xdt = xs * dt[..., None]
    a_cum = jnp.cumsum(a, axis=-1)
    decay = segsum_exp(a)
    cb = jnp.einsum('bclgn,bcsgn->bcgls', cm, bm)
    y_diag = jnp.einsum('bcgrls,bcsgrp->bclgrp', cb[:, :, :, None] * decay, xdt)
    to_end = jnp.moveaxis(jnp.exp(a_cum[..., -1:] - a_cum), -1, 2)
    states = jnp.einsum('bclgn,bclgrp->bcgrpn', bm, xdt * to_end[..., None])
    chunk_decay = jnp.exp(a_cum[..., -1])

    def step(s, inp):
        st, dec = inp
        return s * dec[..., None, None] + st, s

    s0 = jnp.zeros((bsz, g, r, p, n), states.dtype)
    _, prev = lax.scan(step, s0, (jnp.moveaxis(states, 1, 0), jnp.moveaxis(chunk_decay, 1, 0)))
    prev = jnp.moveaxis(prev, 0, 1)
    from_start = jnp.moveaxis(jnp.exp(a_cum), -1, 2)
    y_off = jnp.einsum('bclgn,bcgrpn->bclgrp', cm, prev) * from_start[..., None]
    y = y_diag + y_off + xs * d_skip.reshape(g, r)[:, :, None]
    y = y.reshape(bsz, seqlen, SSD_INNER)
    return rmsnorm(y * jax.nn.silu(z.astype(y.dtype)), norm_w)

def hgrn2_mixer(q_raw, f_raw, i_raw, g_raw, lb, norm_w):
    bsz, seqlen, _ = q_raw.shape
    nc = seqlen // CHUNK
    f = lb + (1.0 - lb) * jax.nn.sigmoid(f_raw.astype(jnp.float32))
    logf = jnp.log(f)
    k = 1.0 - f
    q = jax.nn.silu(q_raw.astype(jnp.float32))
    v = i_raw.astype(jnp.float32)
    mask = jnp.tril(jnp.ones((CHUNK, CHUNK), dtype=bool))[None, :, :, None, None]

    def chunks(t, d):
        return jnp.swapaxes(t.reshape(bsz, nc, CHUNK, HG_HEADS, d), 0, 1)

    def step(s, inp):
        qc, kc, vc, gc = inp
        gcum = jnp.cumsum(gc, axis=1)
        o_inter = jnp.einsum('blhk,bhkv->blhv', qc * jnp.exp(gcum), s)
        diff = gcum[:, :, None] - gcum[:, None, :]
        dec = jnp.where(mask, jnp.exp(jnp.where(mask, diff, 0.0)), 0.0)
        att = jnp.sum(qc[:, :, None] * kc[:, None] * dec, axis=-1)
        o_intra = jnp.einsum('blsh,bshv->blhv', att, vc)
        g_end = gcum[:, -1]
        s_new = s * jnp.exp(g_end)[..., None] + jnp.einsum(
            'bshk,bshv->bhkv', kc * jnp.exp(g_end[:, None] - gcum), vc)
        return s_new, o_inter + o_intra

    s0 = jnp.zeros((bsz, HG_HEADS, HG_KDIM, HG_VDIM), jnp.float32)
    _, o = lax.scan(step, s0, (chunks(q, HG_KDIM), chunks(k, HG_KDIM),
                               chunks(v, HG_VDIM), chunks(logf, HG_KDIM)))
    o = jnp.swapaxes(o, 0, 1).reshape(bsz, seqlen, HG_HEADS, HG_VDIM)
    gate = jax.nn.silu(g_raw.astype(jnp.float32).reshape(bsz, seqlen, HG_HEADS, HG_VDIM))
    o = rmsnorm(o, norm_w.reshape(HG_HEADS, HG_VDIM)) * gate
    return o.reshape(bsz, seqlen, HG_V)

def peer_ffn(x, w_query, sub_keys, u_table, v_table):
    bsz, seqlen, dm = x.shape
    t = bsz * seqlen
    xt = x.reshape(t, dm)
    q = (xt @ w_query).reshape(t, PEER_HEADS, 2, PEER_HALF)
    s = jnp.einsum('thpd,hpnd->thpn', q, sub_keys).astype(jnp.float32)
    s_top, i_top = lax.top_k(s, PEER_TOPK)
    cand = (s_top[:, :, 0, :, None] + s_top[:, :, 1, None, :]).reshape(t, PEER_HEADS, PEER_TOPK * PEER_TOPK)
    c_top, c_idx = lax.top_k(cand, PEER_TOPK)
    idx1 = jnp.take_along_axis(i_top[:, :, 0], c_idx // PEER_TOPK, axis=-1)
    idx2 = jnp.take_along_axis(i_top[:, :, 1], c_idx % PEER_TOPK, axis=-1)
    expert = idx1 * PEER_KEYS + idx2
    gate = jax.nn.softmax(c_top, axis=-1)

    def block(args):
        xb, eb, gb = args
        u = u_table[eb]
        hid = jax.nn.gelu(jnp.einsum('td,thkd->thk', xb, u).astype(jnp.float32), approximate=False) * gb
        return jnp.einsum('thk,thkd->td', hid.astype(xb.dtype), v_table[eb])

    nb = t // PEER_BLOCK
    out = lax.map(block, (xt.reshape(nb, PEER_BLOCK, dm),
                          expert.reshape(nb, PEER_BLOCK, PEER_HEADS, PEER_TOPK),
                          gate.reshape(nb, PEER_BLOCK, PEER_HEADS, PEER_TOPK)))
    return out.reshape(bsz, seqlen, dm)

def setup_inputs(seed: int = 0) -> dict:
    key = jax.random.key(seed)
    ks = jax.random.split(key, 20)
    f32 = jnp.float32
    nrm = lambda k, shape, sc: jax.random.normal(k, shape, f32) * sc
    dt0 = jnp.exp(jax.random.uniform(ks[4], (DEPTH, SSD_HEADS), f32, np.log(1e-3), np.log(1e-1)))
    return {
        "x": nrm(ks[0], (BATCH, SEQ, D_MODEL), 1.0),
        "ln_mix_w": 1.0 + nrm(ks[1], (DEPTH, D_MODEL), 0.05),
        "w_in": nrm(ks[2], (DEPTH, D_MODEL, IN_COLS), D_MODEL ** -0.5),
        "conv_w": nrm(ks[3], (DEPTH, SSD_CONV, SSD_CONV_CH), SSD_CONV ** -0.5),
        "conv_b": nrm(ks[5], (DEPTH, SSD_CONV_CH), 0.02),
        "dt_bias": dt0 + jnp.log(-jnp.expm1(-dt0)),
        "a_log": jnp.log(jax.random.uniform(ks[6], (DEPTH, SSD_HEADS), f32, 1.0, 16.0)),
        "d_skip": 1.0 + nrm(ks[7], (DEPTH, SSD_HEADS), 0.1),
        "ssd_norm_w": 1.0 + nrm(ks[8], (DEPTH, SSD_INNER), 0.05),
        "lb_logits": 1.0 + nrm(ks[9], (DEPTH + 1, HG_K), 0.1),
        "hg_norm_w": 1.0 + nrm(ks[10], (DEPTH, HG_V), 0.05),
        "w_out": nrm(ks[11], (DEPTH, MIX_WIDTH, D_MODEL), MIX_WIDTH ** -0.5),
        "ln_ffn_w": 1.0 + nrm(ks[12], (DEPTH, D_MODEL), 0.05),
        "w_query": nrm(ks[13], (DEPTH, D_MODEL, PEER_HEADS * PEER_QDIM), D_MODEL ** -0.5),
        "sub_keys": nrm(ks[14], (DEPTH, PEER_HEADS, 2, PEER_KEYS, PEER_HALF), PEER_HALF ** -0.5),
        "u_table": nrm(ks[15], (DEPTH, PEER_EXPERTS, D_MODEL), D_MODEL ** -0.5),
        "v_table": nrm(ks[16], (DEPTH, PEER_EXPERTS, D_MODEL), 0.5),
        "ln_final_w": 1.0 + nrm(ks[17], (D_MODEL,), 0.05),
    }

def reference(x, ln_mix_w, w_in, conv_w, conv_b, dt_bias, a_log, d_skip, ssd_norm_w,
              lb_logits, hg_norm_w, w_out, ln_ffn_w, w_query, sub_keys, u_table, v_table,
              ln_final_w):
    split_at = [int(v) for v in np.cumsum(IN_SIZES)[:-1]]
    lb_all = jnp.cumsum(jax.nn.softmax(lb_logits.astype(jnp.float32), axis=0), axis=0)
    h = x
    for l in range(DEPTH):
        hn = rmsnorm(h, ln_mix_w[l])
        proj = hn @ w_in[l]
        z, xbc, dt_raw, q_raw, f_raw, i_raw, g_raw = jnp.split(proj, split_at, axis=-1)
        y_ssd = ssd_mixer(z, xbc, dt_raw, conv_w[l], conv_b[l], dt_bias[l], a_log[l],
                          d_skip[l], ssd_norm_w[l])
        y_hg = hgrn2_mixer(q_raw, f_raw, i_raw, g_raw, lb_all[l], hg_norm_w[l])
        mix = jnp.concatenate([y_ssd.astype(h.dtype), y_hg.astype(h.dtype)], axis=-1)
        h = h + mix @ w_out[l]
        h = h + peer_ffn(rmsnorm(h, ln_ffn_w[l]), w_query[l], sub_keys[l], u_table[l], v_table[l])
    return rmsnorm(h, ln_final_w)


_drawn_inputs = setup_inputs


def setup_inputs(seed=0):
    import zlib

    import numpy as np

    out = dict(_drawn_inputs(seed))
    spreads = {}
    factors = {'lb_logits': 4.035}
    for name, (base, spread) in spreads.items():
        noise = np.random.default_rng([zlib.crc32(name.encode()), seed]).standard_normal(out[name].shape)
        drawn = base * np.exp(spread * noise) if base else spread * noise
        out[name] = __import__('jax').numpy.asarray(drawn.astype(out[name].dtype))
    for name, factor in factors.items():
        out[name] = (out[name] * factor).astype(out[name].dtype)
    return out
```

```python
from contextlib import ExitStack

import concourse.bass as bass
from concourse import mybir

ALU = mybir.AluOpType
ACT = mybir.ActivationFunctionType
AX = mybir.AxisListType
F32 = mybir.dt.float32
U32 = mybir.dt.uint32

P = 128
SEQ, D = 1024, 1024
NB = SEQ // P
KT = D // P
EPS = 1e-6

GROUPS, HPG, HD = 4, 4, 64
XW = HPG * HD
CT = 4
TAPS = 4
SSD_COLS = CT * P + XW + HPG
SSD_PIECES = 2 * CT + NB
NPAR = CT * (TAPS + 1) + 3 * HPG
DTB, ALG, DSK = CT * (TAPS + 1), CT * (TAPS + 1) + HPG, CT * (TAPS + 1) + 2 * HPG

HEADS = 8
HG_COLS = 4 * P
HG_PIECES = 4 + NB
LEVELS = 7
MIX = 2 * D
MT = MIX // P

PH, TOPK, KEYS = 8, 16, 128
EXPERTS = KEYS * KEYS
ROWS_OF = [TOPK // (i + 1) for i in range(TOPK)]
NCAND = sum(ROWS_OF)
RING = 8
BATCH = 4
LOW = -3.0e38


class Own:

    def __init__(self, eng, sem, per=0):
        self.eng, self.sem, self.per, self.base, self.n = eng, sem, per, 0, 0

    def at(self, i):
        self.base, self.n = i * self.per, 0

    def done(self, ins):
        self.step(ins)
        self.wait()

    def step(self, ins):
        ins.then_inc(self.sem, 1)
        self.n += 1

    def wait(self):
        self.eng.wait_ge(self.sem, past(self.base + self.n))

    def check(self):
        assert self.n == self.per, (self.n, self.per)


def past(count):
    return count + 1


def prime(eng, sems):
    for s in sems:
        eng.sem_inc(s, 1)


def constants(nc, C):
    with nc.semaphore("set") as filled, nc.semaphore("cut") as cut, nc.Block() as block:

        @block.gpsimd
        def _(pool):
            nc.gpsimd.memset(C["ident"][:], 0.0)
            nc.gpsimd.memset(C["ones"][:], 1.0)
            nc.gpsimd.memset(C["tri"][:], 1.0)
            nc.gpsimd.memset(C["below"][:], 0.0)
            nc.gpsimd.memset(C["reset"][:], 1.0)
            nc.gpsimd.memset(C["lmask"][:], 1.0).then_inc(filled, 1)
            pool.wait_ge(filled, 1)
            nc.gpsimd.affine_select(out=C["ident"][:], in_=C["ident"][:], compare_op=ALU.not_equal, fill=1.0,
                                    base=0, pattern=[[-1, P]], channel_multiplier=1)
            nc.gpsimd.affine_select(out=C["tri"][:], in_=C["tri"][:], compare_op=ALU.is_ge, fill=0.0,
                                    base=0, pattern=[[1, P]], channel_multiplier=-1)
            nc.gpsimd.affine_select(out=C["below"][:], in_=C["below"][:], compare_op=ALU.is_ge, fill=-1.0e30,
                                    base=0, pattern=[[1, P]], channel_multiplier=-1)
            nc.gpsimd.affine_select(out=C["reset"][:].rearrange("p (c l) -> p c l", l=P),
                                    in_=C["reset"][:].rearrange("p (c l) -> p c l", l=P),
                                    compare_op=ALU.is_gt, fill=0.0,
                                    base=0, pattern=[[0, NB], [1, P]], channel_multiplier=0)
            n = 0
            for j in range(LEVELS):
                h = P >> (j + 1)
                m = C["lmask"][:, j, :].rearrange("p (q two r) -> p q two r", two=2, r=h)
                nq = P // (2 * h)
                nc.gpsimd.memset(m[:, :, 0, :], 0.0)
                right = m[:, :, 1, :]
                nc.gpsimd.affine_select(out=right, in_=right, compare_op=ALU.is_ge, fill=0.0, base=0,
                                        pattern=[[-2 * h, nq], [0, h]], channel_multiplier=1).then_inc(cut, 1)
                n += 1
                pool.wait_ge(cut, n)
                nc.gpsimd.affine_select(out=right, in_=right, compare_op=ALU.is_gt, fill=0.0, base=h,
                                        pattern=[[2 * h, nq], [0, h]], channel_multiplier=-1)
            nc.gpsimd.affine_select(out=C["lmask"][:, LEVELS, :], in_=C["lmask"][:, LEVELS, :],
                                    compare_op=ALU.is_equal, fill=0.0,
                                    base=0, pattern=[[-1, P]], channel_multiplier=1).then_inc(cut, 1)
            pool.wait_ge(cut, n + 1)


def input_norm(nc, x, ln_w, C, hnT):
    with ExitStack() as ctx:
        def sb(name, shape, dt=F32):
            return ctx.enter_context(nc.sbuf_tensor("nrm_" + name, shape, dt))

        primed = []

        def plain_sem(name):
            return ctx.enter_context(nc.semaphore("nrm_" + name))

        def sem(name):
            primed.append(plain_sem(name))
            return primed[-1]

        xs = sb("xs", [P, NB, D])
        sq = sb("sq", [P, D])
        ss = sb("ss", [P, NB])
        rs = sb("rs", [P, NB])
        lnw = sb("lnw", [P, KT])
        ps = ctx.enter_context(nc.psum_tensor("nrm_ps", [P, 2, 512], F32))
        x_in = [plain_sem(f"x_in{b}") for b in range(NB)]
        w_in = plain_sem("w_in")
        squared, rooted, meaned, inverse, scaled, turned, stored = (
            sem("squared"), sem("rooted"), sem("meaned"), sem("inverse"), sem("scaled"), sem("turned"),
            sem("stored"))
        xd = x.rearrange("o (b p) d -> p (o b) d", p=P)
        block = ctx.enter_context(nc.Block())

        @block.sync
        def _(sp):
            prime(sp, primed)
            sp.dma_start(lnw[:], ln_w).then_inc(w_in, 16)
            for b in range(NB):
                sp.dma_start(xs[:, b, :], xd[:, b, :]).then_inc(x_in[b], 16)

        @block.scalar
        def _(act):
            act.wait_ge(w_in, 16)
            for b in range(NB):
                act.wait_ge(x_in[b], 16)
                if b >= 1:
                    act.wait_ge(squared, past(b))
                nc.scalar.activation(sq[:], xs[:, b, :], ACT.Square, accum_out=ss[:, b:b + 1]).then_inc(squared, 1)
            act.wait_ge(meaned, past(1))
            nc.scalar.activation(rs[:], ss[:], ACT.Sqrt).then_inc(rooted, 1)
            for n in range(2 * KT):
                act.wait_ge(turned, past(n + 1))
                k, half = n // 2, n % 2
                nc.scalar.activation(hnT[:, k, half * 512:half * 512 + 512], ps[:, n % 2, :], ACT.Copy,
                                     scale=lnw[:, k:k + 1]).then_inc(stored, 1)

        @block.vector
        def _(dve):
            dve.wait_ge(squared, past(NB))
            nc.vector.tensor_scalar(ss[:], ss[:], 1.0 / D, EPS, ALU.mult, ALU.add).then_inc(meaned, 1)
            dve.wait_ge(rooted, past(1))
            nc.vector.reciprocal(rs[:], rs[:]).then_inc(inverse, 1)
            dve.wait_ge(inverse, past(1))
            for b in range(NB):
                nc.vector.tensor_scalar(xs[:, b, :], xs[:, b, :], rs[:, b:b + 1], None, ALU.mult).then_inc(scaled, 1)

        @block.tensor
        def _(pe):
            for n in range(2 * KT):
                k, half = n // 2, n % 2
                pe.wait_ge(scaled, past(4 * half + 4 if n < 2 else NB))
                if n >= 2:
                    pe.wait_ge(stored, past(n - 1))
                for j in range(4):
                    mm = nc.tensor.transpose(ps[:, n % 2, j * P:(j + 1) * P],
                                             xs[:, 4 * half + j, k * P:(k + 1) * P], C["ident"][:])
                mm.then_inc(turned, 1)


def ssd(nc, w_ssd, par, C, hnT, Y):
    with ExitStack() as ctx:
        def sb(name, shape, dt=F32):
            return ctx.enter_context(nc.sbuf_tensor("ssd_" + name, shape, dt))

        primed = []

        def plain_sem(name):
            return ctx.enter_context(nc.semaphore("ssd_" + name))

        def sem(name):
            primed.append(plain_sem(name))
            return primed[-1]

        def psum(name, shape):
            return ctx.enter_context(nc.psum_tensor("ssd_" + name, shape, F32))

        PAD = TAPS - 1
        w = sb("w", [P, KT, SSD_COLS])
        pr = sb("pr", [P, GROUPS, NPAR])
        ah = sb("ah", [P, GROUPS, HPG])
        raw = sb("raw", [P, CT, PAD + SEQ])
        rawz = sb("rawz", [P, NB, XW + HPG])
        xc = sb("xc", [P, CT, SEQ])
        zs = sb("zs", [P, NB, XW])
        sp5 = sb("sp5", [P, 5, NB, HPG])
        dt = sb("dt", [P, NB, HPG])
        a = sb("a", [P, NB, HPG])
        acum = sb("acum", [P, NB, HPG])
        aend = sb("aend", [P, NB, HPG])
        from_start = sb("from_start", [P, NB, HPG])
        to_end = sb("to_end", [P, NB, HPG])
        decay_all = sb("decay_all", [P, NB, HPG])
        awide = sb("awide", [P, HPG, P])
        natural = sb("natural", [P, 3 * P])
        dec = sb("dec", [P, HPG, P])
        att = sb("att", [P, HPG, P])
        xdt = sb("xdt", [P, HPG, HD])
        xdte = sb("xdte", [P, HPG, HD])
        y = sb("y", [P, HPG, HD])
        skip = sb("skip", [P, HPG, HD])
        state = sb("state", [P, HPG, HD])

        ps_piece = psum("ps_piece", [P, 2, 512])
        ps_cb = psum("ps_cb", [P, 512])
        ps_turn = psum("ps_turn", [P, 512])
        ps_rows = psum("ps_rows", [P, HPG, P])
        ps_y = psum("ps_y", [P, 2, HPG, HD])
        ps_state = psum("ps_state", [P, 512])
        ps_sum = psum("ps_sum", [P, 512])

        par_in, w_in = plain_sem("par_in"), plain_sem("w_in")
        padded = sem("padded")
        piece_made, piece_out = sem("piece_made"), sem("piece_out")
        raw_used = sem("raw_used")
        convolved, activated = sem("convolved"), sem("activated")
        z_activated = sem("z_activated")
        dt_raw, dt_exp, dt_onep, dt_log, dt_ready = (sem("dt_raw"), sem("dt_exp"), sem("dt_onep"),
                                                     sem("dt_log"), sem("dt_ready"))
        summed, sums_out, exps_ready = sem("summed"), sem("sums_out"), sem("exps_ready")
        a_logged = sem("a_logged")
        wide_ready = sem("wide_ready")
        stage_a, natural_out = sem("stage_a"), sem("natural_out")
        diff_ready, dec_ready, att_ready = sem("diff_ready"), sem("dec_ready"), sem("att_ready")
        stage_b, chunk_done = sem("stage_b"), sem("chunk_done")
        dve_own = sem("dve_own")
        state_ready = sem("state_ready")
        block = ctx.enter_context(nc.Block())

        def cols(c):
            return slice(c * P, (c + 1) * P)

        @block.sync
        def _(sp):
            prime(sp, primed)
            sp.dma_start(pr[:], par).then_inc(par_in, 16)
            sp.dma_start(w[:], w_ssd[0]).then_inc(w_in, 16)
            with sp.Fori(1, GROUPS) as u:
                sp.wait_ge(piece_made, past(u * SSD_PIECES))
                sp.dma_start(w[:], w_ssd[bass.ds(u, 1)].rearrange("o p k c -> p (o k) c")).then_inc(w_in, 16)

        @block.gpsimd
        def _(pool):
            nc.gpsimd.memset(raw[:, :, 0:PAD], 0.0).then_inc(padded, 1)
            with pool.Fori(0, GROUPS) as u:
                for c in range(NB):
                    if c == 0:
                        pool.wait_ge(dt_ready, past(u + 1))
                    pool.wait_ge(stage_a, past(u * NB + c))
                    nc.gpsimd.tensor_tensor(awide[:], a[:, c, :].unsqueeze(2).to_broadcast([P, HPG, P]),
                                            C["ones"][:].unsqueeze(1).to_broadcast([P, HPG, P]),
                                            ALU.mult).then_inc(wide_ready, 1)

        def group(pe_u, parts):
            return [list(range(2 * c, 2 * c + 2)) for c in range(NB)]

        @block.tensor
        def _(pe):
            def piece(u, p):
                if p == 0:
                    pe.wait_ge(w_in, (u + 1) * 16)
                if not (isinstance(u, int) and u == 0 and p < 2):
                    pe.wait_ge(piece_out, past(u * SSD_PIECES + p - 1))
                bank = ps_piece[:, p % 2, :]
                for k in range(KT):
                    if p < 2 * CT:
                        i, half = p // 2, p % 2
                        mm = nc.tensor.matmul(bank, w[:, k, i * P:(i + 1) * P],
                                              hnT[:, k, half * 512:(half + 1) * 512],
                                              start=(k == 0), stop=(k == KT - 1))
                    else:
                        mm = nc.tensor.matmul(bank[:, 0:XW + HPG], hnT[:, k, cols(p - 2 * CT)],
                                              w[:, k, CT * P:SSD_COLS], start=(k == 0), stop=(k == KT - 1))
                mm.then_inc(piece_made, 1)

            def mix(u, more):
                pe.wait_ge(dt_ready, past(u + 1))
                pe.wait_ge(sums_out, past(2 * u))
                av = a[:].rearrange("p c r -> p (c r)")
                nc.tensor.matmul(ps_sum[:, 0:NB * HPG], C["tri"][:], av, start=True, stop=True)
                nc.tensor.matmul(ps_sum[:, NB * HPG:2 * NB * HPG], C["ones"][:], av,
                                 start=True, stop=True).then_inc(summed, 1)
                pe.wait_ge(activated, past(u * CT + CT))
                for c in range(NB):
                    pe.wait_ge(wide_ready, past(u * NB + c + 1))
                    pe.wait_ge(att_ready, past(u * NB + c))
                    nc.tensor.matmul(ps_cb[:, 0:P], xc[:, 2, cols(c)], xc[:, 3, cols(c)], start=True, stop=True)
                    for i in range(3):
                        nc.tensor.transpose(ps_turn[:, i * P:(i + 1) * P], xc[:, i, cols(c)], C["ident"][:])
                    for r in range(HPG):
                        mm = nc.tensor.matmul(ps_rows[:, r, :], awide[:, r, :], C["tri"][:], start=True, stop=True)
                    mm.then_inc(stage_a, 1)
                    if more:
                        piece(u + 1, 2 * c)
                        piece(u + 1, 2 * c + 1)
                    pe.wait_ge(state_ready, past(u * NB + c + 1))
                    pe.wait_ge(chunk_done, past(u * NB + c))
                    pe.wait_ge(att_ready, past(u * NB + c + 1))
                    nc.tensor.matmul(ps_y[:, 0].rearrange("p r d -> p (r d)"), xc[:, 3, cols(c)],
                                     state[:].rearrange("p r d -> p (r d)"), start=True, stop=True)
                    for r in range(HPG):
                        nc.tensor.matmul(ps_y[:, 1, r, :], att[:, r, :], xdt[:, r, :], start=True, stop=True)
                    nc.tensor.matmul(ps_state[:, 0:XW], natural[:, 2 * P:3 * P],
                                     xdte[:].rearrange("p r d -> p (r d)"), start=True, stop=True).then_inc(stage_b, 1)

            for p in range(SSD_PIECES):
                piece(0, p)
            with pe.Fori(0, GROUPS - 1) as u:
                mix(u, True)
            mix(GROUPS - 1, False)

        @block.scalar
        def _(act):
            act.wait_ge(par_in, 16)
            act.wait_ge(padded, past(1))
            nc.scalar.activation(ah[:], pr[:, :, ALG:ALG + HPG], ACT.Exp).then_inc(a_logged, 1)

            def out(u, p):
                act.wait_ge(piece_made, past(u * SSD_PIECES + p + 1))
                if p == 0 and not (isinstance(u, int) and u == 0):
                    act.wait_ge(raw_used, past(u))
                    act.wait_ge(z_activated, past(u))
                if p < 2 * CT:
                    i, half = p // 2, p % 2
                    nc.scalar.activation(raw[:, i, PAD + half * 512:PAD + half * 512 + 512], ps_piece[:, p % 2, :],
                                         ACT.Copy).then_inc(piece_out, 1)
                else:
                    nc.scalar.activation(rawz[:, p - 2 * CT, :], ps_piece[:, p % 2, 0:XW + HPG],
                                         ACT.Copy).then_inc(piece_out, 1)

            def mix(u, more):
                act.wait_ge(dt_raw, past(u + 1))
                nc.scalar.activation(sp5[:, 1], sp5[:, 0], ACT.Abs).then_inc(dt_exp, 1)
                act.wait_ge(dt_exp, past(2 * u + 1))
                nc.scalar.activation(sp5[:, 1], sp5[:, 1], ACT.Exp, scale=-1.0).then_inc(dt_exp, 1)
                act.wait_ge(dt_onep, past(u + 1))
                nc.scalar.activation(sp5[:, 3], sp5[:, 2], ACT.Ln).then_inc(dt_log, 1)
                act.wait_ge(chunk_done, past(u * NB))
                nc.scalar.activation(zs[:], rawz[:, :, 0:XW], ACT.Silu).then_inc(z_activated, 1)
                for i in range(CT):
                    act.wait_ge(convolved, past(u * CT + i + 1))
                    nc.scalar.activation(xc[:, i, :], xc[:, i, :], ACT.Silu).then_inc(activated, 1)
                act.wait_ge(sums_out, past(2 * u + 2))
                nc.scalar.activation(from_start[:], acum[:], ACT.Exp)
                nc.scalar.activation(to_end[:], to_end[:], ACT.Exp)
                nc.scalar.activation(decay_all[:], aend[:], ACT.Exp).then_inc(exps_ready, 1)
                for c in range(NB):
                    act.wait_ge(stage_a, past(u * NB + c + 1))
                    act.wait_ge(chunk_done, past(u * NB + c))
                    nc.scalar.activation(natural[:], ps_turn[:, 0:3 * P], ACT.Copy).then_inc(natural_out, 1)
                    act.wait_ge(diff_ready, past(u * NB + c + 1))
                    nc.scalar.activation(dec[:], dec[:], ACT.Exp).then_inc(dec_ready, 1)
                    if more:
                        out(u + 1, 2 * c)
                        out(u + 1, 2 * c + 1)

            for p in range(SSD_PIECES):
                out(0, p)
            with act.Fori(0, GROUPS - 1) as u:
                mix(u, True)
            mix(GROUPS - 1, False)

        @block.vector
        def _(dve):
            own = Own(dve, dve_own, 9 + CT * (TAPS - 1) + NB * 8)

            def mix(u):
                own.at(u)
                dve.wait_ge(piece_out, past(u * SSD_PIECES + SSD_PIECES))
                pu = pr[:, bass.ds(u, 1), :].rearrange("p o c -> p (o c)")
                ahu = ah[:, bass.ds(u, 1), :].rearrange("p o c -> p (o c)")

                def per_head(ap):
                    return ap.unsqueeze(1).to_broadcast([P, NB, HPG])

                nc.vector.tensor_tensor(sp5[:, 0], rawz[:, :, XW:XW + HPG], per_head(pu[:, DTB:DTB + HPG]),
                                        ALU.add).then_inc(dt_raw, 1)
                dve.wait_ge(dt_exp, past(2 * u + 2))
                nc.vector.tensor_scalar(sp5[:, 2], sp5[:, 1], 1.0, None, ALU.add).then_inc(dt_onep, 1)
                dve.wait_ge(dt_onep, past(u + 1))
                own.done(nc.vector.tensor_scalar(sp5[:, 4], sp5[:, 2], 1.0, None, ALU.subtract))
                own.done(nc.vector.tensor_tensor(sp5[:, 4], sp5[:, 1], sp5[:, 4], ALU.subtract))
                dve.wait_ge(dt_log, past(u + 1))
                own.done(nc.vector.reciprocal(sp5[:, 2], sp5[:, 2]))
                own.done(nc.vector.tensor_tensor(sp5[:, 4], sp5[:, 4], sp5[:, 2], ALU.mult))
                own.done(nc.vector.tensor_tensor(sp5[:, 4], sp5[:, 4], sp5[:, 3], ALU.add))
                own.done(nc.vector.scalar_tensor_tensor(out=dt[:], in0=sp5[:, 0], scalar=0.0, in1=sp5[:, 4],
                                                        op0=ALU.max, op1=ALU.add))
                own.done(nc.vector.tensor_tensor(a[:], dt[:], per_head(ahu), ALU.mult))
                nc.vector.tensor_scalar(a[:], a[:], -1.0, None, ALU.mult).then_inc(dt_ready, 1)
                if not (isinstance(u, int) and u == 0):
                    dve.wait_ge(stage_b, past(u * NB))
                for i in range(CT):
                    wi = (TAPS + 1) * i
                    own.done(nc.vector.tensor_scalar(xc[:, i, :], raw[:, i, PAD:PAD + SEQ], pu[:, wi + PAD:wi + PAD + 1],
                                                     pu[:, wi + TAPS:wi + TAPS + 1], ALU.mult, ALU.add))
                    for k in range(PAD):
                        ins = nc.vector.scalar_tensor_tensor(out=xc[:, i, :], in0=raw[:, i, k:k + SEQ],
                                                             scalar=pu[:, wi + k:wi + k + 1], in1=xc[:, i, :],
                                                             op0=ALU.mult, op1=ALU.add)
                        if k < PAD - 1:
                            own.done(ins)
                        else:
                            ins.then_inc(convolved, 1)
                dve.wait_ge(convolved, past(u * CT + CT))
                own.done(nc.vector.memset(state[:], 0.0))
                dve.sem_inc(raw_used, 1)
                dve.sem_inc(state_ready, 1)
                dve.wait_ge(summed, past(u + 1))
                n = NB * HPG
                nc.vector.tensor_copy(aend[:].rearrange("p c r -> p (c r)"), ps_sum[:, n:2 * n])
                own.done(nc.vector.tensor_copy(acum[:].rearrange("p c r -> p (c r)"), ps_sum[:, 0:n]))
                nc.vector.tensor_tensor(to_end[:], aend[:], acum[:], ALU.subtract).then_inc(sums_out, 1)
                dve.sem_inc(sums_out, 1)
                dve.wait_ge(exps_ready, past(u + 1))
                for c in range(NB):
                    def wide(ap):
                        return ap[:, c, :].unsqueeze(2).to_broadcast([P, HPG, HD])

                    dve.wait_ge(stage_a, past(u * NB + c + 1))
                    dve.wait_ge(stage_b, past(u * NB + c))
                    for r in range(HPG):
                        ins = nc.vector.scalar_tensor_tensor(out=dec[:, r, :], in0=ps_rows[:, r, :],
                                                             scalar=acum[:, c, r:r + 1], in1=C["below"][:],
                                                             op0=ALU.subtract, op1=ALU.min)
                    ins.then_inc(diff_ready, 1)
                    dve.wait_ge(natural_out, past(u * NB + c + 1))
                    xn = natural[:, 0:XW].rearrange("p (r d) -> p r d", r=HPG)
                    own.done(nc.vector.tensor_tensor(xdt[:], xn, wide(dt), ALU.mult))
                    nc.vector.tensor_tensor(xdte[:], xdt[:], wide(to_end), ALU.mult)
                    own.done(nc.vector.tensor_tensor(skip[:], xn, pu[:, DSK:DSK + HPG].unsqueeze(2).to_broadcast([P, HPG, HD]),
                                                     ALU.mult))
                    dve.wait_ge(dec_ready, past(u * NB + c + 1))
                    nc.vector.tensor_tensor(att[:], dec[:], ps_cb[:, 0:P].unsqueeze(1).to_broadcast([P, HPG, P]),
                                            ALU.mult).then_inc(att_ready, 1)
                    dve.wait_ge(stage_b, past(u * NB + c + 1))
                    own.done(nc.vector.tensor_tensor(state[:], state[:], wide(decay_all), ALU.mult))
                    own.done(nc.vector.tensor_tensor(state[:], state[:],
                                                     ps_state[:, 0:XW].rearrange("p (r d) -> p r d", r=HPG), ALU.add))
                    if c < NB - 1:
                        dve.sem_inc(state_ready, 1)
                    own.done(nc.vector.tensor_tensor(y[:], ps_y[:, 0], wide(from_start), ALU.mult))
                    own.done(nc.vector.tensor_tensor(y[:], y[:], ps_y[:, 1], ALU.add))
                    own.done(nc.vector.tensor_tensor(y[:], y[:], skip[:], ALU.add))
                    own.done(nc.vector.tensor_tensor(
                        Y[:, c, bass.ds(u * XW, XW)], y[:].rearrange("p r d -> p (r d)"), zs[:, c, :], ALU.mult))
                    dve.sem_inc(chunk_done, 1)
                own.check()

            dve.wait_ge(a_logged, past(1))
            with dve.Fori(0, GROUPS) as u:
                mix(u)


def hgrn(nc, w_hg, lb_logits, C, hnT, Y):
    with ExitStack() as ctx:
        def sb(name, shape, dt=F32):
            return ctx.enter_context(nc.sbuf_tensor("hg_" + name, shape, dt))

        primed = []

        def plain_sem(name):
            return ctx.enter_context(nc.semaphore("hg_" + name))

        def sem(name):
            primed.append(plain_sem(name))
            return primed[-1]

        def psum(name, shape):
            return ctx.enter_context(nc.psum_tensor("hg_" + name, shape, F32))

        w = sb("w", [P, KT, HG_COLS])
        lbl = sb("lbl", [P, 2, HEADS])
        lb = sb("lb", [P, HEADS])
        oml = sb("oml", [P, HEADS])
        q = sb("q", [P, SEQ])
        k = sb("k", [P, SEQ])
        f = sb("f", [P, SEQ])
        G = sb("G", [P, SEQ])
        W = sb("W", [P, LEVELS, SEQ])
        qs = sb("qs", [P, SEQ])
        ke = sb("ke", [P, SEQ])
        gend = sb("gend", [P, NB])
        raw_q = sb("raw_q", [P, SEQ])
        raw_f = sb("raw_f", [P, SEQ])
        raw_vg = sb("raw_vg", [P, NB, 2 * P])
        v = sb("v", [P, NB, P])
        gs = sb("gs", [P, NB, P])
        o = sb("o", [P, NB, P])
        ss = sb("ss", [P, NB])
        rs = sb("rs", [P, NB])
        masked = sb("masked", [P, LEVELS + 1, P])
        att = sb("att", [P, P])
        ken = sb("ken", [P, P])
        state = sb("state", [P, P])

        ps_piece = psum("ps_piece", [P, 2, 512])
        ps_att = psum("ps_att", [P, LEVELS + 1, P])
        ps_turn = psum("ps_turn", [P, 512])
        ps_o = psum("ps_o", [P, 512])
        ps_state = psum("ps_state", [P, 512])

        w_in, lb_in = plain_sem("w_in"), plain_sem("lb_in")
        lb_diff, lb_ready = sem("lb_diff"), sem("lb_ready")
        piece_made, piece_out = sem("piece_made"), sem("piece_out")
        gate_sig, gate_ready, gate_logged, summed = (sem("gate_sig"), sem("gate_ready"), sem("gate_logged"),
                                                     sem("summed"))
        q_ready, v_ready, g_ready = sem("q_ready"), sem("v_ready"), sem("g_ready")
        span, decayed, weighted = sem("span"), sem("decayed"), sem("weighted")
        stage_a, stage_b = sem("stage_a"), sem("stage_b")
        ken_ready, att_ready, state_ready = sem("ken_ready"), sem("att_ready"), sem("state_ready")
        o_squared, o_out, meaned, rooted, stored = (sem("o_squared"), sem("o_out"), sem("meaned"), sem("rooted"),
                                                    sem("stored"))
        mask_done, k_ready = sem("mask_done"), sem("k_ready")
        dve_own = sem("dve_own")
        block = ctx.enter_context(nc.Block())

        def cols(c):
            return slice(c * P, (c + 1) * P)

        parts = [[p for p in range(HG_PIECES) if p * NB // HG_PIECES == c] for c in range(NB)]

        @block.sync
        def _(sp):
            prime(sp, primed)
            sp.dma_start(lbl[:], lb_logits).then_inc(lb_in, 16)
            sp.dma_start(w[:], w_hg[0]).then_inc(w_in, 16)
            with sp.Fori(1, HEADS) as u:
                sp.wait_ge(piece_made, past(u * HG_PIECES))
                sp.dma_start(w[:], w_hg[bass.ds(u, 1)].rearrange("o p k c -> p (o k) c")).then_inc(w_in, 16)

        @block.tensor
        def _(pe):
            def piece(u, p):
                if p == 0:
                    pe.wait_ge(w_in, (u + 1) * 16)
                if not (isinstance(u, int) and u == 0 and p < 2):
                    pe.wait_ge(piece_out, past(u * HG_PIECES + p - 1))
                bank = ps_piece[:, p % 2, :]
                for kt in range(KT):
                    if p < 4:
                        i, half = p // 2, p % 2
                        mm = nc.tensor.matmul(bank, w[:, kt, i * P:(i + 1) * P],
                                              hnT[:, kt, half * 512:(half + 1) * 512],
                                              start=(kt == 0), stop=(kt == KT - 1))
                    else:
                        mm = nc.tensor.matmul(bank[:, 0:2 * P], hnT[:, kt, cols(p - 4)], w[:, kt, 2 * P:4 * P],
                                              start=(kt == 0), stop=(kt == KT - 1))
                mm.then_inc(piece_made, 1)

            def mix(u, more):
                pe.wait_ge(weighted, past((u + 1) * (LEVELS + 2)))
                for c in range(NB):
                    pe.wait_ge(att_ready, past(u * NB + c))
                    pe.wait_ge(ken_ready, past(u * NB + c))
                    for j in range(LEVELS):
                        nc.tensor.matmul(ps_att[:, j, :], W[:, j, cols(c)], W[:, j, cols(c)], start=True, stop=True)
                    nc.tensor.matmul(ps_att[:, LEVELS, :], k[:, cols(c)], q[:, cols(c)], start=True, stop=True)
                    nc.tensor.transpose(ps_turn[:, 0:P], ke[:, cols(c)], C["ident"][:]).then_inc(stage_a, 1)
                    if more:
                        for p in parts[c]:
                            piece(u + 1, p)
                    pe.wait_ge(state_ready, past(u * NB + c + 1))
                    pe.wait_ge(o_out, past(u * NB + c))
                    pe.wait_ge(v_ready, past(u + 1))
                    pe.wait_ge(ken_ready, past(u * NB + c + 1))
                    nc.tensor.matmul(ps_state[:, 0:P], ken[:], v[:, c, :], start=True, stop=True)
                    pe.wait_ge(att_ready, past(u * NB + c + 1))
                    nc.tensor.matmul(ps_o[:, 0:P], qs[:, cols(c)], state[:], start=True, stop=False)
                    nc.tensor.matmul(ps_o[:, 0:P], att[:], v[:, c, :], start=False, stop=True).then_inc(stage_b, 1)

            for p in range(HG_PIECES):
                piece(0, p)
            with pe.Fori(0, HEADS - 1) as u:
                mix(u, True)
            mix(HEADS - 1, False)

        @block.scalar
        def _(act):
            act.wait_ge(lb_diff, past(1))
            nc.scalar.activation(lb[:], lb[:], ACT.Sigmoid).then_inc(lb_ready, 1)
            act.wait_ge(lb_ready, past(1))
            nc.scalar.activation(oml[:], lb[:], ACT.Copy, scale=-1.0, bias=1.0).then_inc(lb_ready, 1)

            def out(u, p):
                act.wait_ge(piece_made, past(u * HG_PIECES + p + 1))
                half = slice((p % 2) * 512, (p % 2) * 512 + 512)
                if p < 4:
                    nc.scalar.activation((raw_q if p < 2 else raw_f)[:, half], ps_piece[:, p % 2, :],
                                         ACT.Copy).then_inc(piece_out, 1)
                else:
                    nc.scalar.activation(raw_vg[:, p - 4, :], ps_piece[:, p % 2, 0:2 * P],
                                         ACT.Copy).then_inc(piece_out, 1)

            def mix(u, more):
                act.wait_ge(piece_out, past((u + 1) * HG_PIECES))
                if not (isinstance(u, int) and u == 0):
                    act.wait_ge(stage_b, past(u * NB))
                nc.scalar.activation(f[:], raw_f[:], ACT.Sigmoid).then_inc(gate_sig, 1)
                nc.scalar.activation(q[:], raw_q[:], ACT.Silu).then_inc(q_ready, 1)
                act.wait_ge(stored, past(u))
                nc.scalar.activation(gs[:], raw_vg[:, :, P:2 * P], ACT.Silu).then_inc(g_ready, 1)
                act.wait_ge(gate_ready, past(u + 1))
                nc.scalar.activation(f[:], f[:], ACT.Ln).then_inc(gate_logged, 1)
                for j in range(LEVELS):
                    act.wait_ge(span, past(u * (LEVELS + 1) + j + 1))
                    nc.scalar.activation(W[:, j, :], W[:, j, :], ACT.Exp).then_inc(decayed, 1)
                act.wait_ge(span, past((u + 1) * (LEVELS + 1)))
                nc.scalar.activation(ke[:], ke[:], ACT.Exp).then_inc(decayed, 1)
                nc.scalar.activation(qs[:], G[:], ACT.Exp).then_inc(decayed, 1)
                nc.scalar.activation(gend[:], G[:].rearrange("p (c l) -> p c l", l=P)[:, :, P - 1],
                                     ACT.Exp).then_inc(decayed, 1)
                for c in range(NB):
                    act.wait_ge(stage_a, past(u * NB + c + 1))
                    act.wait_ge(stage_b, past(u * NB + c))
                    nc.scalar.activation(ken[:], ps_turn[:, 0:P], ACT.Copy).then_inc(ken_ready, 1)
                    if more:
                        for p in parts[c]:
                            out(u + 1, p)
                    act.wait_ge(stage_b, past(u * NB + c + 1))
                    nc.scalar.activation(o[:, c, :], ps_o[:, 0:P], ACT.Square,
                                         accum_out=ss[:, c:c + 1]).then_inc(o_squared, 1)
                    act.wait_ge(o_squared, past(u * NB + c + 1))
                    nc.scalar.activation(o[:, c, :], ps_o[:, 0:P], ACT.Copy).then_inc(o_out, 1)
                act.wait_ge(meaned, past(u + 1))
                nc.scalar.activation(rs[:], ss[:], ACT.Sqrt).then_inc(rooted, 1)
                act.wait_ge(stored, past(u + 1))

            for p in range(HG_PIECES):
                out(0, p)
            with act.Fori(0, HEADS - 1) as u:
                mix(u, True)
            mix(HEADS - 1, False)

        @block.vector
        def _(dve):
            own = Own(dve, dve_own, 4 + 1)
            dve.wait_ge(lb_in, 16)
            nc.vector.tensor_tensor(lb[:], lbl[:, 0, :], lbl[:, 1, :], ALU.subtract).then_inc(lb_diff, 1)
            dve.wait_ge(lb_ready, past(2))
            with dve.Fori(0, HEADS) as u:
                own.at(u)
                dve.wait_ge(gate_sig, past(u + 1))
                own.done(nc.vector.tensor_scalar(f[:], f[:], oml[:, bass.ds(u, 1)], lb[:, bass.ds(u, 1)],
                                                 ALU.mult, ALU.add))
                nc.vector.tensor_scalar(k[:], f[:], -1.0, 1.0, ALU.mult, ALU.add).then_inc(gate_ready, 1)
                nc.vector.tensor_copy(v[:], raw_vg[:, :, 0:P]).then_inc(v_ready, 1)
                dve.wait_ge(gate_logged, past(u + 1))
                nc.vector.tensor_tensor_scan(G[:], C["reset"][:], f[:], 0.0, ALU.mult, ALU.add).then_inc(summed, 1)
                dve.wait_ge(summed, past(u + 1))
                for j in range(LEVELS):
                    h = P >> (j + 1)
                    gv = G[:].rearrange("p (b two h) -> p b two h", two=2, h=h)
                    wv = W[:, j, :].rearrange("p (b two h) -> p b two h", two=2, h=h)
                    at = gv[:, :, 0, h - 1:h].to_broadcast([P, SEQ // (2 * h), h])
                    nc.vector.tensor_tensor(wv[:, :, 0, :], at, gv[:, :, 0, :], ALU.subtract)
                    nc.vector.tensor_tensor(wv[:, :, 1, :], gv[:, :, 1, :], at, ALU.subtract).then_inc(span, 1)
                gc = G[:].rearrange("p (c l) -> p c l", l=P)
                nc.vector.tensor_tensor(ke[:].rearrange("p (c l) -> p c l", l=P),
                                        gc[:, :, P - 1:P].to_broadcast([P, NB, P]), gc, ALU.subtract).then_inc(span, 1)
                dve.wait_ge(q_ready, past(u + 1))
                for j in range(LEVELS):
                    h = P >> (j + 1)
                    dve.wait_ge(decayed, past(u * (LEVELS + 3) + j + 1))
                    qv = q[:].rearrange("p (b two h) -> p b two h", two=2, h=h)
                    kv = k[:].rearrange("p (b two h) -> p b two h", two=2, h=h)
                    wv = W[:, j, :].rearrange("p (b two h) -> p b two h", two=2, h=h)
                    nc.vector.tensor_tensor(wv[:, :, 0, :], wv[:, :, 0, :], kv[:, :, 0, :], ALU.mult)
                    nc.vector.tensor_tensor(wv[:, :, 1, :], wv[:, :, 1, :], qv[:, :, 1, :], ALU.mult).then_inc(weighted, 1)
                dve.wait_ge(decayed, past((u + 1) * (LEVELS + 3)))
                nc.vector.tensor_tensor(ke[:], ke[:], k[:], ALU.mult).then_inc(weighted, 1)
                nc.vector.tensor_tensor(qs[:], qs[:], q[:], ALU.mult).then_inc(weighted, 1)
                own.done(nc.vector.memset(state[:], 0.0))
                dve.sem_inc(state_ready, 1)
                for c in range(NB):
                    dve.wait_ge(stage_a, past(u * NB + c + 1))
                    nc.vector.tensor_tensor(masked[:], ps_att[:], C["lmask"][:], ALU.mult).then_inc(mask_done, 1)
                    dve.wait_ge(mask_done, past(u * NB + c + 1))
                    dve.wait_ge(stage_b, past(u * NB + c))
                    nc.vector.tensor_reduce(att[:], masked[:].rearrange("p j l -> p l j"), AX.X,
                                            ALU.add).then_inc(att_ready, 1)
                    dve.wait_ge(stage_b, past(u * NB + c + 1))
                    if c < NB - 1:
                        nc.vector.scalar_tensor_tensor(out=state[:], in0=state[:], scalar=gend[:, c:c + 1],
                                                       in1=ps_state[:, 0:P], op0=ALU.mult,
                                                       op1=ALU.add).then_inc(state_ready, 1)
                dve.wait_ge(o_out, past((u + 1) * NB))
                nc.vector.tensor_scalar(ss[:], ss[:], 1.0 / P, EPS, ALU.mult, ALU.add).then_inc(meaned, 1)
                dve.wait_ge(rooted, past(u + 1))
                own.done(nc.vector.reciprocal(rs[:], rs[:]))
                own.done(nc.vector.tensor_tensor(o[:], o[:], rs[:].unsqueeze(2).to_broadcast([P, NB, P]), ALU.mult))
                dve.wait_ge(g_ready, past(u + 1))
                own.done(nc.vector.tensor_tensor(Y[:, :, bass.ds(D + u * P, P)], o[:], gs[:], ALU.mult))
                dve.sem_inc(stored, 1)
                own.check()


def mix_out(nc, x, w_out, mix_w, ffn_w, C, Y, xnT):
    with ExitStack() as ctx:
        def sb(name, shape, dt=F32):
            return ctx.enter_context(nc.sbuf_tensor("mo_" + name, shape, dt))

        primed = []

        def plain_sem(name):
            return ctx.enter_context(nc.semaphore("mo_" + name))

        def sem(name):
            primed.append(plain_sem(name))
            return primed[-1]

        def psum(name, shape):
            return ctx.enter_context(nc.psum_tensor("mo_" + name, shape, F32))

        w = sb("w", [P, MT, D])
        mw = sb("mw", [P, MT])
        fw = sb("fw", [P, D])
        ys = sb("ys", [P, MIX])
        yT = sb("yT", [P, MT, P])
        xr = sb("xr", [P, D])
        h = sb("h", [P, D])
        xn = sb("xn", [P, D])
        sq = sb("sq", [P, D])
        ss = sb("ss", [P, 2])
        rs = sb("rs", [P, 2])
        ps_y = psum("ps_y", [P, 4, P])
        ps_y2 = psum("ps_y2", [P, 4, P])
        ps_h = psum("ps_h", [P, 2, 512])
        ps_x = psum("ps_x", [P, KT, P])
        GRP = 4
        NG = MT // GRP

        w_in, s_in, x_in = [plain_sem(f"w_in{k}") for k in range(MT)], plain_sem("s_in"), plain_sem("x_in")
        y_squared, y_meaned, y_rooted, y_inverse = sem("y_squared"), sem("y_meaned"), sem("y_rooted"), sem("y_inverse")
        ys_scaled, ys_copied = sem("ys_scaled"), sem("ys_copied")
        y_turned, yT_ready = sem("y_turned"), sem("yT_ready")
        product, h_ready, h_squared, h_meaned, h_rooted, h_inverse = (
            sem("product"), sem("h_ready"), sem("h_squared"), sem("h_meaned"), sem("h_rooted"), sem("h_inverse"))
        xn_ready, xn_turned, xnT_ready, kept = sem("xn_ready"), sem("xn_turned"), sem("xnT_ready"), sem("kept")
        act_turn, pool_turn = sem("act_turn"), sem("pool_turn")
        xd = x.rearrange("o (b p) d -> p (o b) d", p=P)
        block = ctx.enter_context(nc.Block())

        def in_steps(eng, step):
            step(0, True, False)
            with eng.Fori(1, NB - 1) as b:
                step(b, False, False)
            step(NB - 1, False, True)

        @block.sync
        def _(sp):
            prime(sp, primed)
            sp.dma_start(mw[:], mix_w).then_inc(s_in, 16)
            sp.dma_start(fw[:], ffn_w).then_inc(s_in, 16)
            for k in range(MT):
                sp.dma_start(w[:, k, :], w_out[:, k, :]).then_inc(w_in[k], 16)
            with sp.Fori(0, NB) as b:
                sp.wait_ge(h_ready, past(b))
                sp.dma_start(xr[:], xd[:, bass.ds(b, 1), :].rearrange("p o d -> p (o d)")).then_inc(x_in, 16)

        @block.tensor
        def _(pe):
            def turn_y(b):
                for g in range(NG):
                    pe.wait_ge(ys_scaled if g < NG // 2 else ys_copied, past(b + 1))
                    if not (isinstance(b, int) and g < 2):
                        pe.wait_ge(yT_ready, past(b * MT + GRP * (g - 1)))
                    bank = (ps_y, ps_y2)[g % 2]
                    for j in range(GRP):
                        k = g * GRP + j
                        mm = nc.tensor.transpose(bank[:, j, :], ys[:, k * P:(k + 1) * P], C["ident"][:])
                    mm.then_inc(y_turned, 1)

            def turn_x(b):
                pe.wait_ge(xn_ready, past(b + 1))
                pe.wait_ge(xnT_ready, past(b))
                for k in range(KT):
                    mm = nc.tensor.transpose(ps_x[:, k, :], xn[:, k * P:(k + 1) * P], C["ident"][:])
                mm.then_inc(xn_turned, 1)

            def multiply(b):
                pe.wait_ge(h_ready, past(b))
                for k in range(MT):
                    if isinstance(b, int):
                        pe.wait_ge(w_in[k], 16)
                    pe.wait_ge(yT_ready, past(b * MT + k + 1))
                    for half in range(2):
                        mm = nc.tensor.matmul(ps_h[:, half, :], yT[:, k, :], w[:, k, half * 512:(half + 1) * 512],
                                              start=(k == 0), stop=(k == MT - 1))
                mm.then_inc(product, 1)

            turn_y(0)
            multiply(0)
            with pe.Fori(1, NB) as b:
                turn_y(b)
                turn_x(b - 1)
                multiply(b)
            turn_x(NB - 1)

        @block.scalar
        def _(act):
            act.wait_ge(s_in, 32)

            def root_y(b):
                if not isinstance(b, int):
                    act.wait_ge(h_squared, past(b - 1))
                act.sem_inc(act_turn, 1)
                nc.scalar.activation(sq[:], Y[:, bass.ds(b, 1), 0:D].rearrange("p o d -> p (o d)"), ACT.Square,
                                     accum_out=ss[:, 0:1]).then_inc(y_squared, 1)
                act.wait_ge(y_meaned, past(b + 1))
                nc.scalar.activation(rs[:, 0:1], ss[:, 0:1], ACT.Sqrt).then_inc(y_rooted, 1)

            def out_y(b):
                for k in range(MT):
                    if k % GRP == 0:
                        act.wait_ge(y_turned, past(b * NG + k // GRP + 1))
                        act.wait_ge(product, past(b))
                    nc.scalar.activation(yT[:, k, :], ((ps_y, ps_y2)[k // GRP % 2])[:, k % GRP, :], ACT.Copy,
                                         scale=mw[:, k:k + 1]).then_inc(yT_ready, 1)

            def turned_out(b):
                act.wait_ge(xn_turned, past(b + 1))
                act.sem_inc(act_turn, 1)
                nc.scalar.activation(xnT[:, :, bass.ds(b * P, P)], ps_x[:], ACT.Copy).then_inc(xnT_ready, 1)

            def step(b, first, last):
                out_y(b)
                if not first:
                    turned_out(b - 1)
                if not last:
                    root_y(b + 1)
                act.wait_ge(h_ready, past(b + 1))
                act.wait_ge(y_squared, past(b + 1 if last else b + 2))
                nc.scalar.activation(sq[:], h[:], ACT.Square, accum_out=ss[:, 1:2]).then_inc(h_squared, 1)
                act.wait_ge(h_meaned, past(b + 1))
                nc.scalar.activation(rs[:, 1:2], ss[:, 1:2], ACT.Sqrt).then_inc(h_rooted, 1)

            root_y(0)
            in_steps(act, step)
            turned_out(NB - 1)

        @block.gpsimd
        def _(pool):
            def copy_y(b):
                pool.wait_ge(y_turned, past(b * NG))
                pool.sem_inc(pool_turn, 1)
                nc.gpsimd.tensor_copy(ys[:, D:MIX], Y[:, bass.ds(b, 1), D:MIX].rearrange("p o d -> p (o d)")
                                      ).then_inc(ys_copied, 1)

            def step(b, first, last):
                if not last:
                    copy_y(b + 1)
                pool.wait_ge(h_ready, past(b + 1))
                pool.sem_inc(pool_turn, 1)
                nc.gpsimd.tensor_copy(Y[:, bass.ds(b, 1), 0:D].rearrange("p o d -> p (o d)"), h[:])
                pool.wait_ge(xn_ready, past(b + 1))
                pool.wait_ge(ys_copied, past(b + 1))
                pool.sem_inc(pool_turn, 1)
                nc.gpsimd.tensor_copy(Y[:, bass.ds(b, 1), D:MIX].rearrange("p o d -> p (o d)"), xn[:]).then_inc(kept, 1)

            copy_y(0)
            in_steps(pool, step)

        @block.vector
        def _(dve):
            def scale_y(b):
                dve.wait_ge(y_squared, past(b + 1))
                nc.vector.tensor_scalar(ss[:, 0:1], ss[:, 0:1], 1.0 / D, EPS, ALU.mult, ALU.add).then_inc(y_meaned, 1)
                dve.wait_ge(y_rooted, past(b + 1))
                nc.vector.reciprocal(rs[:, 0:1], rs[:, 0:1]).then_inc(y_inverse, 1)
                dve.wait_ge(y_turned, past(b * NG))
                dve.wait_ge(y_inverse, past(b + 1))
                nc.vector.tensor_scalar(ys[:, 0:D], Y[:, bass.ds(b, 1), 0:D].rearrange("p o d -> p (o d)"),
                                        rs[:, 0:1], None, ALU.mult).then_inc(ys_scaled, 1)

            def step(b, first, last):
                if not last:
                    scale_y(b + 1)
                dve.wait_ge(x_in, (b + 1) * 16)
                dve.wait_ge(kept, past(b))
                dve.wait_ge(product, past(b + 1))
                nc.vector.tensor_tensor(h[:], ps_h[:].rearrange("p a c -> p (a c)"), xr[:], ALU.add).then_inc(h_ready, 1)
                dve.wait_ge(h_squared, past(b + 1))
                nc.vector.tensor_scalar(ss[:, 1:2], ss[:, 1:2], 1.0 / D, EPS, ALU.mult, ALU.add).then_inc(h_meaned, 1)
                dve.wait_ge(h_rooted, past(b + 1))
                nc.vector.reciprocal(rs[:, 1:2], rs[:, 1:2]).then_inc(h_inverse, 1)
                dve.wait_ge(h_inverse, past(b + 1))
                dve.wait_ge(xn_turned, past(b))
                nc.vector.scalar_tensor_tensor(out=xn[:], in0=h[:], scalar=rs[:, 1:2], in1=fw[:],
                                               op0=ALU.mult, op1=ALU.mult).then_inc(xn_ready, 1)

            scale_y(0)
            in_steps(dve, step)
            dve.wait_ge(kept, past(NB))


def peer(nc, w_query, keys, table, C, Y, xnT):
    with ExitStack() as ctx:
        def sb(name, shape, dt=F32):
            return ctx.enter_context(nc.sbuf_tensor("peer_" + name, shape, dt))

        primed = []

        def plain_sem(name):
            return ctx.enter_context(nc.semaphore("peer_" + name))

        def sem(name):
            primed.append(plain_sem(name))
            return primed[-1]

        def psum(name, shape):
            return ctx.enter_context(nc.psum_tensor("peer_" + name, shape, F32))

        ring = sb("ring", [P, RING, 2 * D])
        wq = sb("wq", [P, KT, 2 * P])
        kT = sb("kT", [P, PH * 2 * KEYS])
        qs = sb("qs", [P, 2, P])
        sc = sb("sc", [P, 2, KEYS])
        sc2 = sb("sc2", [P, 2, KEYS])
        top = sb("top", [P, 2, TOPK])
        ix = sb("ix", [P, 2, TOPK], U32)
        ixf = sb("ixf", [P, 2, TOPK])
        cand = sb("cand", [P, NCAND])
        cand2 = sb("cand2", [P, NCAND])
        expert = sb("expert", [P, NCAND])
        best = sb("best", [P, TOPK])
        place = sb("place", [P, TOPK], U32)
        placef = sb("placef", [P, TOPK])
        count_u = sb("count_u", [P, NCAND], U32)
        count = sb("count", [P, NCAND])
        hit = sb("hit", [P, TOPK, NCAND])
        chosen = sb("chosen", [P, TOPK])
        neg = sb("neg", [P, 1])
        gx = sb("gx", [P, TOPK])
        gsum = sb("gsum", [P, 1])
        index = sb("index", [P, NB, TOPK], U32)
        gate = sb("gate", [P, NB, TOPK])
        index_even = sb("index_even", [P, TOPK], U32)
        index_odd = sb("index_odd", [P, TOPK], U32)
        gate_now = sb("gate_now", [P, TOPK])
        junk = sb("junk", [P, D])
        dots = sb("dots", [P, TOPK])
        act_out = sb("act_out", [P, BATCH])
        hid = sb("hid", [P, BATCH])
        diag = sb("diag", [P, RING, P])

        ps_q = psum("ps_q", [P, 2, 256])
        ps_s = psum("ps_s", [P, 2, 256])
        ps_o = psum("ps_o", [P, 2, 512])

        wq_in, k_in = plain_sem("wq_in"), plain_sem("k_in")
        got = [plain_sem(f"got{s}") for s in range(RING)]
        counted = sem("counted")
        q_made, q_out, scores_made, scores_out, picked = (sem("q_made"), sem("q_out"), sem("scores_made"),
                                                          sem("scores_out"), sem("picked"))
        best_ready, gates_ready, routed = sem("best_ready"), sem("gates_ready"), sem("routed")
        index_taken, gate_taken = sem("index_taken"), sem("gate_taken")
        free_slots = plain_sem("free_slots")
        dot_ready, act_own, diag_ready, activated = sem("dot_ready"), sem("act_own"), sem("diag_ready"), sem("activated")
        summed, added = sem("summed"), sem("added")
        dve_own, dve_turn, act_turn, pool_turn = sem("dve_own"), sem("dve_turn"), sem("act_turn"), sem("pool_turn")
        block = ctx.enter_context(nc.Block())

        def loops(eng, route_pass, gather_pass):
            with eng.Fori(0, NB) as b:
                route_pass(b, 0, b, None)
            with eng.Fori(0, PH - 1) as h:
                with eng.Fori(0, NB) as b:
                    gather_pass(h * NB + b, b, lambda: route_pass(h * NB + b + NB, h + 1, b, h * NB + b))
            with eng.Fori(0, NB) as b:
                gather_pass(b + (PH - 1) * NB, b, None)

        @block.sync
        def _(sp):
            prime(sp, primed)
            sp.dma_start(wq[:], w_query[0]).then_inc(wq_in, 16)
            sp.dma_start(kT[:], keys).then_inc(k_in, 16)
            with sp.Fori(1, PH) as h:
                sp.wait_ge(q_made, past(h * NB))
                sp.dma_start(wq[:], w_query[bass.ds(h, 1)].rearrange("o p k c -> p (o k) c")).then_inc(wq_in, 16)

        @block.gpsimd
        def _(pool):
            nc.gpsimd.iota(count_u[:], pattern=[[1, NCAND]], base=0, channel_multiplier=0).then_inc(counted, 1)
            pool.sem_inc(free_slots, RING)

            def gather(n, b, index_now):
                pool.wait_ge(routed, past(n + 1))
                pool.sem_inc(pool_turn, 1)
                nc.gpsimd.tensor_copy(index_now[:], index[:, bass.ds(b, 1), :].rearrange("p o k -> p (o k)")
                                      ).then_inc(index_taken, 1)
                pool.wait_ge(index_taken, past(n + 1))
                for k in range(TOPK):
                    pool.wait_ge(free_slots, n * TOPK + k + 1)
                    pool.sem_inc(pool_turn, 1)
                    pool.indirect_dma_start(ring[:, k % RING, :], None, table,
                                            bass.IndirectOffsetOnAxis(ap=index_now[:, k:k + 1], axis=0)
                                            ).then_inc(got[k % RING], 16)

            with pool.Fori(0, PH) as h:
                with pool.Fori(0, NB // 2) as pair:
                    gather(h * NB + pair * 2, pair * 2, index_even)
                    gather(h * NB + pair * 2 + 1, pair * 2 + 1, index_odd)

        @block.tensor
        def _(pe):
            def query(n, h, b):
                pe.wait_ge(wq_in, (h + 1) * 16)
                pe.wait_ge(q_out, past(n))
                for p in range(2):
                    for k in range(KT):
                        mm = nc.tensor.matmul(ps_q[:, p, 0:P], wq[:, k, p * P:(p + 1) * P],
                                              xnT[:, k, bass.ds(b * P, P)], start=(k == 0), stop=(k == KT - 1))
                mm.then_inc(q_made, 1)

            def score(n, h):
                pe.wait_ge(q_out, past(n + 1))
                pe.wait_ge(scores_out, past(n))
                for p in range(2):
                    mm = nc.tensor.matmul(ps_s[:, p, 0:P], qs[:, p, :], kT[:, bass.ds((h * 2 + p) * KEYS, KEYS)],
                                          start=True, stop=True)
                mm.then_inc(scores_made, 1)

            def route(n, h, b, last):
                query(n, h, b)
                score(n, h)

            def gather(n, b, route_next):
                if route_next:
                    route_next()
                pe.wait_ge(added, past(n))
                for k in range(TOPK):
                    pe.wait_ge(diag_ready, past(n * TOPK + k + 1))
                    for half in range(2):
                        mm = nc.tensor.matmul(ps_o[:, half, :], diag[:, k % RING, :],
                                              ring[:, k % RING, D + half * 512:D + (half + 1) * 512],
                                              start=(k == 0), stop=(k == TOPK - 1))
                    mm.then_inc(free_slots, 1)

            pe.wait_ge(k_in, 16)
            loops(pe, route, gather)

        @block.scalar
        def _(act):
            def scores(n):
                act.wait_ge(q_made, past(n + 1))
                act.wait_ge(scores_made, past(n))
                nc.scalar.activation(qs[:], ps_q[:, :, 0:P], ACT.Copy).then_inc(q_out, 1)
                act.wait_ge(scores_made, past(n + 1))
                act.wait_ge(picked, past(n))
                nc.scalar.activation(sc[:], ps_s[:, :, 0:KEYS], ACT.Copy).then_inc(scores_out, 1)

            def gates(n):
                act.wait_ge(best_ready, past(n + 1))
                nc.scalar.activation(gx[:], best[:], ACT.Exp, bias=neg[:], accum_out=gsum[:]).then_inc(gates_ready, 1)

            def route(n, h, b, last):
                scores(n)
                gates(n)

            def gather(n, b, route_next):
                if route_next:
                    scores(n + NB)
                own = Own(act, act_own, TOPK)
                own.at(n)
                act.wait_ge(routed, past(n + 1))
                act.sem_inc(act_turn, 1)
                nc.scalar.activation(gate_now[:], gate[:, bass.ds(b, 1), :].rearrange("p o k -> p (o k)"),
                                     ACT.Copy).then_inc(gate_taken, 1)
                act.wait_ge(gate_taken, past(n + 1))
                for q in range(TOPK // BATCH):
                    act.wait_ge(dot_ready, past(n * TOPK + (q + 1) * BATCH))
                    nc.scalar.activation(act_out[:], dots[:, q * BATCH:(q + 1) * BATCH], ACT.Gelu).then_inc(activated, 1)
                    act.wait_ge(activated, past(n * (TOPK // BATCH) + q + 1))
                    for j in range(BATCH):
                        k = q * BATCH + j
                        own.step(nc.scalar.activation(hid[:, j:j + 1], act_out[:, j:j + 1], ACT.Copy,
                                                      scale=gate_now[:, k:k + 1]))
                    own.wait()
                    for j in range(BATCH):
                        k = q * BATCH + j
                        act.wait_ge(free_slots, n * TOPK + k + 1)
                        ins = nc.scalar.activation(diag[:, k % RING, :], C["ident"][:], ACT.Copy, scale=hid[:, j:j + 1])
                        ins.then_inc(diag_ready, 1)
                own.check()
                if route_next:
                    gates(n + NB)

            loops(act, route, gather)

        @block.vector
        def _(dve):
            dve.wait_ge(counted, past(1))
            nc.vector.tensor_copy(count[:], count_u[:]).then_inc(counted, 1)
            dve.wait_ge(counted, past(2))

            def route(n, h, b, last):
                own = Own(dve, dve_own, 19)
                own.at(n)

                def hold():
                    own.wait()
                    dve.sem_inc(dve_turn, 1)

                dve.wait_ge(scores_out, past(n + 1))
                dve.sem_inc(dve_turn, 1)
                for p in range(2):
                    own.step(nc.vector.max(top[:, p, 0:8], sc[:, p, :]))
                hold()
                for p in range(2):
                    nc.vector.max_index(ix[:, p, 0:8], top[:, p, 0:8], sc[:, p, :])
                    own.step(nc.vector.match_replace(sc2[:, p, :], top[:, p, 0:8], sc[:, p, :], LOW))
                hold()
                dve.sem_inc(picked, 1)
                for p in range(2):
                    own.step(nc.vector.max(top[:, p, 8:16], sc2[:, p, :]))
                hold()
                for p in range(2):
                    ins = nc.vector.max_index(ix[:, p, 8:16], top[:, p, 8:16], sc2[:, p, :])
                own.done(ins)
                own.done(nc.vector.tensor_copy(ixf[:], ix[:]))
                own.done(nc.vector.tensor_scalar(ixf[:, 0, :], ixf[:, 0, :], float(KEYS), None, ALU.mult))
                at = 0
                for i in range(TOPK // 2):
                    m = ROWS_OF[i]
                    nc.vector.tensor_scalar(cand[:, at:at + m], top[:, 1, 0:m], top[:, 0, i:i + 1], None, ALU.add)
                    nc.vector.tensor_scalar(expert[:, at:at + m], ixf[:, 1, 0:m], ixf[:, 0, i:i + 1], None, ALU.add)
                    at += m
                nc.vector.tensor_scalar(expert[:, at:], ixf[:, 0, 8:16], ixf[:, 1, 0:1], None, ALU.add)
                own.step(nc.vector.tensor_scalar(cand[:, at:], top[:, 0, 8:16], top[:, 1, 0:1], None, ALU.add))
                hold()
                own.step(nc.vector.max(best[:, 0:8], cand[:]))
                hold()
                nc.vector.max_index(place[:, 0:8], best[:, 0:8], cand[:])
                own.step(nc.vector.match_replace(cand2[:], best[:, 0:8], cand[:], LOW))
                hold()
                own.step(nc.vector.max(best[:, 8:16], cand2[:]))
                nc.vector.tensor_scalar(neg[:], best[:, 0:1], -1.0, None, ALU.mult).then_inc(best_ready, 1)
                hold()
                own.done(nc.vector.max_index(place[:, 8:16], best[:, 8:16], cand2[:]))
                own.done(nc.vector.tensor_copy(placef[:], place[:]))
                own.done(nc.vector.tensor_tensor(hit[:], count[:].unsqueeze(1).to_broadcast([P, TOPK, NCAND]),
                                                 placef[:].unsqueeze(2).to_broadcast([P, TOPK, NCAND]), ALU.is_equal))
                own.done(nc.vector.tensor_tensor(hit[:], hit[:], expert[:].unsqueeze(1).to_broadcast([P, TOPK, NCAND]),
                                                 ALU.mult))
                own.step(nc.vector.tensor_reduce(chosen[:], hit[:], AX.X, ALU.add))
                if last is not None:
                    dve.wait_ge(index_taken, past(last + 1))
                    dve.wait_ge(gate_taken, past(last + 1))
                hold()
                nc.vector.tensor_copy(index[:, bass.ds(b, 1), :].rearrange("p o k -> p (o k)"), chosen[:])
                dve.wait_ge(gates_ready, past(n + 1))
                own.done(nc.vector.reciprocal(gsum[:], gsum[:]))
                nc.vector.tensor_scalar(gate[:, bass.ds(b, 1), :].rearrange("p o k -> p (o k)"), gx[:], gsum[:], None,
                                        ALU.mult).then_inc(routed, 1)
                own.check()

            def gather(n, b, route_next):
                for k in range(TOPK):
                    s = k % RING
                    dve.wait_ge(got[s], (n * 2 + k // RING + 1) * 16)
                    dve.wait_ge(dot_ready, past(n * TOPK + k))
                    if k % BATCH == 0:
                        dve.wait_ge(diag_ready, past(n * TOPK))
                    nc.vector.scalar_tensor_tensor(
                        out=junk[:], in0=ring[:, s, 0:D], scalar=1.0,
                        in1=Y[:, bass.ds(b, 1), D:MIX].rearrange("p o d -> p (o d)"),
                        op0=ALU.mult, op1=ALU.mult, accum_out=dots[:, k:k + 1]).then_inc(dot_ready, 1)
                if route_next:
                    route_next()
                dve.wait_ge(free_slots, RING + (n + 1) * TOPK)
                hb = Y[:, bass.ds(b, 1), 0:D].rearrange("p o d -> p (o d)")
                nc.vector.tensor_tensor(hb, hb, ps_o[:].rearrange("p a c -> p (a c)"), ALU.add).then_inc(added, 1)

            loops(dve, route, gather)
            dve.wait_ge(added, past(PH * NB))


def final_norm(nc, fin_w, Y, out):
    with ExitStack() as ctx:
        def sb(name, shape, dt=F32):
            return ctx.enter_context(nc.sbuf_tensor("fin_" + name, shape, dt))

        primed = []

        def plain_sem(name):
            return ctx.enter_context(nc.semaphore("fin_" + name))

        def sem(name):
            primed.append(plain_sem(name))
            return primed[-1]

        fw = sb("fw", [P, D])
        sq = sb("sq", [P, D])
        ss = sb("ss", [P, NB])
        rs = sb("rs", [P, NB])
        w_in, squared, meaned, rooted, inverse, normed, written = (
            plain_sem("w_in"), sem("squared"), sem("meaned"), sem("rooted"), sem("inverse"), sem("normed"), plain_sem("written"))
        od = out.rearrange("o (b p) d -> p (o b) d", p=P)
        block = ctx.enter_context(nc.Block())

        @block.scalar
        def _(act):
            for b in range(NB):
                if b >= 1:
                    act.wait_ge(squared, past(b))
                nc.scalar.activation(sq[:], Y[:, b, 0:D], ACT.Square, accum_out=ss[:, b:b + 1]).then_inc(squared, 1)
            act.wait_ge(meaned, past(1))
            nc.scalar.activation(rs[:], ss[:], ACT.Sqrt).then_inc(rooted, 1)

        @block.vector
        def _(dve):
            dve.wait_ge(squared, past(NB))
            nc.vector.tensor_scalar(ss[:], ss[:], 1.0 / D, EPS, ALU.mult, ALU.add).then_inc(meaned, 1)
            dve.wait_ge(rooted, past(1))
            nc.vector.reciprocal(rs[:], rs[:]).then_inc(inverse, 1)
            dve.wait_ge(inverse, past(1))
            dve.wait_ge(w_in, 16)
            for b in range(NB):
                nc.vector.scalar_tensor_tensor(out=Y[:, b, D:MIX], in0=Y[:, b, 0:D], scalar=rs[:, b:b + 1], in1=fw[:],
                                               op0=ALU.mult, op1=ALU.mult).then_inc(normed, 1)

        @block.sync
        def _(sp):
            prime(sp, primed)
            sp.dma_start(fw[:], fin_w).then_inc(w_in, 16)
            for b in range(NB):
                sp.wait_ge(normed, past(b + 1))
                sp.dma_start(od[:, b, :], Y[:, b, D:MIX]).then_inc(written, 16)
            sp.wait_ge(written, 16 * NB)


def block_program(nc, x, ln_w, w_ssd, par, w_hg, lb_logits, w_out, mix_w, ffn_w, w_query, keys, table, fin_w, out):
    with ExitStack() as ctx:
        C = {n: ctx.enter_context(nc.sbuf_tensor(n, [P, P], F32)) for n in ("ident", "ones", "tri", "below")}
        hnT = ctx.enter_context(nc.sbuf_tensor("hnT", [P, KT, SEQ], F32))
        Y = ctx.enter_context(nc.sbuf_tensor("Y", [P, NB, MIX], F32))
        with nc.sbuf_tensor("reset", [P, SEQ], F32) as reset, nc.sbuf_tensor("lmask", [P, LEVELS + 1, P], F32) as lmask:
            C["reset"], C["lmask"] = reset, lmask
            constants(nc, C)
            input_norm(nc, x, ln_w, C, hnT)
            ssd(nc, w_ssd, par, C, hnT, Y)
            hgrn(nc, w_hg, lb_logits, C, hnT, Y)
        mix_out(nc, x, w_out, mix_w, ffn_w, C, Y, hnT)
        peer(nc, w_query, keys, table, C, Y, hnT)
        final_norm(nc, fin_w, Y, out)


def laid_out(inputs):
    import numpy as np

    def first(name):
        return np.asarray(inputs[name])[0]

    inner, bc = GROUPS * XW, GROUPS * P
    w = first("w_in").reshape(KT, P, -1).transpose(1, 0, 2)
    at_x, at_dt = inner, 2 * inner + 2 * bc
    at_q = at_dt + GROUPS * HPG
    conv = np.concatenate([first("conv_w"), first("conv_b")[None]], 0)
    w_ssd, par = [], []
    for g in range(GROUPS):
        ch = np.concatenate([np.arange(g * XW, (g + 1) * XW), inner + g * P + np.arange(P),
                             inner + bc + g * P + np.arange(P)])
        w_ssd.append(np.concatenate([w[:, :, at_x + ch], w[:, :, g * XW:(g + 1) * XW],
                                     w[:, :, at_dt + g * HPG:at_dt + (g + 1) * HPG]], 2))
        taps = conv[:, ch].reshape(TAPS + 1, CT, P).transpose(2, 1, 0).reshape(P, CT * (TAPS + 1))
        heads = [np.broadcast_to(first(n)[g * HPG:(g + 1) * HPG], (P, HPG)) for n in ("dt_bias", "a_log", "d_skip")]
        par.append(np.concatenate([taps, *heads], 1))
    w_hg = [np.concatenate([w[:, :, at_q + j * D + h * P:at_q + j * D + (h + 1) * P] for j in range(4)], 2)
            for h in range(HEADS)]
    return {
        "x": np.asarray(inputs["x"]),
        "ln_w": first("ln_mix_w").reshape(KT, P).T,
        "w_ssd": np.stack(w_ssd),
        "par": np.stack(par, 1),
        "w_hg": np.stack(w_hg),
        "lb_logits": np.asarray(inputs["lb_logits"]).reshape(2, HEADS, P).transpose(2, 0, 1),
        "w_out": first("w_out").reshape(MT, P, D).transpose(1, 0, 2),
        "mix_w": np.concatenate([first("ssd_norm_w"), first("hg_norm_w")]).reshape(MT, P).T,
        "ffn_w": np.broadcast_to(first("ln_ffn_w"), (P, D)),
        "w_query": first("w_query").reshape(KT, P, PH, 2 * P).transpose(2, 1, 0, 3),
        "keys": first("sub_keys").transpose(3, 0, 1, 2).reshape(P, PH * 2 * KEYS),
        "table": np.concatenate([first("u_table"), first("v_table")], 1),
        "fin_w": np.broadcast_to(np.asarray(inputs["ln_final_w"]), (P, D)),
    }


def kernel(**inputs):
    import numpy as np
    import concourse.bacc as bacc
    from concourse.bass_utils import run_bass_kernel_spmd

    nc = bacc.Bacc("TRN2", target_bir_lowering=False, num_devices=1)
    arrays = {n: np.ascontiguousarray(a) for n, a in laid_out(inputs).items()}
    args = {n: nc.dram_tensor("in_" + n, a.shape, mybir.dt.from_np(a.dtype), kind="ExternalInput").ap()
            for n, a in arrays.items()}
    out = nc.dram_tensor("out_0", [1, SEQ, D], F32, kind="ExternalOutput").ap()
    block_program(nc, out=out, **args)
    r = run_bass_kernel_spmd(nc, [{"in_" + n: a for n, a in arrays.items()}], core_ids=[0])
    return r.results[0]["out_0"]
```

```python
from contextlib import ExitStack

import concourse.bass as bass
from concourse import mybir

ALU = mybir.AluOpType
ACT = mybir.ActivationFunctionType
AX = mybir.AxisListType
F32 = mybir.dt.float32
U32 = mybir.dt.uint32

P = 128
SEQ, D = 1024, 1024
NB = SEQ // P
KT = D // P
EPS = 1e-6
HALF, HC = SEQ // 2, NB // 2

GROUPS, HPG, HD = 4, 4, 64
XW = HPG * HD
CT = 4
TAPS = 4
SSD_COLS = CT * P + XW + HPG
SSD_PARTS = [slice(i * P, (i + 1) * P) for i in range(CT)] + [slice(CT * P, SSD_COLS)]
SSD_PIECES = 2 * CT
NPAR = CT * (TAPS + 1) + 3 * HPG
DTB, ALG, DSK = CT * (TAPS + 1), CT * (TAPS + 1) + HPG, CT * (TAPS + 1) + 2 * HPG

HEADS = 8
HG_COLS = 4 * P
HG_PARTS = [slice(0, P), slice(P, 2 * P), slice(2 * P, HG_COLS)]
HG_PIECES = 2 + NB // 2
HEAD_PARTS = [[0], [1], [2, 3], [4, 5]]
LEVELS = 7
MIX = 2 * D
MT = MIX // P

PH, TOPK, KEYS = 8, 16, 128
EXPERTS = KEYS * KEYS
ROWS_OF = [TOPK // (i + 1) for i in range(TOPK)]
NCAND = sum(ROWS_OF)
RING = 8
LAG = 2
BATCH = 4
LOW = -3.0e38


def cols(c):
    return slice(c * P, (c + 1) * P)


class Own:

    def __init__(self, eng, sem, per=0):
        self.eng, self.sem, self.per, self.base, self.n = eng, sem, per, 0, 0

    def at(self, i):
        self.base, self.n = i * self.per, 0

    def done(self, ins):
        self.step(ins)
        self.wait()

    def step(self, ins):
        ins.then_inc(self.sem, 1)
        self.n += 1

    def skip(self):
        self.eng.sem_inc(self.sem, 1)
        self.n += 1

    def wait(self):
        self.eng.wait_ge(self.sem, past(self.base + self.n))

    def check(self):
        assert self.n == self.per, (self.n, self.per)


def past(count):
    return count + 1


def prime(eng, sems):
    for s in sems:
        eng.sem_inc(s, 1)


def constants(nc, pool, C, filled, cut, ident_ready):
    nc.gpsimd.memset(C["ident"][:], 0.0).then_inc(filled, 1)
    pool.wait_ge(filled, 1)
    nc.gpsimd.affine_select(out=C["ident"][:], in_=C["ident"][:], compare_op=ALU.not_equal, fill=1.0,
                            base=0, pattern=[[-1, P]], channel_multiplier=1).then_inc(ident_ready, 1)
    nc.gpsimd.memset(C["ones"][:], 1.0)
    nc.gpsimd.memset(C["tri"][:], 1.0)
    nc.gpsimd.memset(C["below"][:], 0.0)
    nc.gpsimd.memset(C["reset"][:], 1.0)
    nc.gpsimd.memset(C["lmask"][:], 1.0).then_inc(filled, 1)
    pool.wait_ge(filled, 2)
    nc.gpsimd.affine_select(out=C["tri"][:], in_=C["tri"][:], compare_op=ALU.is_ge, fill=0.0,
                            base=0, pattern=[[1, P]], channel_multiplier=-1)
    nc.gpsimd.affine_select(out=C["below"][:], in_=C["below"][:], compare_op=ALU.is_ge, fill=1.0e30,
                            base=0, pattern=[[1, P]], channel_multiplier=-1)
    nc.gpsimd.affine_select(out=C["reset"][:].rearrange("p (c l) -> p c l", l=P),
                            in_=C["reset"][:].rearrange("p (c l) -> p c l", l=P),
                            compare_op=ALU.is_gt, fill=0.0,
                            base=0, pattern=[[0, NB], [1, P]], channel_multiplier=0)
    n = 0
    for j in range(LEVELS):
        h = P >> (j + 1)
        m = C["lmask"][:, j, :].rearrange("p (q two r) -> p q two r", two=2, r=h)
        nq = P // (2 * h)
        nc.gpsimd.memset(m[:, :, 0, :], 0.0)
        right = m[:, :, 1, :]
        nc.gpsimd.affine_select(out=right, in_=right, compare_op=ALU.is_ge, fill=0.0, base=0,
                                pattern=[[-2 * h, nq], [0, h]], channel_multiplier=1).then_inc(cut, 1)
        n += 1
        pool.wait_ge(cut, n)
        nc.gpsimd.affine_select(out=right, in_=right, compare_op=ALU.is_gt, fill=0.0, base=h,
                                pattern=[[2 * h, nq], [0, h]], channel_multiplier=-1)
    nc.gpsimd.affine_select(out=C["lmask"][:, LEVELS, :], in_=C["lmask"][:, LEVELS, :],
                            compare_op=ALU.is_equal, fill=0.0,
                            base=0, pattern=[[-1, P]], channel_multiplier=1).then_inc(cut, 1)
    pool.wait_ge(cut, n + 1)


def input_norm(nc, x, ln_w, w_ssd, C, hnT, w_group, group_in):
    with ExitStack() as ctx:
        def sb(name, shape, dt=F32):
            return ctx.enter_context(nc.sbuf_tensor("nrm_" + name, shape, dt))

        primed = []

        def plain_sem(name):
            return ctx.enter_context(nc.semaphore("nrm_" + name))

        def sem(name):
            primed.append(plain_sem(name))
            return primed[-1]

        xs = sb("xs", [P, NB, D])
        sq = sb("sq", [P, D])
        ss = sb("ss", [P, NB])
        rs = sb("rs", [P, NB])
        lnw = sb("lnw", [P, KT])
        BANKS = 4
        ps = ctx.enter_context(nc.psum_tensor("nrm_ps", [P, BANKS, 512], F32))
        x_in = [plain_sem(f"x_in{b}") for b in range(NB)]
        w_in = plain_sem("w_in")
        squared, rooted, meaned, inverse, scaled, turned, stored = (
            sem("squared"), sem("rooted"), sem("meaned"), sem("inverse"), sem("scaled"), sem("turned"),
            sem("stored"))
        filled, cut, ident_ready = plain_sem("filled"), plain_sem("cut"), plain_sem("ident_ready")
        xd = x.rearrange("o (b p) d -> p (o b) d", p=P)
        block = ctx.enter_context(nc.Block())

        @block.sync
        def _(sp):
            for b in range(NB):
                sp.dma_start(xs[:, b, :], xd[:, b, :]).then_inc(x_in[b], 16)
                if b == 0:
                    prime(sp, primed)
                    sp.dma_start(lnw[:], ln_w).then_inc(w_in, 16)
            for i, part in enumerate(SSD_PARTS):
                sp.dma_start(w_group[:, :, part], w_ssd[0, :, :, part]).then_inc(group_in[i], 16)

        @block.gpsimd
        def _(pool):
            constants(nc, pool, C, filled, cut, ident_ready)

        @block.scalar
        def _(act):
            for half in range(2):
                for b in range(HC * half, HC * (half + 1)):
                    act.wait_ge(x_in[b], 16)
                    if b >= 1:
                        act.wait_ge(squared, past(b))
                    nc.scalar.activation(sq[:], xs[:, b, :], ACT.Square, accum_out=ss[:, b:b + 1]).then_inc(squared, 1)
                hb = slice(HC * half, HC * (half + 1))
                act.wait_ge(meaned, past(half + 1))
                nc.scalar.activation(rs[:, hb], ss[:, hb], ACT.Sqrt).then_inc(rooted, 1)
            act.wait_ge(w_in, 16)
            for n in range(2 * KT):
                act.wait_ge(turned, past(n + 1))
                half, k = n // KT, n % KT
                nc.scalar.activation(hnT[:, k, half * 512:half * 512 + 512], ps[:, n % BANKS, :], ACT.Copy,
                                     scale=lnw[:, k:k + 1]).then_inc(stored, 1)

        @block.vector
        def _(dve):
            for half in range(2):
                hb = slice(HC * half, HC * (half + 1))
                dve.wait_ge(squared, past(HC * (half + 1)))
                nc.vector.tensor_scalar(ss[:, hb], ss[:, hb], 1.0 / D, EPS, ALU.mult, ALU.add).then_inc(meaned, 1)
                dve.wait_ge(rooted, past(half + 1))
                nc.vector.reciprocal(rs[:, hb], rs[:, hb]).then_inc(inverse, 1)
                dve.wait_ge(inverse, past(half + 1))
                for b in range(HC * half, HC * (half + 1)):
                    nc.vector.tensor_scalar(xs[:, b, :], xs[:, b, :], rs[:, b:b + 1], None, ALU.mult).then_inc(scaled, 1)

        @block.tensor
        def _(pe):
            pe.wait_ge(ident_ready, 1)
            for n in range(2 * KT):
                half, k = n // KT, n % KT
                pe.wait_ge(scaled, past(HC * (half + 1)))
                if n >= BANKS:
                    pe.wait_ge(stored, past(n - BANKS + 1))
                for j in range(HC):
                    mm = nc.tensor.transpose(ps[:, n % BANKS, j * P:(j + 1) * P],
                                             xs[:, HC * half + j, k * P:(k + 1) * P], C["ident"][:])
                mm.then_inc(turned, 1)


def first_weights(Y, kt):
    return Y[:, kt // 2, D + kt % 2 * HG_COLS:D + (kt % 2 + 1) * HG_COLS]


def first_piece(Y, half, p):
    if p < 2:
        return Y[:, KT // 2 + p, D + half * HALF:D + (half + 1) * HALF]
    return Y[:, KT // 2 + 2 + half, D + (p - 2) * 2 * P:D + (p - 1) * 2 * P]


def ssd(nc, w, w_in, w_ssd, par, w_hg, C, hnT, Y):
    with ExitStack() as ctx:
        def sb(name, shape, dt=F32):
            return ctx.enter_context(nc.sbuf_tensor("ssd_" + name, shape, dt))

        primed = []

        def plain_sem(name):
            return ctx.enter_context(nc.semaphore("ssd_" + name))

        def sem(name):
            primed.append(plain_sem(name))
            return primed[-1]

        def psum(name, shape):
            return ctx.enter_context(nc.psum_tensor("ssd_" + name, shape, F32))

        PAD = TAPS - 1
        pr = sb("pr", [P, GROUPS, NPAR])
        ah = sb("ah", [P, GROUPS, HPG])
        raw = sb("raw", [P, 2, CT, PAD + HALF])
        rawz = sb("rawz", [P, NB, XW + HPG])
        xc = sb("xc", [P, CT, SEQ])
        zs = sb("zs", [P, NB, XW])
        step5 = sb("step5", [P, 5, HC, HPG])
        dt = sb("dt", [P, NB, HPG])
        a = sb("a", [P, NB, HPG])
        acum = sb("acum", [P, NB, HPG])
        aend = sb("aend", [P, NB, HPG])
        from_start = sb("from_start", [P, NB, HPG])
        to_end = sb("to_end", [P, NB, HPG])
        decay_all = sb("decay_all", [P, NB, HPG])
        awide = sb("awide", [P, HPG, P])
        natural = sb("natural", [P, 3 * P])
        dec = sb("dec", [P, HPG, P])
        att = sb("att", [P, HPG, P])
        xdt = sb("xdt", [P, HPG, HD])
        xdte = sb("xdte", [P, HPG, HD])
        y = sb("y", [P, HPG, HD])
        skip = sb("skip", [P, HPG, HD])
        state = sb("state", [P, HPG, HD])

        ps_piece = psum("ps_piece", [P, 2, 512])
        ps_cb = psum("ps_cb", [P, 512])
        ps_turn = psum("ps_turn", [P, 512])
        ps_rows = psum("ps_rows", [P, HPG, P])
        ps_y = psum("ps_y", [P, 2, HPG, HD])
        ps_state = psum("ps_state", [P, 512])
        ps_sum = psum("ps_sum", [P, 512])

        par_in, head_in = plain_sem("par_in"), plain_sem("head_in")
        padded, a_logged = sem("padded"), sem("a_logged")
        piece_made, piece_out = sem("piece_made"), sem("piece_out")
        raw_used = sem("raw_used")
        convolved, activated, z_activated = sem("convolved"), sem("activated"), sem("z_activated")
        dt_raw, dt_exp, dt_onep, dt_log, dt_ready = (sem("dt_raw"), sem("dt_exp"), sem("dt_onep"),
                                                     sem("dt_log"), sem("dt_ready"))
        summed, sums_out, exps_ready = sem("summed"), sem("sums_out"), sem("exps_ready")
        wide_ready = sem("wide_ready")
        stage_a, natural_out = sem("stage_a"), sem("natural_out")
        diff_ready, dec_ready, att_ready = sem("diff_ready"), sem("dec_ready"), sem("att_ready")
        stage_b, chunk_done, state_ready = sem("stage_b"), sem("chunk_done"), sem("state_ready")
        own_prep, own_mix = sem("own_prep"), sem("own_mix")
        block = ctx.enter_context(nc.Block())

        def groups(eng, body):
            with eng.Fori(0, GROUPS - 1) as u:
                body(u, False)
            body(GROUPS - 1, True)

        @block.sync
        def _(sp):
            prime(sp, primed)
            sp.dma_start(pr[:], par).then_inc(par_in, 16)
            for kt in range(KT):
                sp.dma_start(first_weights(Y, kt), w_hg[0, :, kt, :]).then_inc(head_in, 16)
            with sp.Fori(1, GROUPS) as u:
                for i, part in enumerate(SSD_PARTS):
                    sp.wait_ge(piece_made, past(u * 2 * SSD_PIECES - (SSD_PIECES - 2 * i - 1 if i < CT else 0)))
                    sp.dma_start(w[:, :, part], w_ssd[bass.ds(u, 1), :, :, part].rearrange("o p k c -> p (o k) c")
                                 ).then_inc(w_in[i], 16)

        @block.gpsimd
        def _(pool):
            nc.gpsimd.memset(raw[:, 0, :, 0:PAD], 0.0).then_inc(padded, 1)
            with pool.Fori(0, GROUPS) as u:
                for c in range(NB):
                    if c % HC == 0:
                        pool.wait_ge(dt_ready, past(u * 2 + c // HC + 1))
                    pool.wait_ge(stage_a, past(u * NB + c))
                    nc.gpsimd.tensor_tensor(awide[:], a[:, c, :].unsqueeze(2).to_broadcast([P, HPG, P]),
                                            C["ones"][:].unsqueeze(1).to_broadcast([P, HPG, P]),
                                            ALU.mult).then_inc(wide_ready, 1)

        @block.tensor
        def _(pe):
            def piece(u, half, p):
                if half == 0 and (p % 2 == 0 or p == 1):
                    pe.wait_ge(w_in[p // 2 if p % 2 == 0 else CT], (u + 1) * 16)
                n = (u * 2 + half) * SSD_PIECES + p
                if not (isinstance(n, int) and n < 2):
                    pe.wait_ge(piece_out, past(n - 1))
                bank = ps_piece[:, p % 2, :]
                for k in range(KT):
                    if p % 2 == 0:
                        i = p // 2
                        mm = nc.tensor.matmul(bank, w[:, k, i * P:(i + 1) * P],
                                              hnT[:, k, half * HALF:(half + 1) * HALF],
                                              start=(k == 0), stop=(k == KT - 1))
                    else:
                        mm = nc.tensor.matmul(bank[:, 0:XW + HPG], hnT[:, k, cols(half * HC + p // 2)],
                                              w[:, k, CT * P:SSD_COLS], start=(k == 0), stop=(k == KT - 1))
                mm.then_inc(piece_made, 1)

            def head_piece(half, p):
                pe.wait_ge(head_in, 16 * KT)
                pe.wait_ge(piece_out, past(GROUPS * 2 * SSD_PIECES + half * HG_PIECES + p - 1))
                bank = ps_piece[:, p % 2, :]
                for kt in range(KT):
                    wk = first_weights(Y, kt)
                    if p < 2:
                        mm = nc.tensor.matmul(bank, wk[:, p * P:(p + 1) * P], hnT[:, kt, half * HALF:(half + 1) * HALF],
                                              start=(kt == 0), stop=(kt == KT - 1))
                    else:
                        mm = nc.tensor.matmul(bank[:, 0:2 * P], hnT[:, kt, cols(half * HC + p - 2)],
                                              wk[:, 2 * P:4 * P], start=(kt == 0), stop=(kt == KT - 1))
                mm.then_inc(piece_made, 1)

            def sums(n, half):
                pe.wait_ge(dt_ready, past(n + 1))
                pe.wait_ge(sums_out, past(n))
                av = a[:, half * HC:(half + 1) * HC, :].rearrange("p c r -> p (c r)")
                m = HC * HPG
                nc.tensor.matmul(ps_sum[:, 0:m], C["tri"][:], av, start=True, stop=True)
                nc.tensor.matmul(ps_sum[:, m:2 * m], C["ones"][:], av, start=True, stop=True).then_inc(summed, 1)

            def body(u, last):
                for c in range(NB):
                    half = c // HC
                    if c % HC == 0:
                        pe.wait_ge(activated, past((u * 2 + half + 1) * CT))
                    pe.wait_ge(wide_ready, past(u * NB + c + 1))
                    pe.wait_ge(att_ready, past(u * NB + c))
                    nc.tensor.matmul(ps_cb[:, 0:P], xc[:, 2, cols(c)], xc[:, 3, cols(c)], start=True, stop=True)
                    for i in range(3):
                        nc.tensor.transpose(ps_turn[:, i * P:(i + 1) * P], xc[:, i, cols(c)], C["ident"][:])
                    for r in range(HPG):
                        mm = nc.tensor.matmul(ps_rows[:, r, :], awide[:, r, :], C["tri"][:], start=True, stop=True)
                    mm.then_inc(stage_a, 1)
                    if not last:
                        piece(u + 1, half, 2 * (c % HC))
                        piece(u + 1, half, 2 * (c % HC) + 1)
                    else:
                        for p in HEAD_PARTS[c % HC]:
                            head_piece(half, p)
                    if c % HC == HC - 2 and not (last and half == 1):
                        sums(u * 2 + half + 1, 1 - half)
                    pe.wait_ge(state_ready, past(u * NB + c + 1))
                    pe.wait_ge(chunk_done, past(u * NB + c))
                    pe.wait_ge(att_ready, past(u * NB + c + 1))
                    nc.tensor.matmul(ps_y[:, 0].rearrange("p r d -> p (r d)"), xc[:, 3, cols(c)],
                                     state[:].rearrange("p r d -> p (r d)"), start=True, stop=True)
                    for r in range(HPG):
                        nc.tensor.matmul(ps_y[:, 1, r, :], att[:, r, :], xdt[:, r, :], start=True, stop=True)
                    nc.tensor.matmul(ps_state[:, 0:XW], natural[:, 2 * P:3 * P],
                                     xdte[:].rearrange("p r d -> p (r d)"), start=True, stop=True).then_inc(stage_b, 1)

            for half in range(2):
                for p in range(SSD_PIECES):
                    piece(0, half, p)
            sums(0, 0)
            groups(pe, body)

        @block.scalar
        def _(act):
            act.wait_ge(par_in, 16)
            act.wait_ge(padded, past(1))
            nc.scalar.activation(ah[:], pr[:, :, ALG:ALG + HPG], ACT.Exp).then_inc(a_logged, 1)

            def out(u, half, p):
                n = u * 2 + half
                act.wait_ge(piece_made, past(n * SSD_PIECES + p + 1))
                if p == 0 and not isinstance(n, int):
                    act.wait_ge(raw_used, past(n - 1))
                if p % 2 == 0:
                    nc.scalar.activation(raw[:, half, p // 2, PAD:PAD + HALF], ps_piece[:, p % 2, :],
                                         ACT.Copy).then_inc(piece_out, 1)
                else:
                    nc.scalar.activation(rawz[:, half * HC + p // 2, :], ps_piece[:, p % 2, 0:XW + HPG],
                                         ACT.Copy).then_inc(piece_out, 1)

            def head_out(half, p):
                act.wait_ge(piece_made, past(GROUPS * 2 * SSD_PIECES + half * HG_PIECES + p + 1))
                bank = ps_piece[:, p % 2, 0:HALF if p < 2 else 2 * P]
                nc.scalar.activation(first_piece(Y, half, p), bank, ACT.Copy).then_inc(piece_out, 1)

            def prepare(n, half, part):
                hb, ht = slice(half * HC, (half + 1) * HC), slice(half * HALF, (half + 1) * HALF)
                if part == 0:
                    act.wait_ge(dt_raw, past(n + 1))
                    nc.scalar.activation(step5[:, 1], step5[:, 0], ACT.Abs).then_inc(dt_exp, 1)
                    act.wait_ge(dt_exp, past(2 * n + 1))
                    nc.scalar.activation(step5[:, 1], step5[:, 1], ACT.Exp, scale=-1.0).then_inc(dt_exp, 1)
                    act.wait_ge(dt_onep, past(n + 1))
                    nc.scalar.activation(step5[:, 3], step5[:, 2], ACT.Ln).then_inc(dt_log, 1)
                elif part in (1, 2):
                    if part == 1:
                        nc.scalar.activation(zs[:, hb, :], rawz[:, hb, 0:XW], ACT.Silu).then_inc(z_activated, 1)
                    for i in (0, 1) if part == 1 else (2, 3):
                        act.wait_ge(convolved, past(n * CT + i + 1))
                        nc.scalar.activation(xc[:, i, ht], xc[:, i, ht], ACT.Silu).then_inc(activated, 1)
                else:
                    act.wait_ge(sums_out, past(n + 1))
                    nc.scalar.activation(from_start[:, hb, :], acum[:, hb, :], ACT.Exp, scale=-1.0)
                    nc.scalar.activation(to_end[:, hb, :], to_end[:, hb, :], ACT.Exp, scale=-1.0)
                    nc.scalar.activation(decay_all[:, hb, :], aend[:, hb, :], ACT.Exp, scale=-1.0).then_inc(exps_ready, 1)

            def body(u, last):
                for c in range(NB):
                    half = c // HC
                    act.wait_ge(stage_a, past(u * NB + c + 1))
                    act.wait_ge(chunk_done, past(u * NB + c))
                    nc.scalar.activation(natural[:], ps_turn[:, 0:3 * P], ACT.Copy).then_inc(natural_out, 1)
                    act.wait_ge(diff_ready, past(u * NB + c + 1))
                    nc.scalar.activation(dec[:], dec[:], ACT.Exp, scale=-1.0).then_inc(dec_ready, 1)
                    if not last:
                        out(u + 1, half, 2 * (c % HC))
                    else:
                        head_out(half, HEAD_PARTS[c % HC][0])
                    if not (last and half == 1):
                        prepare(u * 2 + half + 1, 1 - half, c % HC)
                    if not last:
                        out(u + 1, half, 2 * (c % HC) + 1)
                    else:
                        for p in HEAD_PARTS[c % HC][1:]:
                            head_out(half, p)

            for half in range(2):
                for p in range(SSD_PIECES):
                    out(0, half, p)
                if half == 0:
                    for part in range(3):
                        prepare(0, 0, part)
            prepare(0, 0, 3)
            groups(act, body)

        @block.vector
        def _(dve):
            prep, own = Own(dve, own_prep, 6 + CT * (TAPS - 1) + 2), Own(dve, own_mix, HC * 8)

            def per_head(ap):
                return ap.unsqueeze(1).to_broadcast([P, HC, HPG])

            def prepare(u, half, part):
                n = u * 2 + half
                hb, ht = slice(half * HC, (half + 1) * HC), slice(half * HALF, (half + 1) * HALF)
                pu = pr[:, bass.ds(u, 1), :].rearrange("p o c -> p (o c)")
                ahu = ah[:, bass.ds(u, 1), :].rearrange("p o c -> p (o c)")

                def convolve(i):
                    wi = (TAPS + 1) * i
                    prep.done(nc.vector.tensor_scalar(xc[:, i, ht], raw[:, half, i, PAD:PAD + HALF],
                                                      pu[:, wi + PAD:wi + PAD + 1], pu[:, wi + TAPS:wi + TAPS + 1],
                                                      ALU.mult, ALU.add))
                    for k in range(PAD):
                        ins = nc.vector.scalar_tensor_tensor(out=xc[:, i, ht], in0=raw[:, half, i, k:k + HALF],
                                                             scalar=pu[:, wi + k:wi + k + 1], in1=xc[:, i, ht],
                                                             op0=ALU.mult, op1=ALU.add)
                        if k < PAD - 1:
                            prep.done(ins)
                        else:
                            ins.then_inc(convolved, 1)

                if part == 0:
                    prep.at(n)
                    dve.wait_ge(piece_out, past((n + 1) * SSD_PIECES))
                    nc.vector.tensor_tensor(step5[:, 0], rawz[:, hb, XW:XW + HPG], per_head(pu[:, DTB:DTB + HPG]),
                                            ALU.add).then_inc(dt_raw, 1)
                    convolve(0)
                    dve.wait_ge(dt_exp, past(2 * n + 2))
                    nc.vector.tensor_scalar(step5[:, 2], step5[:, 1], 1.0, None, ALU.add).then_inc(dt_onep, 1)
                elif part == 1:
                    dve.wait_ge(dt_onep, past(n + 1))
                    prep.done(nc.vector.tensor_scalar(step5[:, 4], step5[:, 2], 1.0, None, ALU.subtract))
                    prep.done(nc.vector.tensor_tensor(step5[:, 4], step5[:, 1], step5[:, 4], ALU.subtract))
                    dve.wait_ge(dt_log, past(n + 1))
                    prep.done(nc.vector.reciprocal(step5[:, 2], step5[:, 2]))
                    prep.done(nc.vector.tensor_tensor(step5[:, 4], step5[:, 4], step5[:, 2], ALU.mult))
                    prep.done(nc.vector.tensor_tensor(step5[:, 4], step5[:, 4], step5[:, 3], ALU.add))
                    prep.done(nc.vector.scalar_tensor_tensor(out=dt[:, hb, :], in0=step5[:, 0], scalar=0.0,
                                                             in1=step5[:, 4], op0=ALU.max, op1=ALU.add))
                    nc.vector.tensor_tensor(a[:, hb, :], dt[:, hb, :], per_head(ahu), ALU.mult).then_inc(dt_ready, 1)
                    convolve(1)
                elif part == 2:
                    convolve(2)
                    convolve(3)
                    if half == 1:
                        prep.skip()
                    else:
                        prep.done(nc.vector.tensor_copy(raw[:, 1, :, 0:PAD], raw[:, 0, :, HALF:HALF + PAD]))
                    dve.wait_ge(convolved, past((n + 1) * CT))
                    dve.sem_inc(raw_used, 1)
                else:
                    dve.wait_ge(summed, past(n + 1))
                    m = HC * HPG
                    nc.vector.tensor_copy(aend[:, hb, :].rearrange("p c r -> p (c r)"), ps_sum[:, m:2 * m])
                    prep.done(nc.vector.tensor_copy(acum[:, hb, :].rearrange("p c r -> p (c r)"), ps_sum[:, 0:m]))
                    nc.vector.tensor_tensor(to_end[:, hb, :], aend[:, hb, :], acum[:, hb, :],
                                            ALU.subtract).then_inc(sums_out, 1)
                    prep.check()

            def body(u, last):
                pu = pr[:, bass.ds(u, 1), :].rearrange("p o c -> p (o c)")
                for c in range(NB):
                    half = c // HC
                    if c % HC == 0:
                        own.at(u * 2 + half)
                        dve.wait_ge(exps_ready, past(u * 2 + half + 1))
                    if c == 0:
                        dve.wait_ge(stage_b, past(u * NB))
                        nc.vector.memset(state[:], 0.0).then_inc(state_ready, 1)

                    def wide(ap):
                        return ap[:, c, :].unsqueeze(2).to_broadcast([P, HPG, HD])

                    dve.wait_ge(stage_a, past(u * NB + c + 1))
                    dve.wait_ge(stage_b, past(u * NB + c))
                    for r in range(HPG):
                        ins = nc.vector.scalar_tensor_tensor(out=dec[:, r, :], in0=ps_rows[:, r, :],
                                                             scalar=acum[:, c, r:r + 1], in1=C["below"][:],
                                                             op0=ALU.subtract, op1=ALU.max)
                    ins.then_inc(diff_ready, 1)
                    dve.wait_ge(natural_out, past(u * NB + c + 1))
                    xn = natural[:, 0:XW].rearrange("p (r d) -> p r d", r=HPG)
                    own.done(nc.vector.tensor_tensor(xdt[:], xn, wide(dt), ALU.mult))
                    nc.vector.tensor_tensor(xdte[:], xdt[:], wide(to_end), ALU.mult)
                    own.done(nc.vector.tensor_tensor(
                        skip[:], xn, pu[:, DSK:DSK + HPG].unsqueeze(2).to_broadcast([P, HPG, HD]), ALU.mult))
                    dve.wait_ge(dec_ready, past(u * NB + c + 1))
                    nc.vector.tensor_tensor(att[:], dec[:], ps_cb[:, 0:P].unsqueeze(1).to_broadcast([P, HPG, P]),
                                            ALU.mult).then_inc(att_ready, 1)
                    if not (last and half == 1):
                        prepare(u + half, 1 - half, c % HC)
                    dve.wait_ge(stage_b, past(u * NB + c + 1))
                    own.done(nc.vector.tensor_tensor(state[:], state[:], wide(decay_all), ALU.mult))
                    ins = nc.vector.tensor_tensor(state[:], state[:],
                                                  ps_state[:, 0:XW].rearrange("p (r d) -> p r d", r=HPG), ALU.add)
                    own.done(ins)
                    if c < NB - 1:
                        dve.sem_inc(state_ready, 1)
                    own.done(nc.vector.tensor_tensor(y[:], ps_y[:, 0], wide(from_start), ALU.mult))
                    own.done(nc.vector.tensor_tensor(y[:], y[:], ps_y[:, 1], ALU.add))
                    own.done(nc.vector.tensor_tensor(y[:], y[:], skip[:], ALU.add))
                    own.done(nc.vector.tensor_tensor(
                        Y[:, c, bass.ds(u * XW, XW)], y[:].rearrange("p r d -> p (r d)"), zs[:, c, :], ALU.mult))
                    dve.sem_inc(chunk_done, 1)
                    if c % HC == HC - 1:
                        own.check()

            dve.wait_ge(a_logged, past(1))
            for part in range(4):
                prepare(0, 0, part)
            groups(dve, body)


def hgrn(nc, w_hg, lb_logits, C, hnT, Y, osq):
    with ExitStack() as ctx:
        def sb(name, shape, dt=F32):
            return ctx.enter_context(nc.sbuf_tensor("hg_" + name, shape, dt))

        primed = []

        def plain_sem(name):
            return ctx.enter_context(nc.semaphore("hg_" + name))

        def sem(name):
            primed.append(plain_sem(name))
            return primed[-1]

        def psum(name, shape):
            return ctx.enter_context(nc.psum_tensor("hg_" + name, shape, F32))

        w = sb("w", [P, KT, HG_COLS])
        lbl = sb("lbl", [P, 2, HEADS])
        lb = sb("lb", [P, HEADS])
        oml = sb("oml", [P, HEADS])
        raw_q = sb("raw_q", [P, SEQ])
        raw_f = sb("raw_f", [P, SEQ])
        raw_vg = sb("raw_vg", [P, NB, 2 * P])
        q = sb("q", [P, SEQ])
        k = sb("k", [P, SEQ])
        G = sb("G", [P, SEQ])
        W = sb("W", [P, LEVELS, SEQ])
        qs = sb("qs", [P, SEQ])
        ke = sb("ke", [P, SEQ])
        gend = sb("gend", [P, NB])
        v = sb("v", [P, NB, P])
        gs = sb("gs", [P, NB, P])
        junk = sb("junk", [P, P])
        ss = sb("ss", [P, NB])
        masked = sb("masked", [P, LEVELS + 1, P])
        att = sb("att", [P, P])
        ken = sb("ken", [P, P])
        state = sb("state", [P, P])

        ps_piece = psum("ps_piece", [P, 2, 512])
        ps_att = psum("ps_att", [P, LEVELS + 1, P])
        ps_turn = psum("ps_turn", [P, 512])
        ps_o = psum("ps_o", [P, 512])
        ps_state = psum("ps_state", [P, 512])

        w_in, lb_in = [plain_sem(f"w_in{i}") for i in range(len(HG_PARTS))], plain_sem("lb_in")
        lb_diff, lb_ready = sem("lb_diff"), sem("lb_ready")
        piece_made, piece_out = sem("piece_made"), sem("piece_out")
        gate_sig, gate_ready, gate_logged, summed = (sem("gate_sig"), sem("gate_ready"), sem("gate_logged"),
                                                     sem("summed"))
        q_ready, v_ready, g_ready = sem("q_ready"), sem("v_ready"), sem("g_ready")
        span, decayed, weighted = sem("span"), sem("decayed"), sem("weighted")
        stage_a, stage_b, mask_done = sem("stage_a"), sem("stage_b"), sem("mask_done")
        ken_ready, att_ready, state_ready = sem("ken_ready"), sem("att_ready"), sem("state_ready")
        o_squared, o_gated, kept = sem("o_squared"), sem("o_gated"), sem("kept")
        own_prep, cleared = sem("own_prep"), sem("cleared")
        block = ctx.enter_context(nc.Block())

        EARLY = 4

        def heads(eng, body):
            with eng.Fori(0, HEADS - 1) as u:
                body(u, False)
            body(HEADS - 1, True)

        @block.sync
        def _(sp):
            prime(sp, primed)
            sp.dma_start(lbl[:], lb_logits).then_inc(lb_in, 16)
            for i, part in enumerate(HG_PARTS):
                sp.dma_start(w[:, :, part], w_hg[1, :, :, part]).then_inc(w_in[i], 16)
            with sp.Fori(2, HEADS) as u:
                for i, part in enumerate(HG_PARTS):
                    sp.wait_ge(piece_made, past(u * 2 * HG_PIECES - (HG_PIECES - i - 1 if i < 2 else 0)))
                    sp.dma_start(w[:, :, part], w_hg[bass.ds(u, 1), :, :, part].rearrange("o p k c -> p (o k) c")
                                 ).then_inc(w_in[i], 16)

        @block.tensor
        def _(pe):
            def piece(u, half, p):
                if half == 0 and p <= 2:
                    pe.wait_ge(w_in[p], u * 16)
                n = (u * 2 + half) * HG_PIECES + p
                pe.wait_ge(piece_out, past(n - 1))
                bank = ps_piece[:, p % 2, :]
                for kt in range(KT):
                    if p < 2:
                        mm = nc.tensor.matmul(bank, w[:, kt, p * P:(p + 1) * P],
                                              hnT[:, kt, half * HALF:(half + 1) * HALF],
                                              start=(kt == 0), stop=(kt == KT - 1))
                    else:
                        mm = nc.tensor.matmul(bank[:, 0:2 * P], hnT[:, kt, cols(half * HC + p - 2)],
                                              w[:, kt, 2 * P:4 * P], start=(kt == 0), stop=(kt == KT - 1))
                mm.then_inc(piece_made, 1)

            def body(u, last):
                for c in range(NB):
                    half = c // HC
                    if c % HC == 0:
                        pe.wait_ge(weighted, past((u * 2 + half + 1) * (LEVELS + 2)))
                        pe.wait_ge(v_ready, past(u * 2 + half + 1))
                    pe.wait_ge(att_ready, past(u * NB + c))
                    pe.wait_ge(ken_ready, past(u * NB + c))
                    for j in range(LEVELS):
                        right = W[:, j, cols(c)].rearrange("p (b two h) -> p b two h", two=2, h=P >> (j + 1))
                        nc.tensor.matmul(ps_att[:, j, 0:P // 2], W[:, j, cols(c)], right[:, :, 1, :],
                                         start=True, stop=True)
                    nc.tensor.matmul(ps_att[:, LEVELS, :], k[:, cols(c)], q[:, cols(c)], start=True, stop=True)
                    nc.tensor.transpose(ps_turn[:, 0:P], ke[:, cols(c)], C["ident"][:]).then_inc(stage_a, 1)
                    if not last:
                        for p in HEAD_PARTS[c % HC]:
                            piece(u + 1, half, p)
                    pe.wait_ge(state_ready, past(u * NB + c + 1))
                    pe.wait_ge(o_gated, past(u * NB + c))
                    pe.wait_ge(o_squared, past(u * NB + c))
                    pe.wait_ge(ken_ready, past(u * NB + c + 1))
                    nc.tensor.matmul(ps_state[:, 0:P], ken[:], v[:, c, :], start=True, stop=True)
                    nc.tensor.matmul(ps_o[:, 0:P], qs[:, cols(c)], state[:], start=True, stop=False)
                    pe.wait_ge(att_ready, past(u * NB + c + 1))
                    nc.tensor.matmul(ps_o[:, 0:P], att[:], v[:, c, :], start=False, stop=True).then_inc(stage_b, 1)

            pe.sem_inc(piece_made, 2 * HG_PIECES)
            heads(pe, body)

        @block.scalar
        def _(act):
            act.wait_ge(lb_diff, past(1))
            nc.scalar.activation(lb[:], lb[:], ACT.Sigmoid).then_inc(lb_ready, 1)
            act.wait_ge(lb_ready, past(1))
            nc.scalar.activation(oml[:], lb[:], ACT.Copy, scale=-1.0, bias=1.0).then_inc(lb_ready, 1)

            def first_out(half, p):
                place = (raw_q, raw_f)[p][:, half * HALF:(half + 1) * HALF] if p < 2 else raw_vg[:, half * HC + p - 2, :]
                nc.scalar.activation(place, first_piece(Y, half, p), ACT.Copy).then_inc(piece_out, 1)

            def out(u, half, p):
                n = u * 2 + half
                act.wait_ge(piece_made, past(n * HG_PIECES + p + 1))
                if p < 2:
                    nc.scalar.activation((raw_q, raw_f)[p][:, half * HALF:(half + 1) * HALF], ps_piece[:, p % 2, :],
                                         ACT.Copy).then_inc(piece_out, 1)
                else:
                    if p == 2:
                        act.wait_ge(v_ready, past(n - 1))
                    nc.scalar.activation(raw_vg[:, half * HC + p - 2, :], ps_piece[:, p % 2, 0:2 * P],
                                         ACT.Copy).then_inc(piece_out, 1)

            def prepare(n, half, part):
                hb, ht = slice(half * HC, (half + 1) * HC), slice(half * HALF, (half + 1) * HALF)
                if part == 0:
                    act.wait_ge(piece_out, past((n + 1) * HG_PIECES))
                    nc.scalar.activation(G[:, ht], raw_f[:, ht], ACT.Sigmoid).then_inc(gate_sig, 1)
                    nc.scalar.activation(q[:, ht], raw_q[:, ht], ACT.Silu).then_inc(q_ready, 1)
                    nc.scalar.activation(gs[:, hb, :], raw_vg[:, hb, P:2 * P], ACT.Silu).then_inc(g_ready, 1)
                    act.wait_ge(gate_ready, past(n + 1))
                    nc.scalar.activation(G[:, ht], G[:, ht], ACT.Ln).then_inc(gate_logged, 1)
                elif part in (1, 2):
                    for j in range(EARLY) if part == 1 else range(EARLY, LEVELS):
                        act.wait_ge(span, past(n * (LEVELS + 1) + j + 1))
                        nc.scalar.activation(W[:, j, ht], W[:, j, ht], ACT.Exp).then_inc(decayed, 1)
                    if part == 2:
                        act.wait_ge(span, past((n + 1) * (LEVELS + 1)))
                        nc.scalar.activation(ke[:, ht], ke[:, ht], ACT.Exp).then_inc(decayed, 1)
                        nc.scalar.activation(qs[:, ht], G[:, ht], ACT.Exp).then_inc(decayed, 1)
                        nc.scalar.activation(gend[:, hb], G[:, ht].rearrange("p (c l) -> p c l", l=P)[:, :, P - 1],
                                             ACT.Exp).then_inc(decayed, 1)

            def body(u, last):
                for c in range(NB):
                    half = c // HC
                    act.wait_ge(stage_a, past(u * NB + c + 1))
                    act.wait_ge(stage_b, past(u * NB + c))
                    nc.scalar.activation(ken[:], ps_turn[:, 0:P], ACT.Copy).then_inc(ken_ready, 1)
                    if not last:
                        for p in HEAD_PARTS[c % HC]:
                            out(u + 1, half, p)
                    if not (last and half == 1):
                        prepare(u * 2 + half + 1, 1 - half, c % HC)
                    act.wait_ge(o_gated, past(u * NB + c + 1))
                    if c == 0:
                        act.wait_ge(kept, past(u))
                    act.wait_ge(o_squared, past(u * NB + c))
                    nc.scalar.activation(junk[:], ps_o[:, 0:P], ACT.Square,
                                         accum_out=ss[:, c:c + 1]).then_inc(o_squared, 1)

            for half in range(2):
                for p in range(HG_PIECES):
                    first_out(half, p)
                if half == 0:
                    prepare(0, 0, 0)
            for part in (1, 2):
                prepare(0, 0, part)
            heads(act, body)

        @block.vector
        def _(dve):
            prep = Own(dve, own_prep, 1)
            nc.vector.memset(masked[:], 0.0).then_inc(cleared, 1)
            dve.wait_ge(cleared, past(1))
            dve.wait_ge(lb_in, 16)
            nc.vector.tensor_tensor(lb[:], lbl[:, 0, :], lbl[:, 1, :], ALU.subtract).then_inc(lb_diff, 1)
            dve.wait_ge(lb_ready, past(2))

            def prepare(u, half, part):
                n = u * 2 + half
                hb, ht = slice(half * HC, (half + 1) * HC), slice(half * HALF, (half + 1) * HALF)

                def halves(ap, j):
                    return ap.rearrange("p (b two h) -> p b two h", two=2, h=P >> (j + 1))

                def spans(js):
                    for j in js:
                        h = P >> (j + 1)
                        gv, wv = halves(G[:, ht], j), halves(W[:, j, ht], j)
                        at = gv[:, :, 0, h - 1:h].to_broadcast([P, HALF // (2 * h), h])
                        nc.vector.tensor_tensor(wv[:, :, 0, :], at, gv[:, :, 0, :], ALU.subtract)
                        nc.vector.tensor_tensor(wv[:, :, 1, :], gv[:, :, 1, :], at, ALU.subtract).then_inc(span, 1)

                def weights(js):
                    for j in js:
                        dve.wait_ge(decayed, past(n * (LEVELS + 3) + j + 1))
                        wv = halves(W[:, j, ht], j)
                        nc.vector.tensor_tensor(wv[:, :, 0, :], wv[:, :, 0, :], halves(k[:, ht], j)[:, :, 0, :], ALU.mult)
                        nc.vector.tensor_tensor(wv[:, :, 1, :], wv[:, :, 1, :], halves(q[:, ht], j)[:, :, 1, :],
                                                ALU.mult).then_inc(weighted, 1)

                if part == 0:
                    prep.at(n)
                    dve.wait_ge(gate_sig, past(n + 1))
                    prep.done(nc.vector.tensor_scalar(G[:, ht], G[:, ht], oml[:, bass.ds(u, 1)], lb[:, bass.ds(u, 1)],
                                                      ALU.mult, ALU.add))
                    nc.vector.tensor_scalar(k[:, ht], G[:, ht], -1.0, 1.0, ALU.mult, ALU.add).then_inc(gate_ready, 1)
                    dve.wait_ge(piece_out, past((n + 1) * HG_PIECES))
                    nc.vector.tensor_copy(v[:, hb, :], raw_vg[:, hb, 0:P]).then_inc(v_ready, 1)
                elif part == 1:
                    dve.wait_ge(gate_logged, past(n + 1))
                    nc.vector.tensor_tensor_scan(G[:, ht], C["reset"][:, ht], G[:, ht], 0.0,
                                                 ALU.mult, ALU.add).then_inc(summed, 1)
                    dve.wait_ge(summed, past(n + 1))
                    spans(range(EARLY))
                elif part == 2:
                    spans(range(EARLY, LEVELS))
                    gc = G[:, ht].rearrange("p (c l) -> p c l", l=P)
                    nc.vector.tensor_tensor(ke[:, ht].rearrange("p (c l) -> p c l", l=P),
                                            gc[:, :, P - 1:P].to_broadcast([P, HC, P]), gc, ALU.subtract).then_inc(span, 1)
                    dve.wait_ge(q_ready, past(n + 1))
                    weights(range(EARLY))
                else:
                    weights(range(EARLY, LEVELS))
                    dve.wait_ge(decayed, past((n + 1) * (LEVELS + 3)))
                    nc.vector.tensor_tensor(ke[:, ht], ke[:, ht], k[:, ht], ALU.mult).then_inc(weighted, 1)
                    nc.vector.tensor_tensor(qs[:, ht], qs[:, ht], q[:, ht], ALU.mult).then_inc(weighted, 1)
                    prep.check()

            def body(u, last):
                dve.wait_ge(stage_b, past(u * NB))
                nc.vector.memset(state[:], 0.0).then_inc(state_ready, 1)
                for c in range(NB):
                    half = c // HC
                    if c % HC == 0:
                        dve.wait_ge(g_ready, past(u * 2 + half + 1))
                    dve.wait_ge(stage_a, past(u * NB + c + 1))
                    for j in range(LEVELS):
                        h = P >> (j + 1)

                        def right(ap):
                            return ap[:, j, :].rearrange("p (b two h) -> p b two h", two=2, h=h)[:, :, 1, :]

                        nc.vector.tensor_tensor(right(masked[:]), ps_att[:, j, 0:P // 2].rearrange("p (b h) -> p b h", h=h),
                                                right(C["lmask"][:]), ALU.mult)
                    nc.vector.tensor_tensor(masked[:, LEVELS, :], ps_att[:, LEVELS, :], C["lmask"][:, LEVELS, :],
                                            ALU.mult).then_inc(mask_done, 1)
                    dve.wait_ge(mask_done, past(u * NB + c + 1))
                    dve.wait_ge(stage_b, past(u * NB + c))
                    nc.vector.tensor_reduce(att[:], masked[:].rearrange("p j l -> p l j"), AX.X,
                                            ALU.add).then_inc(att_ready, 1)
                    if not (last and half == 1):
                        prepare(u + half, 1 - half, c % HC)
                    dve.wait_ge(stage_b, past(u * NB + c + 1))
                    if c < NB - 1:
                        dve.wait_ge(state_ready, past(u * NB + c + 1))
                        nc.vector.scalar_tensor_tensor(out=state[:], in0=state[:], scalar=gend[:, c:c + 1],
                                                       in1=ps_state[:, 0:P], op0=ALU.mult,
                                                       op1=ALU.add).then_inc(state_ready, 1)
                    nc.vector.tensor_tensor(Y[:, c, bass.ds(D + u * P, P)], ps_o[:, 0:P], gs[:, c, :],
                                            ALU.mult).then_inc(o_gated, 1)
                dve.wait_ge(o_squared, past((u + 1) * NB))
                nc.vector.tensor_scalar(osq[:, :, bass.ds(u, 1)].rearrange("p c o -> p (c o)"), ss[:], 1.0, None,
                                        ALU.mult).then_inc(kept, 1)

            for part in range(4):
                prepare(0, 0, part)
            heads(dve, body)
            dve.wait_ge(kept, past(HEADS))


def mix_out(nc, x, w_out, mix_w, ffn_w, C, Y, osq, xnT):
    with ExitStack() as ctx:
        def sb(name, shape, dt=F32):
            return ctx.enter_context(nc.sbuf_tensor("mo_" + name, shape, dt))

        primed = []

        def plain_sem(name):
            return ctx.enter_context(nc.semaphore("mo_" + name))

        def sem(name):
            primed.append(plain_sem(name))
            return primed[-1]

        def psum(name, shape):
            return ctx.enter_context(nc.psum_tensor("mo_" + name, shape, F32))

        w = sb("w", [P, MT, D])
        mw = sb("mw", [P, MT])
        fw = sb("fw", [P, D])
        ys = sb("ys", [P, MIX])
        yT = sb("yT", [P, MT, P])
        xr = sb("xr", [P, D])
        h = sb("h", [P, D])
        xn = sb("xn", [P, D])
        sq = sb("sq", [P, D])
        ss = sb("ss", [P, 2])
        rs = sb("rs", [P, 2])
        ps_y = psum("ps_y", [P, 4, P])
        ps_y2 = psum("ps_y2", [P, 4, P])
        ps_h = psum("ps_h", [P, 2, 512])
        ps_x = psum("ps_x", [P, KT, P])
        GRP = 4
        NG = MT // GRP

        w_in, s_in, x_in = [plain_sem(f"w_in{g}") for g in range(NG)], plain_sem("s_in"), plain_sem("x_in")
        y_squared, y_meaned, y_rooted, y_inverse = sem("y_squared"), sem("y_meaned"), sem("y_rooted"), sem("y_inverse")
        o_rooted, o_inverse = sem("o_rooted"), sem("o_inverse")
        ys_scaled, ys_copied = sem("ys_scaled"), sem("ys_copied")
        y_turned, yT_ready = sem("y_turned"), sem("yT_ready")
        product, h_ready, h_squared, h_meaned, h_rooted, h_inverse = (
            sem("product"), sem("h_ready"), sem("h_squared"), sem("h_meaned"), sem("h_rooted"), sem("h_inverse"))
        xn_ready, xn_turned, xnT_ready, kept = sem("xn_ready"), sem("xn_turned"), sem("xnT_ready"), sem("kept")
        act_turn, pool_turn = sem("act_turn"), sem("pool_turn")
        xd = x.rearrange("o (b p) d -> p (o b) d", p=P)
        block = ctx.enter_context(nc.Block())

        def in_steps(eng, step):
            step(0, True, False)
            with eng.Fori(1, NB - 1) as b:
                step(b, False, False)
            step(NB - 1, False, True)

        @block.sync
        def _(sp):
            prime(sp, primed)
            sp.dma_start(mw[:], mix_w).then_inc(s_in, 16)
            sp.dma_start(fw[:], ffn_w).then_inc(s_in, 16)
            for g in range(NG):
                ks = slice(g * GRP, (g + 1) * GRP)
                sp.dma_start(w[:, ks, :], w_out[:, ks, :]).then_inc(w_in[g], 16)
            with sp.Fori(0, NB) as b:
                sp.wait_ge(h_ready, past(b))
                sp.dma_start(xr[:], xd[:, bass.ds(b, 1), :].rearrange("p o d -> p (o d)")).then_inc(x_in, 16)

        @block.tensor
        def _(pe):
            def turn_y(b):
                for g in range(NG):
                    pe.wait_ge(ys_scaled if g < NG // 2 else ys_copied, past(b + 1))
                    if not (isinstance(b, int) and g < 2):
                        pe.wait_ge(yT_ready, past(b * MT + GRP * (g - 1)))
                    bank = (ps_y, ps_y2)[g % 2]
                    for j in range(GRP):
                        k = g * GRP + j
                        mm = nc.tensor.transpose(bank[:, j, :], ys[:, k * P:(k + 1) * P], C["ident"][:])
                    mm.then_inc(y_turned, 1)

            def turn_x(b):
                pe.wait_ge(xn_ready, past(b + 1))
                pe.wait_ge(xnT_ready, past(b))
                for k in range(KT):
                    mm = nc.tensor.transpose(ps_x[:, k, :], xn[:, k * P:(k + 1) * P], C["ident"][:])
                mm.then_inc(xn_turned, 1)

            def multiply(b):
                pe.wait_ge(h_ready, past(b))
                for k in range(MT):
                    if isinstance(b, int) and k % GRP == 0:
                        pe.wait_ge(w_in[k // GRP], 16)
                    pe.wait_ge(yT_ready, past(b * MT + k + 1))
                    for half in range(2):
                        mm = nc.tensor.matmul(ps_h[:, half, :], yT[:, k, :], w[:, k, half * 512:(half + 1) * 512],
                                              start=(k == 0), stop=(k == MT - 1))
                mm.then_inc(product, 1)

            turn_y(0)
            multiply(0)
            with pe.Fori(1, NB) as b:
                turn_y(b)
                turn_x(b - 1)
                multiply(b)
            turn_x(NB - 1)

        @block.scalar
        def _(act):
            act.wait_ge(s_in, 32)

            def root_y(b):
                if not isinstance(b, int):
                    act.wait_ge(h_squared, past(b - 1))
                act.sem_inc(act_turn, 1)
                nc.scalar.activation(sq[:], Y[:, bass.ds(b, 1), 0:D].rearrange("p o d -> p (o d)"), ACT.Square,
                                     accum_out=ss[:, 0:1]).then_inc(y_squared, 1)
                act.wait_ge(y_meaned, past(b + 1))
                nc.scalar.activation(rs[:, 0:1], ss[:, 0:1], ACT.Sqrt).then_inc(y_rooted, 1)

            def out_y(b):
                for k in range(MT):
                    if k % GRP == 0:
                        act.wait_ge(y_turned, past(b * NG + k // GRP + 1))
                        act.wait_ge(product, past(b))
                    nc.scalar.activation(yT[:, k, :], ((ps_y, ps_y2)[k // GRP % 2])[:, k % GRP, :], ACT.Copy,
                                         scale=mw[:, k:k + 1]).then_inc(yT_ready, 1)

            def turned_out(b):
                act.wait_ge(xn_turned, past(b + 1))
                act.sem_inc(act_turn, 1)
                nc.scalar.activation(xnT[:, :, bass.ds(b * P, P)], ps_x[:], ACT.Copy).then_inc(xnT_ready, 1)

            def step(b, first, last):
                out_y(b)
                if not first:
                    turned_out(b - 1)
                if not last:
                    root_y(b + 1)
                act.wait_ge(h_ready, past(b + 1))
                act.wait_ge(y_squared, past(b + 1 if last else b + 2))
                nc.scalar.activation(sq[:], h[:], ACT.Square, accum_out=ss[:, 1:2]).then_inc(h_squared, 1)
                act.wait_ge(h_meaned, past(b + 1))
                nc.scalar.activation(rs[:, 1:2], ss[:, 1:2], ACT.Sqrt).then_inc(h_rooted, 1)

            act.wait_ge(o_inverse, past(1))
            nc.scalar.activation(osq[:], osq[:], ACT.Sqrt).then_inc(o_rooted, 1)
            root_y(0)
            in_steps(act, step)
            turned_out(NB - 1)

        @block.gpsimd
        def _(pool):
            def copy_y(b):
                pool.wait_ge(y_turned, past(b * NG))
                pool.sem_inc(pool_turn, 1)
                nc.gpsimd.tensor_tensor(ys[:, D:MIX].rearrange("p (h d) -> p h d", h=HEADS),
                                        Y[:, bass.ds(b, 1), D:MIX].rearrange("p o (h d) -> p (o h) d", h=HEADS),
                                        osq[:, bass.ds(b, 1), :].rearrange("p o h -> p (o h)").unsqueeze(2)
                                        .to_broadcast([P, HEADS, P]), ALU.mult).then_inc(ys_copied, 1)

            def step(b, first, last):
                if not last:
                    copy_y(b + 1)
                pool.wait_ge(h_ready, past(b + 1))
                pool.sem_inc(pool_turn, 1)
                nc.gpsimd.tensor_copy(Y[:, bass.ds(b, 1), 0:D].rearrange("p o d -> p (o d)"), h[:])
                pool.wait_ge(xn_ready, past(b + 1))
                pool.wait_ge(ys_copied, past(b + 1))
                pool.sem_inc(pool_turn, 1)
                nc.gpsimd.tensor_copy(Y[:, bass.ds(b, 1), D:MIX].rearrange("p o d -> p (o d)"), xn[:]).then_inc(kept, 1)

            pool.wait_ge(o_inverse, past(2))
            copy_y(0)
            in_steps(pool, step)

        @block.vector
        def _(dve):
            def scale_y(b):
                dve.wait_ge(y_squared, past(b + 1))
                nc.vector.tensor_scalar(ss[:, 0:1], ss[:, 0:1], 1.0 / D, EPS, ALU.mult, ALU.add).then_inc(y_meaned, 1)
                dve.wait_ge(y_rooted, past(b + 1))
                nc.vector.reciprocal(rs[:, 0:1], rs[:, 0:1]).then_inc(y_inverse, 1)
                dve.wait_ge(y_turned, past(b * NG))
                dve.wait_ge(y_inverse, past(b + 1))
                nc.vector.tensor_scalar(ys[:, 0:D], Y[:, bass.ds(b, 1), 0:D].rearrange("p o d -> p (o d)"),
                                        rs[:, 0:1], None, ALU.mult).then_inc(ys_scaled, 1)

            def step(b, first, last):
                if not last:
                    scale_y(b + 1)
                dve.wait_ge(x_in, (b + 1) * 16)
                dve.wait_ge(kept, past(b))
                dve.wait_ge(product, past(b + 1))
                nc.vector.tensor_tensor(h[:], ps_h[:].rearrange("p a c -> p (a c)"), xr[:], ALU.add).then_inc(h_ready, 1)
                dve.wait_ge(h_squared, past(b + 1))
                nc.vector.tensor_scalar(ss[:, 1:2], ss[:, 1:2], 1.0 / D, EPS, ALU.mult, ALU.add).then_inc(h_meaned, 1)
                dve.wait_ge(h_rooted, past(b + 1))
                nc.vector.reciprocal(rs[:, 1:2], rs[:, 1:2]).then_inc(h_inverse, 1)
                dve.wait_ge(h_inverse, past(b + 1))
                dve.wait_ge(xn_turned, past(b))
                nc.vector.scalar_tensor_tensor(out=xn[:], in0=h[:], scalar=rs[:, 1:2], in1=fw[:],
                                               op0=ALU.mult, op1=ALU.mult).then_inc(xn_ready, 1)

            nc.vector.tensor_scalar(osq[:], osq[:], 1.0 / P, EPS, ALU.mult, ALU.add).then_inc(o_inverse, 1)
            dve.wait_ge(o_rooted, past(1))
            nc.vector.reciprocal(osq[:], osq[:]).then_inc(o_inverse, 1)
            scale_y(0)
            in_steps(dve, step)
            dve.wait_ge(kept, past(NB))


def peer(nc, w_query, keys, table, C, Y, xnT):
    with ExitStack() as ctx:
        def sb(name, shape, dt=F32):
            return ctx.enter_context(nc.sbuf_tensor("peer_" + name, shape, dt))

        primed = []

        def plain_sem(name):
            return ctx.enter_context(nc.semaphore("peer_" + name))

        def sem(name):
            primed.append(plain_sem(name))
            return primed[-1]

        def psum(name, shape):
            return ctx.enter_context(nc.psum_tensor("peer_" + name, shape, F32))

        ring = sb("ring", [P, RING, 2 * D])
        wq = sb("wq", [P, KT, 2 * P])
        kT = sb("kT", [P, PH * 2 * KEYS])
        qs = sb("qs", [P, 2, P])
        sc = sb("sc", [P, 2, KEYS])
        sc2 = sb("sc2", [P, 2, KEYS])
        top = sb("top", [P, 2, TOPK])
        ix = sb("ix", [P, 2, TOPK], U32)
        ixf = sb("ixf", [P, 2, TOPK])
        cand = sb("cand", [P, NCAND])
        cand2 = sb("cand2", [P, NCAND])
        expert = sb("expert", [P, NCAND])
        best = sb("best", [P, TOPK])
        place = sb("place", [P, TOPK], U32)
        placef = sb("placef", [P, TOPK])
        count_u = sb("count_u", [P, NCAND], U32)
        count = sb("count", [P, NCAND])
        hit = sb("hit", [P, TOPK, NCAND])
        chosen = sb("chosen", [P, TOPK])
        neg = sb("neg", [P, 1])
        gx = sb("gx", [P, TOPK])
        gsum = sb("gsum", [P, 1])
        index = sb("index", [P, NB, TOPK], U32)
        gate = sb("gate", [P, NB, TOPK])
        index_even = sb("index_even", [P, TOPK], U32)
        index_odd = sb("index_odd", [P, TOPK], U32)
        gate_now = sb("gate_now", [P, TOPK])
        junk = sb("junk", [P, D])
        dots = sb("dots", [P, TOPK])
        act_out = sb("act_out", [P, BATCH])
        hid = sb("hid", [P, BATCH])
        diag = sb("diag", [P, RING, P])

        ps_q = psum("ps_q", [P, 2, 256])
        ps_s = psum("ps_s", [P, 2, 256])
        ps_o = psum("ps_o", [P, 2, 512])

        wq_in, k_in = plain_sem("wq_in"), plain_sem("k_in")
        got = [plain_sem(f"got{s}") for s in range(RING)]
        counted = sem("counted")
        q_made, q_out, scores_made, scores_out, picked = (sem("q_made"), sem("q_out"), sem("scores_made"),
                                                          sem("scores_out"), sem("picked"))
        best_ready, gates_ready, routed = sem("best_ready"), sem("gates_ready"), sem("routed")
        index_taken, gate_taken = sem("index_taken"), sem("gate_taken")
        free_slots = plain_sem("free_slots")
        dot_ready, act_own, diag_ready, activated = sem("dot_ready"), sem("act_own"), sem("diag_ready"), sem("activated")
        summed, added = sem("summed"), sem("added")
        dve_own, dve_turn, act_turn, pool_turn = sem("dve_own"), sem("dve_turn"), sem("act_turn"), sem("pool_turn")
        block = ctx.enter_context(nc.Block())

        def loops(eng, route_pass, gather_pass):
            def same_head(h):
                with eng.Fori(0, NB - LAG) as b:
                    n = h * NB + b
                    gather_pass(n, b, lambda: route_pass(n + LAG, h, b + LAG, n))

            with eng.Fori(0, LAG) as b:
                route_pass(b, 0, b, None)
            with eng.Fori(0, PH - 1) as h:
                same_head(h)
                with eng.Fori(0, LAG) as b:
                    n = h * NB + (NB - LAG) + b
                    gather_pass(n, b + (NB - LAG), lambda: route_pass(n + LAG, h + 1, b, n))
            same_head(PH - 1)
            with eng.Fori(0, LAG) as b:
                gather_pass(b + (PH * NB - LAG), b + (NB - LAG), None)

        @block.sync
        def _(sp):
            prime(sp, primed)
            sp.dma_start(wq[:], w_query[0]).then_inc(wq_in, 16)
            sp.dma_start(kT[:], keys).then_inc(k_in, 16)
            with sp.Fori(1, PH) as h:
                sp.wait_ge(q_made, past(h * NB))
                sp.dma_start(wq[:], w_query[bass.ds(h, 1)].rearrange("o p k c -> p (o k) c")).then_inc(wq_in, 16)

        @block.gpsimd
        def _(pool):
            nc.gpsimd.iota(count_u[:], pattern=[[1, NCAND]], base=0, channel_multiplier=0).then_inc(counted, 1)
            pool.sem_inc(free_slots, RING)

            def gather(n, b, index_now):
                pool.wait_ge(routed, past(n + 1))
                pool.sem_inc(pool_turn, 1)
                nc.gpsimd.tensor_copy(index_now[:], index[:, bass.ds(b, 1), :].rearrange("p o k -> p (o k)")
                                      ).then_inc(index_taken, 1)
                pool.wait_ge(index_taken, past(n + 1))
                for k in range(TOPK):
                    pool.wait_ge(free_slots, n * TOPK + k + 1)
                    pool.sem_inc(pool_turn, 1)
                    pool.indirect_dma_start(ring[:, k % RING, :], None, table,
                                            bass.IndirectOffsetOnAxis(ap=index_now[:, k:k + 1], axis=0)
                                            ).then_inc(got[k % RING], 16)

            with pool.Fori(0, PH) as h:
                with pool.Fori(0, NB // 2) as pair:
                    gather(h * NB + pair * 2, pair * 2, index_even)
                    gather(h * NB + pair * 2 + 1, pair * 2 + 1, index_odd)

        @block.tensor
        def _(pe):
            def query(n, h, b):
                pe.wait_ge(wq_in, (h + 1) * 16)
                pe.wait_ge(q_out, past(n))
                for p in range(2):
                    for k in range(KT):
                        mm = nc.tensor.matmul(ps_q[:, p, 0:P], wq[:, k, p * P:(p + 1) * P],
                                              xnT[:, k, bass.ds(b * P, P)], start=(k == 0), stop=(k == KT - 1))
                mm.then_inc(q_made, 1)

            def score(n, h):
                pe.wait_ge(q_out, past(n + 1))
                pe.wait_ge(scores_out, past(n))
                for p in range(2):
                    mm = nc.tensor.matmul(ps_s[:, p, 0:P], qs[:, p, :], kT[:, bass.ds((h * 2 + p) * KEYS, KEYS)],
                                          start=True, stop=True)
                mm.then_inc(scores_made, 1)

            def route(n, h, b, last):
                query(n, h, b)
                score(n, h)

            def gather(n, b, route_next):
                if route_next:
                    route_next()
                pe.wait_ge(added, past(n))
                for k in range(TOPK):
                    pe.wait_ge(diag_ready, past(n * TOPK + k + 1))
                    for half in range(2):
                        mm = nc.tensor.matmul(ps_o[:, half, :], diag[:, k % RING, :],
                                              ring[:, k % RING, D + half * 512:D + (half + 1) * 512],
                                              start=(k == 0), stop=(k == TOPK - 1))
                    mm.then_inc(free_slots, 1)

            pe.wait_ge(k_in, 16)
            loops(pe, route, gather)

        @block.scalar
        def _(act):
            def scores(n):
                act.wait_ge(q_made, past(n + 1))
                act.wait_ge(scores_made, past(n))
                nc.scalar.activation(qs[:], ps_q[:, :, 0:P], ACT.Copy).then_inc(q_out, 1)
                act.wait_ge(scores_made, past(n + 1))
                act.wait_ge(picked, past(n))
                nc.scalar.activation(sc[:], ps_s[:, :, 0:KEYS], ACT.Copy).then_inc(scores_out, 1)

            def gates(n):
                act.wait_ge(best_ready, past(n + 1))
                nc.scalar.activation(gx[:], best[:], ACT.Exp, bias=neg[:], accum_out=gsum[:]).then_inc(gates_ready, 1)

            def route(n, h, b, last):
                scores(n)
                gates(n)

            def gather(n, b, route_next):
                if route_next:
                    scores(n + LAG)
                own = Own(act, act_own, TOPK)
                own.at(n)
                act.wait_ge(routed, past(n + 1))
                act.sem_inc(act_turn, 1)
                nc.scalar.activation(gate_now[:], gate[:, bass.ds(b, 1), :].rearrange("p o k -> p (o k)"),
                                     ACT.Copy).then_inc(gate_taken, 1)
                act.wait_ge(gate_taken, past(n + 1))
                for q in range(TOPK // BATCH):
                    act.wait_ge(dot_ready, past(n * TOPK + (q + 1) * BATCH))
                    nc.scalar.activation(act_out[:], dots[:, q * BATCH:(q + 1) * BATCH], ACT.Gelu).then_inc(activated, 1)
                    act.wait_ge(activated, past(n * (TOPK // BATCH) + q + 1))
                    for j in range(BATCH):
                        k = q * BATCH + j
                        own.step(nc.scalar.activation(hid[:, j:j + 1], act_out[:, j:j + 1], ACT.Copy,
                                                      scale=gate_now[:, k:k + 1]))
                    own.wait()
                    for j in range(BATCH):
                        k = q * BATCH + j
                        act.wait_ge(free_slots, n * TOPK + k + 1)
                        ins = nc.scalar.activation(diag[:, k % RING, :], C["ident"][:], ACT.Copy, scale=hid[:, j:j + 1])
                        ins.then_inc(diag_ready, 1)
                own.check()
                if route_next:
                    gates(n + LAG)

            loops(act, route, gather)

        @block.vector
        def _(dve):
            dve.wait_ge(counted, past(1))
            nc.vector.tensor_copy(count[:], count_u[:]).then_inc(counted, 1)
            dve.wait_ge(counted, past(2))

            def route(n, h, b, last):
                own = Own(dve, dve_own, 19)
                own.at(n)

                def hold():
                    own.wait()
                    dve.sem_inc(dve_turn, 1)

                dve.wait_ge(scores_out, past(n + 1))
                dve.sem_inc(dve_turn, 1)
                for p in range(2):
                    own.step(nc.vector.max(top[:, p, 0:8], sc[:, p, :]))
                hold()
                for p in range(2):
                    nc.vector.max_index(ix[:, p, 0:8], top[:, p, 0:8], sc[:, p, :])
                    own.step(nc.vector.match_replace(sc2[:, p, :], top[:, p, 0:8], sc[:, p, :], LOW))
                hold()
                dve.sem_inc(picked, 1)
                for p in range(2):
                    own.step(nc.vector.max(top[:, p, 8:16], sc2[:, p, :]))
                hold()
                for p in range(2):
                    ins = nc.vector.max_index(ix[:, p, 8:16], top[:, p, 8:16], sc2[:, p, :])
                own.done(ins)
                own.done(nc.vector.tensor_copy(ixf[:], ix[:]))
                own.done(nc.vector.tensor_scalar(ixf[:, 0, :], ixf[:, 0, :], float(KEYS), None, ALU.mult))
                at = 0
                for i in range(TOPK // 2):
                    m = ROWS_OF[i]
                    nc.vector.tensor_scalar(cand[:, at:at + m], top[:, 1, 0:m], top[:, 0, i:i + 1], None, ALU.add)
                    nc.vector.tensor_scalar(expert[:, at:at + m], ixf[:, 1, 0:m], ixf[:, 0, i:i + 1], None, ALU.add)
                    at += m
                nc.vector.tensor_scalar(expert[:, at:], ixf[:, 0, 8:16], ixf[:, 1, 0:1], None, ALU.add)
                own.step(nc.vector.tensor_scalar(cand[:, at:], top[:, 0, 8:16], top[:, 1, 0:1], None, ALU.add))
                hold()
                own.step(nc.vector.max(best[:, 0:8], cand[:]))
                hold()
                nc.vector.max_index(place[:, 0:8], best[:, 0:8], cand[:])
                own.step(nc.vector.match_replace(cand2[:], best[:, 0:8], cand[:], LOW))
                hold()
                own.step(nc.vector.max(best[:, 8:16], cand2[:]))
                nc.vector.tensor_scalar(neg[:], best[:, 0:1], -1.0, None, ALU.mult).then_inc(best_ready, 1)
                hold()
                own.done(nc.vector.max_index(place[:, 8:16], best[:, 8:16], cand2[:]))
                own.done(nc.vector.tensor_copy(placef[:], place[:]))
                own.done(nc.vector.tensor_tensor(hit[:], count[:].unsqueeze(1).to_broadcast([P, TOPK, NCAND]),
                                                 placef[:].unsqueeze(2).to_broadcast([P, TOPK, NCAND]), ALU.is_equal))
                own.done(nc.vector.tensor_tensor(hit[:], hit[:], expert[:].unsqueeze(1).to_broadcast([P, TOPK, NCAND]),
                                                 ALU.mult))
                own.step(nc.vector.tensor_reduce(chosen[:], hit[:], AX.X, ALU.add))
                if last is not None:
                    dve.wait_ge(index_taken, past(last + 1))
                    dve.wait_ge(gate_taken, past(last + 1))
                hold()
                nc.vector.tensor_copy(index[:, bass.ds(b, 1), :].rearrange("p o k -> p (o k)"), chosen[:])
                dve.wait_ge(gates_ready, past(n + 1))
                own.done(nc.vector.reciprocal(gsum[:], gsum[:]))
                nc.vector.tensor_scalar(gate[:, bass.ds(b, 1), :].rearrange("p o k -> p (o k)"), gx[:], gsum[:], None,
                                        ALU.mult).then_inc(routed, 1)
                own.check()

            def gather(n, b, route_next):
                for k in range(TOPK):
                    s = k % RING
                    dve.wait_ge(got[s], (n * 2 + k // RING + 1) * 16)
                    dve.wait_ge(dot_ready, past(n * TOPK + k))
                    if k % BATCH == 0:
                        dve.wait_ge(diag_ready, past(n * TOPK))
                    nc.vector.scalar_tensor_tensor(
                        out=junk[:], in0=ring[:, s, 0:D], scalar=1.0,
                        in1=Y[:, bass.ds(b, 1), D:MIX].rearrange("p o d -> p (o d)"),
                        op0=ALU.mult, op1=ALU.mult, accum_out=dots[:, k:k + 1]).then_inc(dot_ready, 1)
                if route_next:
                    route_next()
                dve.wait_ge(free_slots, RING + (n + 1) * TOPK)
                hb = Y[:, bass.ds(b, 1), 0:D].rearrange("p o d -> p (o d)")
                nc.vector.tensor_tensor(hb, hb, ps_o[:].rearrange("p a c -> p (a c)"), ALU.add).then_inc(added, 1)

            loops(dve, route, gather)
            dve.wait_ge(added, past(PH * NB))


def final_norm(nc, fin_w, Y, out):
    with ExitStack() as ctx:
        def sb(name, shape, dt=F32):
            return ctx.enter_context(nc.sbuf_tensor("fin_" + name, shape, dt))

        primed = []

        def plain_sem(name):
            return ctx.enter_context(nc.semaphore("fin_" + name))

        def sem(name):
            primed.append(plain_sem(name))
            return primed[-1]

        fw = sb("fw", [P, D])
        sq = sb("sq", [P, D])
        ss = sb("ss", [P, NB])
        rs = sb("rs", [P, NB])
        w_in, squared, meaned, rooted, inverse, normed, written = (
            plain_sem("w_in"), sem("squared"), sem("meaned"), sem("rooted"), sem("inverse"), sem("normed"), plain_sem("written"))
        od = out.rearrange("o (b p) d -> p (o b) d", p=P)
        block = ctx.enter_context(nc.Block())

        @block.scalar
        def _(act):
            for b in range(NB):
                if b >= 1:
                    act.wait_ge(squared, past(b))
                nc.scalar.activation(sq[:], Y[:, b, 0:D], ACT.Square, accum_out=ss[:, b:b + 1]).then_inc(squared, 1)
            act.wait_ge(meaned, past(1))
            nc.scalar.activation(rs[:], ss[:], ACT.Sqrt).then_inc(rooted, 1)

        @block.vector
        def _(dve):
            dve.wait_ge(squared, past(NB))
            nc.vector.tensor_scalar(ss[:], ss[:], 1.0 / D, EPS, ALU.mult, ALU.add).then_inc(meaned, 1)
            dve.wait_ge(rooted, past(1))
            nc.vector.reciprocal(rs[:], rs[:]).then_inc(inverse, 1)
            dve.wait_ge(inverse, past(1))
            dve.wait_ge(w_in, 16)
            for b in range(NB):
                nc.vector.scalar_tensor_tensor(out=Y[:, b, D:MIX], in0=Y[:, b, 0:D], scalar=rs[:, b:b + 1], in1=fw[:],
                                               op0=ALU.mult, op1=ALU.mult).then_inc(normed, 1)

        @block.sync
        def _(sp):
            prime(sp, primed)
            sp.dma_start(fw[:], fin_w).then_inc(w_in, 16)
            for b in range(NB):
                sp.wait_ge(normed, past(b + 1))
                sp.dma_start(od[:, b, :], Y[:, b, D:MIX]).then_inc(written, 16)
            sp.wait_ge(written, 16 * NB)


def block_program(nc, x, ln_w, w_ssd, par, w_hg, lb_logits, w_out, mix_w, ffn_w, w_query, keys, table, fin_w, out):
    with ExitStack() as ctx:
        C = {n: ctx.enter_context(nc.sbuf_tensor(n, [P, P], F32)) for n in ("ident", "ones", "tri", "below")}
        hnT = ctx.enter_context(nc.sbuf_tensor("hnT", [P, KT, SEQ], F32))
        Y = ctx.enter_context(nc.sbuf_tensor("Y", [P, NB, MIX], F32))
        osq = ctx.enter_context(nc.sbuf_tensor("osq", [P, NB, HEADS], F32))
        with nc.sbuf_tensor("reset", [P, SEQ], F32) as reset, nc.sbuf_tensor("lmask", [P, LEVELS + 1, P], F32) as lmask:
            C["reset"], C["lmask"] = reset, lmask
            with nc.sbuf_tensor("w_group", [P, KT, SSD_COLS], F32) as w_group, ExitStack() as sems:
                group_in = [sems.enter_context(nc.semaphore(f"group_in{i}")) for i in range(len(SSD_PARTS))]
                input_norm(nc, x, ln_w, w_ssd, C, hnT, w_group, group_in)
                ssd(nc, w_group, group_in, w_ssd, par, w_hg, C, hnT, Y)
            hgrn(nc, w_hg, lb_logits, C, hnT, Y, osq)
        mix_out(nc, x, w_out, mix_w, ffn_w, C, Y, osq, hnT)
        peer(nc, w_query, keys, table, C, Y, hnT)
        final_norm(nc, fin_w, Y, out)


def laid_out(inputs):
    import numpy as np

    def first(name):
        return np.asarray(inputs[name])[0]

    inner, bc = GROUPS * XW, GROUPS * P
    w = first("w_in").reshape(KT, P, -1).transpose(1, 0, 2)
    at_x, at_dt = inner, 2 * inner + 2 * bc
    at_q = at_dt + GROUPS * HPG
    conv = np.concatenate([first("conv_w"), first("conv_b")[None]], 0)
    w_ssd, par = [], []
    for g in range(GROUPS):
        ch = np.concatenate([np.arange(g * XW, (g + 1) * XW), inner + g * P + np.arange(P),
                             inner + bc + g * P + np.arange(P)])
        w_ssd.append(np.concatenate([w[:, :, at_x + ch], w[:, :, g * XW:(g + 1) * XW],
                                     w[:, :, at_dt + g * HPG:at_dt + (g + 1) * HPG]], 2))
        taps = conv[:, ch].reshape(TAPS + 1, CT, P).transpose(2, 1, 0).reshape(P, CT * (TAPS + 1))
        heads = [np.broadcast_to(first(n)[g * HPG:(g + 1) * HPG], (P, HPG)) for n in ("dt_bias", "a_log", "d_skip")]
        par.append(np.concatenate([taps, *heads], 1))
    w_hg = [np.concatenate([w[:, :, at_q + j * D + h * P:at_q + j * D + (h + 1) * P] for j in range(4)], 2)
            for h in range(HEADS)]
    return {
        "x": np.asarray(inputs["x"]),
        "ln_w": first("ln_mix_w").reshape(KT, P).T,
        "w_ssd": np.stack(w_ssd),
        "par": np.stack(par, 1),
        "w_hg": np.stack(w_hg),
        "lb_logits": np.asarray(inputs["lb_logits"]).reshape(2, HEADS, P).transpose(2, 0, 1),
        "w_out": first("w_out").reshape(MT, P, D).transpose(1, 0, 2),
        "mix_w": np.concatenate([first("ssd_norm_w"), first("hg_norm_w")]).reshape(MT, P).T,
        "ffn_w": np.broadcast_to(first("ln_ffn_w"), (P, D)),
        "w_query": first("w_query").reshape(KT, P, PH, 2 * P).transpose(2, 1, 0, 3),
        "keys": first("sub_keys").transpose(3, 0, 1, 2).reshape(P, PH * 2 * KEYS),
        "table": np.concatenate([first("u_table"), first("v_table")], 1),
        "fin_w": np.broadcast_to(np.asarray(inputs["ln_final_w"]), (P, D)),
    }


def kernel(**inputs):
    import numpy as np
    import concourse.bacc as bacc
    from concourse.bass_utils import run_bass_kernel_spmd

    nc = bacc.Bacc("TRN2", target_bir_lowering=False, num_devices=1)
    arrays = {n: np.ascontiguousarray(a) for n, a in laid_out(inputs).items()}
    args = {n: nc.dram_tensor("in_" + n, a.shape, mybir.dt.from_np(a.dtype), kind="ExternalInput").ap()
            for n, a in arrays.items()}
    out = nc.dram_tensor("out_0", [1, SEQ, D], F32, kind="ExternalOutput").ap()
    block_program(nc, out=out, **args)
    r = run_bass_kernel_spmd(nc, [{"in_" + n: a for n, a in arrays.items()}], core_ids=[0])
    return r.results[0]["out_0"]
```

```python
from contextlib import ExitStack

import concourse.bass as bass
from concourse import mybir

ALU = mybir.AluOpType
ACT = mybir.ActivationFunctionType
AX = mybir.AxisListType
F32 = mybir.dt.float32
U32 = mybir.dt.uint32

P = 128
SEQ, D = 1024, 1024
NB = SEQ // P
KT = D // P
EPS = 1e-6
HALF, HC = SEQ // 2, NB // 2

GROUPS, HPG, HD = 4, 4, 64
XW = HPG * HD
CT = 4
TAPS = 4
SSD_COLS = CT * P + XW + HPG
SSD_PARTS = [slice(i * P, (i + 1) * P) for i in range(CT)] + [slice(CT * P, SSD_COLS)]
SSD_PIECES = 2 * CT
NPAR = CT * (TAPS + 1) + 3 * HPG
DTB, ALG, DSK = CT * (TAPS + 1), CT * (TAPS + 1) + HPG, CT * (TAPS + 1) + 2 * HPG

HEADS = 8
HG_COLS = 4 * P
HG_PARTS = [slice(0, P), slice(P, 2 * P), slice(2 * P, HG_COLS)]
HG_PIECES = 2 + NB // 2
HEAD_PARTS = [[0], [1], [2, 3], [4, 5]]
LEVELS = 7
MIX = 2 * D
MT = MIX // P

PH, TOPK, KEYS = 8, 16, 128
EXPERTS = KEYS * KEYS
ROWS_OF = [TOPK // (i + 1) for i in range(TOPK)]
NCAND = sum(ROWS_OF)
RING = 8
LAG = 2
BATCH = 2
LOW = -3.0e38


def cols(c):
    return slice(c * P, (c + 1) * P)


class Own:

    def __init__(self, eng, sem, per=0):
        self.eng, self.sem, self.per, self.base, self.n = eng, sem, per, 0, 0

    def at(self, i):
        self.base, self.n = i * self.per, 0

    def done(self, ins):
        self.step(ins)
        self.wait()

    def step(self, ins):
        ins.then_inc(self.sem, 1)
        self.n += 1

    def skip(self):
        self.eng.sem_inc(self.sem, 1)
        self.n += 1

    def wait(self):
        self.eng.wait_ge(self.sem, past(self.base + self.n))

    def check(self):
        assert self.n == self.per, (self.n, self.per)


def past(count):
    return count + 1


def prime(eng, sems):
    for s in sems:
        eng.sem_inc(s, 1)


def constants(nc, pool, C, filled, cut, ident_ready):
    nc.gpsimd.memset(C["ident"][:], 0.0).then_inc(filled, 1)
    pool.wait_ge(filled, 1)
    nc.gpsimd.affine_select(out=C["ident"][:], in_=C["ident"][:], compare_op=ALU.not_equal, fill=1.0,
                            base=0, pattern=[[-1, P]], channel_multiplier=1).then_inc(ident_ready, 1)
    nc.gpsimd.memset(C["ones"][:], 1.0)
    nc.gpsimd.memset(C["tri"][:], 1.0)
    nc.gpsimd.memset(C["below"][:], 0.0)
    nc.gpsimd.memset(C["reset"][:], 1.0)
    nc.gpsimd.memset(C["lmask"][:], 1.0).then_inc(filled, 1)
    pool.wait_ge(filled, 2)
    nc.gpsimd.affine_select(out=C["tri"][:], in_=C["tri"][:], compare_op=ALU.is_ge, fill=0.0,
                            base=0, pattern=[[1, P]], channel_multiplier=-1)
    nc.gpsimd.affine_select(out=C["below"][:], in_=C["below"][:], compare_op=ALU.is_ge, fill=1.0e30,
                            base=0, pattern=[[1, P]], channel_multiplier=-1)
    nc.gpsimd.affine_select(out=C["reset"][:].rearrange("p (c l) -> p c l", l=P),
                            in_=C["reset"][:].rearrange("p (c l) -> p c l", l=P),
                            compare_op=ALU.is_gt, fill=0.0,
                            base=0, pattern=[[0, NB], [1, P]], channel_multiplier=0)
    n = 0
    for j in range(LEVELS):
        h = P >> (j + 1)
        m = C["lmask"][:, j, :].rearrange("p (q two r) -> p q two r", two=2, r=h)
        nq = P // (2 * h)
        nc.gpsimd.memset(m[:, :, 0, :], 0.0)
        right = m[:, :, 1, :]
        nc.gpsimd.affine_select(out=right, in_=right, compare_op=ALU.is_ge, fill=0.0, base=0,
                                pattern=[[-2 * h, nq], [0, h]], channel_multiplier=1).then_inc(cut, 1)
        n += 1
        pool.wait_ge(cut, n)
        nc.gpsimd.affine_select(out=right, in_=right, compare_op=ALU.is_gt, fill=0.0, base=h,
                                pattern=[[2 * h, nq], [0, h]], channel_multiplier=-1)
    nc.gpsimd.affine_select(out=C["lmask"][:, LEVELS, :], in_=C["lmask"][:, LEVELS, :],
                            compare_op=ALU.is_equal, fill=0.0,
                            base=0, pattern=[[-1, P]], channel_multiplier=1).then_inc(cut, 1)
    pool.wait_ge(cut, n + 1)


def input_norm(nc, x, ln_w, w_ssd, C, hnT, w_group, group_in):
    with ExitStack() as ctx:
        def sb(name, shape, dt=F32):
            return ctx.enter_context(nc.sbuf_tensor("nrm_" + name, shape, dt))

        primed = []

        def plain_sem(name):
            return ctx.enter_context(nc.semaphore("nrm_" + name))

        def sem(name):
            primed.append(plain_sem(name))
            return primed[-1]

        xs = sb("xs", [P, NB, D])
        sq = sb("sq", [P, D])
        ss = sb("ss", [P, NB])
        rs = sb("rs", [P, NB])
        lnw = sb("lnw", [P, KT])
        BANKS = 4
        ps = ctx.enter_context(nc.psum_tensor("nrm_ps", [P, BANKS, 512], F32))
        x_in = [plain_sem(f"x_in{b}") for b in range(NB)]
        w_in = plain_sem("w_in")
        squared, rooted, meaned, inverse, scaled, turned, stored = (
            sem("squared"), sem("rooted"), sem("meaned"), sem("inverse"), sem("scaled"), sem("turned"),
            sem("stored"))
        filled, cut, ident_ready = plain_sem("filled"), plain_sem("cut"), plain_sem("ident_ready")
        xd = x.rearrange("o (b p) d -> p (o b) d", p=P)
        block = ctx.enter_context(nc.Block())

        @block.sync
        def _(sp):
            for b in range(NB):
                sp.dma_start(xs[:, b, :], xd[:, b, :]).then_inc(x_in[b], 16)
                if b == 0:
                    prime(sp, primed)
                    sp.dma_start(lnw[:], ln_w).then_inc(w_in, 16)
            for i, part in enumerate(SSD_PARTS):
                sp.dma_start(w_group[:, :, part], w_ssd[0, :, :, part]).then_inc(group_in[i], 16)

        @block.gpsimd
        def _(pool):
            constants(nc, pool, C, filled, cut, ident_ready)

        @block.scalar
        def _(act):
            for half in range(2):
                for b in range(HC * half, HC * (half + 1)):
                    act.wait_ge(x_in[b], 16)
                    if b >= 1:
                        act.wait_ge(squared, past(b))
                    nc.scalar.activation(sq[:], xs[:, b, :], ACT.Square, accum_out=ss[:, b:b + 1]).then_inc(squared, 1)
                hb = slice(HC * half, HC * (half + 1))
                act.wait_ge(meaned, past(half + 1))
                nc.scalar.activation(rs[:, hb], ss[:, hb], ACT.Sqrt).then_inc(rooted, 1)
            act.wait_ge(w_in, 16)
            for n in range(2 * KT):
                act.wait_ge(turned, past(n + 1))
                half, k = n // KT, n % KT
                nc.scalar.activation(hnT[:, k, half * 512:half * 512 + 512], ps[:, n % BANKS, :], ACT.Copy,
                                     scale=lnw[:, k:k + 1]).then_inc(stored, 1)

        @block.vector
        def _(dve):
            for half in range(2):
                hb = slice(HC * half, HC * (half + 1))
                dve.wait_ge(squared, past(HC * (half + 1)))
                nc.vector.tensor_scalar(ss[:, hb], ss[:, hb], 1.0 / D, EPS, ALU.mult, ALU.add).then_inc(meaned, 1)
                dve.wait_ge(rooted, past(half + 1))
                nc.vector.reciprocal(rs[:, hb], rs[:, hb]).then_inc(inverse, 1)
                dve.wait_ge(inverse, past(half + 1))
                for b in range(HC * half, HC * (half + 1)):
                    nc.vector.tensor_scalar(xs[:, b, :], xs[:, b, :], rs[:, b:b + 1], None, ALU.mult).then_inc(scaled, 1)

        @block.tensor
        def _(pe):
            pe.wait_ge(ident_ready, 1)
            for n in range(2 * KT):
                half, k = n // KT, n % KT
                pe.wait_ge(scaled, past(HC * (half + 1)))
                if n >= BANKS:
                    pe.wait_ge(stored, past(n - BANKS + 1))
                for j in range(HC):
                    mm = nc.tensor.transpose(ps[:, n % BANKS, j * P:(j + 1) * P],
                                             xs[:, HC * half + j, k * P:(k + 1) * P], C["ident"][:])
                mm.then_inc(turned, 1)


def first_weights(Y, kt):
    return Y[:, kt // 2, D + kt % 2 * HG_COLS:D + (kt % 2 + 1) * HG_COLS]


def first_piece(Y, half, p):
    if p < 2:
        return Y[:, KT // 2 + p, D + half * HALF:D + (half + 1) * HALF]
    return Y[:, KT // 2 + 2 + half, D + (p - 2) * 2 * P:D + (p - 1) * 2 * P]


def ssd(nc, w, w_in, w_ssd, par, w_hg, C, hnT, Y):
    with ExitStack() as ctx:
        def sb(name, shape, dt=F32):
            return ctx.enter_context(nc.sbuf_tensor("ssd_" + name, shape, dt))

        primed = []

        def plain_sem(name):
            return ctx.enter_context(nc.semaphore("ssd_" + name))

        def sem(name):
            primed.append(plain_sem(name))
            return primed[-1]

        def psum(name, shape):
            return ctx.enter_context(nc.psum_tensor("ssd_" + name, shape, F32))

        PAD = TAPS - 1
        pr = sb("pr", [P, GROUPS, NPAR])
        ah = sb("ah", [P, GROUPS, HPG])
        raw = sb("raw", [P, 2, CT, PAD + HALF])
        rawz = sb("rawz", [P, NB, XW + HPG])
        xc = sb("xc", [P, CT, SEQ])
        zs = sb("zs", [P, NB, XW])
        step5 = sb("step5", [P, 5, HC, HPG])
        dt = sb("dt", [P, NB, HPG])
        a = sb("a", [P, NB, HPG])
        acum = sb("acum", [P, NB, HPG])
        aend = sb("aend", [P, NB, HPG])
        from_start = sb("from_start", [P, NB, HPG])
        to_end = sb("to_end", [P, NB, HPG])
        decay_all = sb("decay_all", [P, NB, HPG])
        awide = sb("awide", [P, HPG, P])
        natural = sb("natural", [P, 3 * P])
        dec = sb("dec", [P, HPG, P])
        att = sb("att", [P, HPG, P])
        xdt = sb("xdt", [P, HPG, HD])
        xdte = sb("xdte", [P, HPG, HD])
        y = sb("y", [P, HPG, HD])
        skip = sb("skip", [P, HPG, HD])
        state = sb("state", [P, HPG, HD])

        ps_piece = psum("ps_piece", [P, 2, 512])
        ps_cb = psum("ps_cb", [P, 512])
        ps_turn = psum("ps_turn", [P, 512])
        ps_rows = psum("ps_rows", [P, HPG, P])
        ps_y = psum("ps_y", [P, 2, HPG, HD])
        ps_state = psum("ps_state", [P, 512])
        ps_sum = psum("ps_sum", [P, 512])

        par_in, head_in = plain_sem("par_in"), plain_sem("head_in")
        padded, a_logged = sem("padded"), sem("a_logged")
        piece_made, piece_out = sem("piece_made"), sem("piece_out")
        raw_used = sem("raw_used")
        convolved, activated, z_activated = sem("convolved"), sem("activated"), sem("z_activated")
        dt_raw, dt_exp, dt_onep, dt_log, dt_ready = (sem("dt_raw"), sem("dt_exp"), sem("dt_onep"),
                                                     sem("dt_log"), sem("dt_ready"))
        summed, sums_out, exps_ready = sem("summed"), sem("sums_out"), sem("exps_ready")
        wide_ready = sem("wide_ready")
        stage_a, natural_out = sem("stage_a"), sem("natural_out")
        diff_ready, dec_ready, att_ready = sem("diff_ready"), sem("dec_ready"), sem("att_ready")
        stage_b, chunk_done, state_ready = sem("stage_b"), sem("chunk_done"), sem("state_ready")
        own_prep, own_mix = sem("own_prep"), sem("own_mix")
        block = ctx.enter_context(nc.Block())

        def groups(eng, body):
            with eng.Fori(0, GROUPS - 1) as u:
                body(u, False)
            body(GROUPS - 1, True)

        @block.sync
        def _(sp):
            prime(sp, primed)
            sp.dma_start(pr[:], par).then_inc(par_in, 16)
            for kt in range(KT):
                sp.dma_start(first_weights(Y, kt), w_hg[0, :, kt, :]).then_inc(head_in, 16)
            with sp.Fori(1, GROUPS) as u:
                for i, part in enumerate(SSD_PARTS):
                    sp.wait_ge(piece_made, past(u * 2 * SSD_PIECES - (SSD_PIECES - 2 * i - 1 if i < CT else 0)))
                    sp.dma_start(w[:, :, part], w_ssd[bass.ds(u, 1), :, :, part].rearrange("o p k c -> p (o k) c")
                                 ).then_inc(w_in[i], 16)

        @block.gpsimd
        def _(pool):
            nc.gpsimd.memset(raw[:, 0, :, 0:PAD], 0.0).then_inc(padded, 1)
            with pool.Fori(0, GROUPS) as u:
                for c in range(NB):
                    if c % HC == 0:
                        pool.wait_ge(dt_ready, past(u * 2 + c // HC + 1))
                    pool.wait_ge(stage_a, past(u * NB + c))
                    nc.gpsimd.tensor_tensor(awide[:], a[:, c, :].unsqueeze(2).to_broadcast([P, HPG, P]),
                                            C["ones"][:].unsqueeze(1).to_broadcast([P, HPG, P]),
                                            ALU.mult).then_inc(wide_ready, 1)

        @block.tensor
        def _(pe):
            def piece(u, half, p):
                if half == 0 and (p % 2 == 0 or p == 1):
                    pe.wait_ge(w_in[p // 2 if p % 2 == 0 else CT], (u + 1) * 16)
                n = (u * 2 + half) * SSD_PIECES + p
                if not (isinstance(n, int) and n < 2):
                    pe.wait_ge(piece_out, past(n - 1))
                bank = ps_piece[:, p % 2, :]
                for k in range(KT):
                    if p % 2 == 0:
                        i = p // 2
                        mm = nc.tensor.matmul(bank, w[:, k, i * P:(i + 1) * P],
                                              hnT[:, k, half * HALF:(half + 1) * HALF],
                                              start=(k == 0), stop=(k == KT - 1))
                    else:
                        mm = nc.tensor.matmul(bank[:, 0:XW + HPG], hnT[:, k, cols(half * HC + p // 2)],
                                              w[:, k, CT * P:SSD_COLS], start=(k == 0), stop=(k == KT - 1))
                mm.then_inc(piece_made, 1)

            def head_piece(half, p):
                pe.wait_ge(head_in, 16 * KT)
                pe.wait_ge(piece_out, past(GROUPS * 2 * SSD_PIECES + half * HG_PIECES + p - 1))
                bank = ps_piece[:, p % 2, :]
                for kt in range(KT):
                    wk = first_weights(Y, kt)
                    if p < 2:
                        mm = nc.tensor.matmul(bank, wk[:, p * P:(p + 1) * P], hnT[:, kt, half * HALF:(half + 1) * HALF],
                                              start=(kt == 0), stop=(kt == KT - 1))
                    else:
                        mm = nc.tensor.matmul(bank[:, 0:2 * P], hnT[:, kt, cols(half * HC + p - 2)],
                                              wk[:, 2 * P:4 * P], start=(kt == 0), stop=(kt == KT - 1))
                mm.then_inc(piece_made, 1)

            def sums(n, half):
                pe.wait_ge(dt_ready, past(n + 1))
                pe.wait_ge(sums_out, past(n))
                av = a[:, half * HC:(half + 1) * HC, :].rearrange("p c r -> p (c r)")
                m = HC * HPG
                nc.tensor.matmul(ps_sum[:, 0:m], C["tri"][:], av, start=True, stop=True)
                nc.tensor.matmul(ps_sum[:, m:2 * m], C["ones"][:], av, start=True, stop=True).then_inc(summed, 1)

            def body(u, last):
                for c in range(NB):
                    half = c // HC
                    if c % HC == 0:
                        pe.wait_ge(activated, past((u * 2 + half + 1) * CT))
                    pe.wait_ge(wide_ready, past(u * NB + c + 1))
                    pe.wait_ge(att_ready, past(u * NB + c))
                    nc.tensor.matmul(ps_cb[:, 0:P], xc[:, 2, cols(c)], xc[:, 3, cols(c)], start=True, stop=True)
                    for i in range(3):
                        nc.tensor.transpose(ps_turn[:, i * P:(i + 1) * P], xc[:, i, cols(c)], C["ident"][:])
                    for r in range(HPG):
                        mm = nc.tensor.matmul(ps_rows[:, r, :], awide[:, r, :], C["tri"][:], start=True, stop=True)
                    mm.then_inc(stage_a, 1)
                    if not last:
                        piece(u + 1, half, 2 * (c % HC))
                        piece(u + 1, half, 2 * (c % HC) + 1)
                    else:
                        for p in HEAD_PARTS[c % HC]:
                            head_piece(half, p)
                    if c % HC == HC - 2 and not (last and half == 1):
                        sums(u * 2 + half + 1, 1 - half)
                    pe.wait_ge(state_ready, past(u * NB + c + 1))
                    pe.wait_ge(chunk_done, past(u * NB + c))
                    pe.wait_ge(att_ready, past(u * NB + c + 1))
                    nc.tensor.matmul(ps_y[:, 0].rearrange("p r d -> p (r d)"), xc[:, 3, cols(c)],
                                     state[:].rearrange("p r d -> p (r d)"), start=True, stop=True)
                    for r in range(HPG):
                        nc.tensor.matmul(ps_y[:, 1, r, :], att[:, r, :], xdt[:, r, :], start=True, stop=True)
                    nc.tensor.matmul(ps_state[:, 0:XW], natural[:, 2 * P:3 * P],
                                     xdte[:].rearrange("p r d -> p (r d)"), start=True, stop=True).then_inc(stage_b, 1)

            for half in range(2):
                for p in range(SSD_PIECES):
                    piece(0, half, p)
            sums(0, 0)
            groups(pe, body)

        @block.scalar
        def _(act):
            act.wait_ge(par_in, 16)
            act.wait_ge(padded, past(1))
            nc.scalar.activation(ah[:], pr[:, :, ALG:ALG + HPG], ACT.Exp).then_inc(a_logged, 1)

            def out(u, half, p):
                n = u * 2 + half
                act.wait_ge(piece_made, past(n * SSD_PIECES + p + 1))
                if p == 0 and not isinstance(n, int):
                    act.wait_ge(raw_used, past(n - 1))
                if p % 2 == 0:
                    nc.scalar.activation(raw[:, half, p // 2, PAD:PAD + HALF], ps_piece[:, p % 2, :],
                                         ACT.Copy).then_inc(piece_out, 1)
                else:
                    nc.scalar.activation(rawz[:, half * HC + p // 2, :], ps_piece[:, p % 2, 0:XW + HPG],
                                         ACT.Copy).then_inc(piece_out, 1)

            def head_out(half, p):
                act.wait_ge(piece_made, past(GROUPS * 2 * SSD_PIECES + half * HG_PIECES + p + 1))
                bank = ps_piece[:, p % 2, 0:HALF if p < 2 else 2 * P]
                nc.scalar.activation(first_piece(Y, half, p), bank, ACT.Copy).then_inc(piece_out, 1)

            def prepare(n, half, part):
                hb, ht = slice(half * HC, (half + 1) * HC), slice(half * HALF, (half + 1) * HALF)
                if part == 0:
                    act.wait_ge(dt_raw, past(n + 1))
                    nc.scalar.activation(step5[:, 1], step5[:, 0], ACT.Abs).then_inc(dt_exp, 1)
                    act.wait_ge(dt_exp, past(2 * n + 1))
                    nc.scalar.activation(step5[:, 1], step5[:, 1], ACT.Exp, scale=-1.0).then_inc(dt_exp, 1)
                    act.wait_ge(dt_onep, past(n + 1))
                    nc.scalar.activation(step5[:, 3], step5[:, 2], ACT.Ln).then_inc(dt_log, 1)
                elif part in (1, 2):
                    if part == 1:
                        nc.scalar.activation(zs[:, hb, :], rawz[:, hb, 0:XW], ACT.Silu).then_inc(z_activated, 1)
                    for i in (0, 1) if part == 1 else (2, 3):
                        act.wait_ge(convolved, past(n * CT + i + 1))
                        nc.scalar.activation(xc[:, i, ht], xc[:, i, ht], ACT.Silu).then_inc(activated, 1)
                else:
                    act.wait_ge(sums_out, past(n + 1))
                    nc.scalar.activation(from_start[:, hb, :], acum[:, hb, :], ACT.Exp, scale=-1.0)
                    nc.scalar.activation(to_end[:, hb, :], to_end[:, hb, :], ACT.Exp, scale=-1.0)
                    nc.scalar.activation(decay_all[:, hb, :], aend[:, hb, :], ACT.Exp, scale=-1.0).then_inc(exps_ready, 1)

            def body(u, last):
                for c in range(NB):
                    half = c // HC
                    act.wait_ge(stage_a, past(u * NB + c + 1))
                    act.wait_ge(chunk_done, past(u * NB + c))
                    nc.scalar.activation(natural[:], ps_turn[:, 0:3 * P], ACT.Copy).then_inc(natural_out, 1)
                    act.wait_ge(diff_ready, past(u * NB + c + 1))
                    nc.scalar.activation(dec[:], dec[:], ACT.Exp, scale=-1.0).then_inc(dec_ready, 1)
                    if not last:
                        out(u + 1, half, 2 * (c % HC))
                    else:
                        head_out(half, HEAD_PARTS[c % HC][0])
                    if not (last and half == 1):
                        prepare(u * 2 + half + 1, 1 - half, c % HC)
                    if not last:
                        out(u + 1, half, 2 * (c % HC) + 1)
                    else:
                        for p in HEAD_PARTS[c % HC][1:]:
                            head_out(half, p)

            for half in range(2):
                for p in range(SSD_PIECES):
                    out(0, half, p)
                if half == 0:
                    for part in range(3):
                        prepare(0, 0, part)
            prepare(0, 0, 3)
            groups(act, body)

        @block.vector
        def _(dve):
            prep, own = Own(dve, own_prep, 6 + CT * (TAPS - 1) + 2), Own(dve, own_mix, HC * 8)

            def per_head(ap):
                return ap.unsqueeze(1).to_broadcast([P, HC, HPG])

            def prepare(u, half, part):
                n = u * 2 + half
                hb, ht = slice(half * HC, (half + 1) * HC), slice(half * HALF, (half + 1) * HALF)
                pu = pr[:, bass.ds(u, 1), :].rearrange("p o c -> p (o c)")
                ahu = ah[:, bass.ds(u, 1), :].rearrange("p o c -> p (o c)")

                def convolve(i):
                    wi = (TAPS + 1) * i
                    prep.done(nc.vector.tensor_scalar(xc[:, i, ht], raw[:, half, i, PAD:PAD + HALF],
                                                      pu[:, wi + PAD:wi + PAD + 1], pu[:, wi + TAPS:wi + TAPS + 1],
                                                      ALU.mult, ALU.add))
                    for k in range(PAD):
                        ins = nc.vector.scalar_tensor_tensor(out=xc[:, i, ht], in0=raw[:, half, i, k:k + HALF],
                                                             scalar=pu[:, wi + k:wi + k + 1], in1=xc[:, i, ht],
                                                             op0=ALU.mult, op1=ALU.add)
                        if k < PAD - 1:
                            prep.done(ins)
                        else:
                            ins.then_inc(convolved, 1)

                if part == 0:
                    prep.at(n)
                    dve.wait_ge(piece_out, past((n + 1) * SSD_PIECES))
                    nc.vector.tensor_tensor(step5[:, 0], rawz[:, hb, XW:XW + HPG], per_head(pu[:, DTB:DTB + HPG]),
                                            ALU.add).then_inc(dt_raw, 1)
                    convolve(0)
                    dve.wait_ge(dt_exp, past(2 * n + 2))
                    nc.vector.tensor_scalar(step5[:, 2], step5[:, 1], 1.0, None, ALU.add).then_inc(dt_onep, 1)
                elif part == 1:
                    dve.wait_ge(dt_onep, past(n + 1))
                    prep.done(nc.vector.tensor_scalar(step5[:, 4], step5[:, 2], 1.0, None, ALU.subtract))
                    prep.done(nc.vector.tensor_tensor(step5[:, 4], step5[:, 1], step5[:, 4], ALU.subtract))
                    dve.wait_ge(dt_log, past(n + 1))
                    prep.done(nc.vector.reciprocal(step5[:, 2], step5[:, 2]))
                    prep.done(nc.vector.tensor_tensor(step5[:, 4], step5[:, 4], step5[:, 2], ALU.mult))
                    prep.done(nc.vector.tensor_tensor(step5[:, 4], step5[:, 4], step5[:, 3], ALU.add))
                    prep.done(nc.vector.scalar_tensor_tensor(out=dt[:, hb, :], in0=step5[:, 0], scalar=0.0,
                                                             in1=step5[:, 4], op0=ALU.max, op1=ALU.add))
                    nc.vector.tensor_tensor(a[:, hb, :], dt[:, hb, :], per_head(ahu), ALU.mult).then_inc(dt_ready, 1)
                    convolve(1)
                elif part == 2:
                    convolve(2)
                    convolve(3)
                    if half == 1:
                        prep.skip()
                    else:
                        prep.done(nc.vector.tensor_copy(raw[:, 1, :, 0:PAD], raw[:, 0, :, HALF:HALF + PAD]))
                    dve.wait_ge(convolved, past((n + 1) * CT))
                    dve.sem_inc(raw_used, 1)
                else:
                    dve.wait_ge(summed, past(n + 1))
                    m = HC * HPG
                    nc.vector.tensor_copy(aend[:, hb, :].rearrange("p c r -> p (c r)"), ps_sum[:, m:2 * m])
                    prep.done(nc.vector.tensor_copy(acum[:, hb, :].rearrange("p c r -> p (c r)"), ps_sum[:, 0:m]))
                    nc.vector.tensor_tensor(to_end[:, hb, :], aend[:, hb, :], acum[:, hb, :],
                                            ALU.subtract).then_inc(sums_out, 1)
                    prep.check()

            def body(u, last):
                pu = pr[:, bass.ds(u, 1), :].rearrange("p o c -> p (o c)")
                for c in range(NB):
                    half = c // HC
                    if c % HC == 0:
                        own.at(u * 2 + half)
                        dve.wait_ge(exps_ready, past(u * 2 + half + 1))
                    if c == 0:
                        dve.wait_ge(stage_b, past(u * NB))
                        nc.vector.memset(state[:], 0.0).then_inc(state_ready, 1)

                    def wide(ap):
                        return ap[:, c, :].unsqueeze(2).to_broadcast([P, HPG, HD])

                    dve.wait_ge(stage_a, past(u * NB + c + 1))
                    dve.wait_ge(stage_b, past(u * NB + c))
                    for r in range(HPG):
                        ins = nc.vector.scalar_tensor_tensor(out=dec[:, r, :], in0=ps_rows[:, r, :],
                                                             scalar=acum[:, c, r:r + 1], in1=C["below"][:],
                                                             op0=ALU.subtract, op1=ALU.max)
                    ins.then_inc(diff_ready, 1)
                    dve.wait_ge(natural_out, past(u * NB + c + 1))
                    xn = natural[:, 0:XW].rearrange("p (r d) -> p r d", r=HPG)
                    own.done(nc.vector.tensor_tensor(xdt[:], xn, wide(dt), ALU.mult))
                    nc.vector.tensor_tensor(xdte[:], xdt[:], wide(to_end), ALU.mult)
                    own.done(nc.vector.tensor_tensor(
                        skip[:], xn, pu[:, DSK:DSK + HPG].unsqueeze(2).to_broadcast([P, HPG, HD]), ALU.mult))
                    dve.wait_ge(dec_ready, past(u * NB + c + 1))
                    nc.vector.tensor_tensor(att[:], dec[:], ps_cb[:, 0:P].unsqueeze(1).to_broadcast([P, HPG, P]),
                                            ALU.mult).then_inc(att_ready, 1)
                    if not (last and half == 1):
                        prepare(u + half, 1 - half, c % HC)
                    dve.wait_ge(stage_b, past(u * NB + c + 1))
                    own.done(nc.vector.tensor_tensor(state[:], state[:], wide(decay_all), ALU.mult))
                    ins = nc.vector.tensor_tensor(state[:], state[:],
                                                  ps_state[:, 0:XW].rearrange("p (r d) -> p r d", r=HPG), ALU.add)
                    own.done(ins)
                    if c < NB - 1:
                        dve.sem_inc(state_ready, 1)
                    own.done(nc.vector.tensor_tensor(y[:], ps_y[:, 0], wide(from_start), ALU.mult))
                    own.done(nc.vector.tensor_tensor(y[:], y[:], ps_y[:, 1], ALU.add))
                    own.done(nc.vector.tensor_tensor(y[:], y[:], skip[:], ALU.add))
                    own.done(nc.vector.tensor_tensor(
                        Y[:, c, bass.ds(u * XW, XW)], y[:].rearrange("p r d -> p (r d)"), zs[:, c, :], ALU.mult))
                    dve.sem_inc(chunk_done, 1)
                    if c % HC == HC - 1:
                        own.check()

            dve.wait_ge(a_logged, past(1))
            for part in range(4):
                prepare(0, 0, part)
            groups(dve, body)


def hgrn(nc, w_hg, lb_logits, C, hnT, Y, osq, ysq):
    with ExitStack() as ctx:
        def sb(name, shape, dt=F32):
            return ctx.enter_context(nc.sbuf_tensor("hg_" + name, shape, dt))

        primed = []

        def plain_sem(name):
            return ctx.enter_context(nc.semaphore("hg_" + name))

        def sem(name):
            primed.append(plain_sem(name))
            return primed[-1]

        def psum(name, shape):
            return ctx.enter_context(nc.psum_tensor("hg_" + name, shape, F32))

        w = sb("w", [P, KT, HG_COLS])
        lbl = sb("lbl", [P, 2, HEADS])
        lb = sb("lb", [P, HEADS])
        oml = sb("oml", [P, HEADS])
        raw_q = sb("raw_q", [P, SEQ])
        raw_f = sb("raw_f", [P, SEQ])
        raw_vg = sb("raw_vg", [P, NB, 2 * P])
        q = sb("q", [P, SEQ])
        k = sb("k", [P, SEQ])
        G = sb("G", [P, SEQ])
        W = sb("W", [P, LEVELS, SEQ])
        qs = sb("qs", [P, SEQ])
        ke = sb("ke", [P, SEQ])
        gend = sb("gend", [P, NB])
        v = sb("v", [P, NB, P])
        gs = sb("gs", [P, NB, P])
        junk = sb("junk", [P, P])
        ss = sb("ss", [P, NB])
        masked = sb("masked", [P, LEVELS + 1, P])
        att = sb("att", [P, P])
        ken = sb("ken", [P, P])
        state = sb("state", [P, P])

        ps_piece = psum("ps_piece", [P, 2, 512])
        ps_att = psum("ps_att", [P, LEVELS + 1, P])
        ps_turn = psum("ps_turn", [P, 512])
        ps_o = psum("ps_o", [P, 512])
        ps_state = psum("ps_state", [P, 512])

        w_in, lb_in = [plain_sem(f"w_in{i}") for i in range(len(HG_PARTS))], plain_sem("lb_in")
        lb_diff, lb_ready = sem("lb_diff"), sem("lb_ready")
        piece_made, piece_out = sem("piece_made"), sem("piece_out")
        gate_sig, gate_ready, gate_logged, summed = (sem("gate_sig"), sem("gate_ready"), sem("gate_logged"),
                                                     sem("summed"))
        q_ready, v_ready, g_ready = sem("q_ready"), sem("v_ready"), sem("g_ready")
        span, decayed, weighted = sem("span"), sem("decayed"), sem("weighted")
        stage_a, stage_b, mask_done = sem("stage_a"), sem("stage_b"), sem("mask_done")
        ken_ready, att_ready, state_ready = sem("ken_ready"), sem("att_ready"), sem("state_ready")
        o_squared, o_gated, kept = sem("o_squared"), sem("o_gated"), sem("kept")
        own_prep, cleared, y_squared = sem("own_prep"), sem("cleared"), sem("y_squared")
        block = ctx.enter_context(nc.Block())

        EARLY = 4

        def heads(eng, body):
            with eng.Fori(0, HEADS - 1) as u:
                body(u, False)
            body(HEADS - 1, True)

        @block.sync
        def _(sp):
            prime(sp, primed)
            sp.dma_start(lbl[:], lb_logits).then_inc(lb_in, 16)
            for i, part in enumerate(HG_PARTS):
                sp.dma_start(w[:, :, part], w_hg[1, :, :, part]).then_inc(w_in[i], 16)
            with sp.Fori(2, HEADS) as u:
                for i, part in enumerate(HG_PARTS):
                    sp.wait_ge(piece_made, past(u * 2 * HG_PIECES - (HG_PIECES - i - 1 if i < 2 else 0)))
                    sp.dma_start(w[:, :, part], w_hg[bass.ds(u, 1), :, :, part].rearrange("o p k c -> p (o k) c")
                                 ).then_inc(w_in[i], 16)

        @block.tensor
        def _(pe):
            def piece(u, half, p):
                if half == 0 and p <= 2:
                    pe.wait_ge(w_in[p], u * 16)
                n = (u * 2 + half) * HG_PIECES + p
                pe.wait_ge(piece_out, past(n - 1))
                bank = ps_piece[:, p % 2, :]
                for kt in range(KT):
                    if p < 2:
                        mm = nc.tensor.matmul(bank, w[:, kt, p * P:(p + 1) * P],
                                              hnT[:, kt, half * HALF:(half + 1) * HALF],
                                              start=(kt == 0), stop=(kt == KT - 1))
                    else:
                        mm = nc.tensor.matmul(bank[:, 0:2 * P], hnT[:, kt, cols(half * HC + p - 2)],
                                              w[:, kt, 2 * P:4 * P], start=(kt == 0), stop=(kt == KT - 1))
                mm.then_inc(piece_made, 1)

            def body(u, last):
                for c in range(NB):
                    half = c // HC
                    if c % HC == 0:
                        pe.wait_ge(weighted, past((u * 2 + half + 1) * (LEVELS + 2)))
                        pe.wait_ge(v_ready, past(u * 2 + half + 1))
                    pe.wait_ge(att_ready, past(u * NB + c))
                    pe.wait_ge(ken_ready, past(u * NB + c))
                    for j in range(LEVELS):
                        right = W[:, j, cols(c)].rearrange("p (b two h) -> p b two h", two=2, h=P >> (j + 1))
                        nc.tensor.matmul(ps_att[:, j, 0:P // 2], W[:, j, cols(c)], right[:, :, 1, :],
                                         start=True, stop=True)
                    nc.tensor.matmul(ps_att[:, LEVELS, :], k[:, cols(c)], q[:, cols(c)], start=True, stop=True)
                    nc.tensor.transpose(ps_turn[:, 0:P], ke[:, cols(c)], C["ident"][:]).then_inc(stage_a, 1)
                    if not last:
                        for p in HEAD_PARTS[c % HC]:
                            piece(u + 1, half, p)
                    pe.wait_ge(state_ready, past(u * NB + c + 1))
                    pe.wait_ge(o_gated, past(u * NB + c))
                    pe.wait_ge(o_squared, past(u * NB + c))
                    pe.wait_ge(ken_ready, past(u * NB + c + 1))
                    nc.tensor.matmul(ps_state[:, 0:P], ken[:], v[:, c, :], start=True, stop=True)
                    nc.tensor.matmul(ps_o[:, 0:P], qs[:, cols(c)], state[:], start=True, stop=False)
                    pe.wait_ge(att_ready, past(u * NB + c + 1))
                    nc.tensor.matmul(ps_o[:, 0:P], att[:], v[:, c, :], start=False, stop=True).then_inc(stage_b, 1)

            pe.sem_inc(piece_made, 2 * HG_PIECES)
            heads(pe, body)

        @block.scalar
        def _(act):
            def first_out(half, p):
                place = (raw_q, raw_f)[p][:, half * HALF:(half + 1) * HALF] if p < 2 else raw_vg[:, half * HC + p - 2, :]
                nc.scalar.activation(place, first_piece(Y, half, p), ACT.Copy).then_inc(piece_out, 1)

            def out(u, half, p):
                n = u * 2 + half
                act.wait_ge(piece_made, past(n * HG_PIECES + p + 1))
                if p < 2:
                    nc.scalar.activation((raw_q, raw_f)[p][:, half * HALF:(half + 1) * HALF], ps_piece[:, p % 2, :],
                                         ACT.Copy).then_inc(piece_out, 1)
                else:
                    if p == 2:
                        act.wait_ge(v_ready, past(n - 1))
                    nc.scalar.activation(raw_vg[:, half * HC + p - 2, :], ps_piece[:, p % 2, 0:2 * P],
                                         ACT.Copy).then_inc(piece_out, 1)

            def prepare(n, half, part):
                hb, ht = slice(half * HC, (half + 1) * HC), slice(half * HALF, (half + 1) * HALF)
                if part == 0:
                    act.wait_ge(piece_out, past((n + 1) * HG_PIECES))
                    nc.scalar.activation(G[:, ht], raw_f[:, ht], ACT.Sigmoid).then_inc(gate_sig, 1)
                    nc.scalar.activation(q[:, ht], raw_q[:, ht], ACT.Silu).then_inc(q_ready, 1)
                    nc.scalar.activation(gs[:, hb, :], raw_vg[:, hb, P:2 * P], ACT.Silu).then_inc(g_ready, 1)
                    act.wait_ge(gate_ready, past(n + 1))
                    nc.scalar.activation(G[:, ht], G[:, ht], ACT.Ln).then_inc(gate_logged, 1)
                elif part in (1, 2):
                    for j in range(EARLY) if part == 1 else range(EARLY, LEVELS):
                        act.wait_ge(span, past(n * (LEVELS + 1) + j + 1))
                        nc.scalar.activation(W[:, j, ht], W[:, j, ht], ACT.Exp).then_inc(decayed, 1)
                    if part == 2:
                        act.wait_ge(span, past((n + 1) * (LEVELS + 1)))
                        nc.scalar.activation(ke[:, ht], ke[:, ht], ACT.Exp).then_inc(decayed, 1)
                        nc.scalar.activation(qs[:, ht], G[:, ht], ACT.Exp).then_inc(decayed, 1)
                        nc.scalar.activation(gend[:, hb], G[:, ht].rearrange("p (c l) -> p c l", l=P)[:, :, P - 1],
                                             ACT.Exp).then_inc(decayed, 1)

            def body(u, last):
                for c in range(NB):
                    half = c // HC
                    act.wait_ge(stage_a, past(u * NB + c + 1))
                    act.wait_ge(stage_b, past(u * NB + c))
                    nc.scalar.activation(ken[:], ps_turn[:, 0:P], ACT.Copy).then_inc(ken_ready, 1)
                    if not last:
                        for p in HEAD_PARTS[c % HC]:
                            out(u + 1, half, p)
                    if not (last and half == 1):
                        prepare(u * 2 + half + 1, 1 - half, c % HC)
                    if last and half == 1:
                        for b in (2 * (c % HC), 2 * (c % HC) + 1):
                            act.wait_ge(y_squared, past(b))
                            nc.scalar.activation(raw_f[:], Y[:, b, 0:D], ACT.Square,
                                                 accum_out=ysq[:, b:b + 1]).then_inc(y_squared, 1)
                    act.wait_ge(o_gated, past(u * NB + c + 1))
                    if c == 0:
                        act.wait_ge(kept, past(u))
                    act.wait_ge(o_squared, past(u * NB + c))
                    nc.scalar.activation(junk[:], ps_o[:, 0:P], ACT.Square,
                                         accum_out=ss[:, c:c + 1]).then_inc(o_squared, 1)

            for p in range(HG_PIECES):
                first_out(0, p)
            act.wait_ge(lb_diff, past(1))
            nc.scalar.activation(lb[:], lb[:], ACT.Sigmoid).then_inc(lb_ready, 1)
            act.wait_ge(lb_ready, past(1))
            nc.scalar.activation(oml[:], lb[:], ACT.Copy, scale=-1.0, bias=1.0).then_inc(lb_ready, 1)
            prepare(0, 0, 0)
            for p in range(HG_PIECES):
                first_out(1, p)
            for part in (1, 2):
                prepare(0, 0, part)
            heads(act, body)

        @block.vector
        def _(dve):
            prep = Own(dve, own_prep, 1)
            nc.vector.memset(masked[:], 0.0).then_inc(cleared, 1)
            dve.wait_ge(cleared, past(1))
            dve.wait_ge(lb_in, 16)
            nc.vector.tensor_tensor(lb[:], lbl[:, 0, :], lbl[:, 1, :], ALU.subtract).then_inc(lb_diff, 1)
            dve.wait_ge(lb_ready, past(2))

            def prepare(u, half, part):
                n = u * 2 + half
                hb, ht = slice(half * HC, (half + 1) * HC), slice(half * HALF, (half + 1) * HALF)

                def halves(ap, j):
                    return ap.rearrange("p (b two h) -> p b two h", two=2, h=P >> (j + 1))

                def spans(js):
                    for j in js:
                        h = P >> (j + 1)
                        gv, wv = halves(G[:, ht], j), halves(W[:, j, ht], j)
                        at = gv[:, :, 0, h - 1:h].to_broadcast([P, HALF // (2 * h), h])
                        nc.vector.tensor_tensor(wv[:, :, 0, :], at, gv[:, :, 0, :], ALU.subtract)
                        nc.vector.tensor_tensor(wv[:, :, 1, :], gv[:, :, 1, :], at, ALU.subtract).then_inc(span, 1)

                def weights(js):
                    for j in js:
                        dve.wait_ge(decayed, past(n * (LEVELS + 3) + j + 1))
                        wv = halves(W[:, j, ht], j)
                        nc.vector.tensor_tensor(wv[:, :, 0, :], wv[:, :, 0, :], halves(k[:, ht], j)[:, :, 0, :], ALU.mult)
                        nc.vector.tensor_tensor(wv[:, :, 1, :], wv[:, :, 1, :], halves(q[:, ht], j)[:, :, 1, :],
                                                ALU.mult).then_inc(weighted, 1)

                if part == 0:
                    prep.at(n)
                    dve.wait_ge(gate_sig, past(n + 1))
                    prep.done(nc.vector.tensor_scalar(G[:, ht], G[:, ht], oml[:, bass.ds(u, 1)], lb[:, bass.ds(u, 1)],
                                                      ALU.mult, ALU.add))
                    nc.vector.tensor_scalar(k[:, ht], G[:, ht], -1.0, 1.0, ALU.mult, ALU.add).then_inc(gate_ready, 1)
                    dve.wait_ge(piece_out, past((n + 1) * HG_PIECES))
                    nc.vector.tensor_copy(v[:, hb, :], raw_vg[:, hb, 0:P]).then_inc(v_ready, 1)
                elif part == 1:
                    dve.wait_ge(gate_logged, past(n + 1))
                    nc.vector.tensor_tensor_scan(G[:, ht], C["reset"][:, ht], G[:, ht], 0.0,
                                                 ALU.mult, ALU.add).then_inc(summed, 1)
                    dve.wait_ge(summed, past(n + 1))
                    spans(range(EARLY))
                elif part == 2:
                    spans(range(EARLY, LEVELS))
                    gc = G[:, ht].rearrange("p (c l) -> p c l", l=P)
                    nc.vector.tensor_tensor(ke[:, ht].rearrange("p (c l) -> p c l", l=P),
                                            gc[:, :, P - 1:P].to_broadcast([P, HC, P]), gc, ALU.subtract).then_inc(span, 1)
                    dve.wait_ge(q_ready, past(n + 1))
                    weights(range(EARLY))
                else:
                    weights(range(EARLY, LEVELS))
                    dve.wait_ge(decayed, past((n + 1) * (LEVELS + 3)))
                    nc.vector.tensor_tensor(ke[:, ht], ke[:, ht], k[:, ht], ALU.mult).then_inc(weighted, 1)
                    nc.vector.tensor_tensor(qs[:, ht], qs[:, ht], q[:, ht], ALU.mult).then_inc(weighted, 1)
                    prep.check()

            def body(u, last):
                dve.wait_ge(stage_b, past(u * NB))
                nc.vector.memset(state[:], 0.0).then_inc(state_ready, 1)
                for c in range(NB):
                    half = c // HC
                    if c % HC == 0:
                        dve.wait_ge(g_ready, past(u * 2 + half + 1))
                    dve.wait_ge(stage_a, past(u * NB + c + 1))
                    for j in range(LEVELS):
                        h = P >> (j + 1)

                        def right(ap):
                            return ap[:, j, :].rearrange("p (b two h) -> p b two h", two=2, h=h)[:, :, 1, :]

                        nc.vector.tensor_tensor(right(masked[:]), ps_att[:, j, 0:P // 2].rearrange("p (b h) -> p b h", h=h),
                                                right(C["lmask"][:]), ALU.mult)
                    nc.vector.tensor_tensor(masked[:, LEVELS, :], ps_att[:, LEVELS, :], C["lmask"][:, LEVELS, :],
                                            ALU.mult).then_inc(mask_done, 1)
                    dve.wait_ge(mask_done, past(u * NB + c + 1))
                    dve.wait_ge(stage_b, past(u * NB + c))
                    nc.vector.tensor_reduce(att[:], masked[:].rearrange("p j l -> p l j"), AX.X,
                                            ALU.add).then_inc(att_ready, 1)
                    if not (last and half == 1):
                        prepare(u + half, 1 - half, c % HC)
                    dve.wait_ge(stage_b, past(u * NB + c + 1))
                    if c < NB - 1:
                        dve.wait_ge(state_ready, past(u * NB + c + 1))
                        nc.vector.scalar_tensor_tensor(out=state[:], in0=state[:], scalar=gend[:, c:c + 1],
                                                       in1=ps_state[:, 0:P], op0=ALU.mult,
                                                       op1=ALU.add).then_inc(state_ready, 1)
                    nc.vector.tensor_tensor(Y[:, c, bass.ds(D + u * P, P)], ps_o[:, 0:P], gs[:, c, :],
                                            ALU.mult).then_inc(o_gated, 1)
                dve.wait_ge(o_squared, past((u + 1) * NB))
                nc.vector.tensor_scalar(osq[:, :, bass.ds(u, 1)].rearrange("p c o -> p (c o)"), ss[:], 1.0, None,
                                        ALU.mult).then_inc(kept, 1)

            for part in range(4):
                prepare(0, 0, part)
            heads(dve, body)
            dve.wait_ge(kept, past(HEADS))


def mix_out(nc, x, w_out, mix_w, ffn_w, w_query, C, Y, osq, ysq, xnT, wq, wq_in):
    with ExitStack() as ctx:
        def sb(name, shape, dt=F32):
            return ctx.enter_context(nc.sbuf_tensor("mo_" + name, shape, dt))

        primed = []

        def plain_sem(name):
            return ctx.enter_context(nc.semaphore("mo_" + name))

        def sem(name):
            primed.append(plain_sem(name))
            return primed[-1]

        def psum(name, shape):
            return ctx.enter_context(nc.psum_tensor("mo_" + name, shape, F32))

        w = sb("w", [P, MT, D])
        mw = sb("mw", [P, MT])
        fw = sb("fw", [P, D])
        ys = sb("ys", [P, MIX])
        yT = sb("yT", [P, MT, P])
        xr = sb("xr", [P, D])
        h = sb("h", [P, D])
        xn = sb("xn", [P, D])
        sq = sb("sq", [P, D])
        ss = sb("ss", [P, 1])
        rs = sb("rs", [P, 1])
        ry = sb("ry", [P, 1])
        ps_y = psum("ps_y", [P, 4, P])
        ps_y2 = psum("ps_y2", [P, 4, P])
        ps_h = psum("ps_h", [P, 2, 512])
        ps_x = psum("ps_x", [P, KT, P])
        GRP = 4
        NG = MT // GRP
        EARLY, LATE = [0, 1], [2, 3]

        w_in, s_in, x_in = [plain_sem(f"w_in{g}") for g in range(NG)], plain_sem("s_in"), plain_sem("x_in")
        meaned, rooted, inverse = sem("meaned"), sem("rooted"), sem("inverse")
        root_taken, early_used = sem("root_taken"), sem("early_used")
        ys_scaled, ys_copied = sem("ys_scaled"), sem("ys_copied")
        y_turned, yT_ready = sem("y_turned"), sem("yT_ready")
        product, h_ready, h_squared, h_meaned, h_rooted, h_inverse = (
            sem("product"), sem("h_ready"), sem("h_squared"), sem("h_meaned"), sem("h_rooted"), sem("h_inverse"))
        xn_ready, xn_turned, xnT_ready, kept = sem("xn_ready"), sem("xn_turned"), sem("xnT_ready"), sem("kept")
        act_turn, dve_turn, pool_turn = sem("act_turn"), sem("dve_turn"), sem("pool_turn")
        xd = x.rearrange("o (b p) d -> p (o b) d", p=P)
        block = ctx.enter_context(nc.Block())

        def in_steps(eng, step):
            step(0, True, False)
            with eng.Fori(1, NB - 1) as b:
                step(b, False, False)
            step(NB - 1, False, True)

        @block.sync
        def _(sp):
            prime(sp, primed)
            sp.dma_start(mw[:], mix_w).then_inc(s_in, 16)
            sp.dma_start(fw[:], ffn_w).then_inc(s_in, 16)
            for g in range(NG):
                ks = slice(g * GRP, (g + 1) * GRP)
                sp.dma_start(w[:, ks, :], w_out[:, ks, :]).then_inc(w_in[g], 16)
            with sp.Fori(0, NB) as b:
                sp.wait_ge(h_ready, past(b))
                sp.dma_start(xr[:], xd[:, bass.ds(b, 1), :].rearrange("p o d -> p (o d)")).then_inc(x_in, 16)
            sp.dma_start(wq[:], w_query[0]).then_inc(wq_in, 16)

        @block.tensor
        def _(pe):
            def turn_y(b, gs):
                for g in gs:
                    pe.wait_ge(ys_scaled if g < NG // 2 else ys_copied, past(b + 1))
                    if not (isinstance(b, int) and b == 0 and g < 2):
                        pe.wait_ge(yT_ready, past(b * MT + GRP * (g - 1)))
                    bank = (ps_y, ps_y2)[g % 2]
                    for j in range(GRP):
                        k = g * GRP + j
                        mm = nc.tensor.transpose(bank[:, j, :], ys[:, k * P:(k + 1) * P], C["ident"][:])
                    mm.then_inc(y_turned, 1)

            def turn_x(b):
                pe.wait_ge(xn_ready, past(b + 1))
                pe.wait_ge(xnT_ready, past(b))
                for k in range(KT):
                    mm = nc.tensor.transpose(ps_x[:, k, :], xn[:, k * P:(k + 1) * P], C["ident"][:])
                mm.then_inc(xn_turned, 1)

            def multiply(b, gs):
                for k in range(gs[0] * GRP, (gs[-1] + 1) * GRP):
                    if isinstance(b, int) and k % GRP == 0:
                        pe.wait_ge(w_in[k // GRP], 16)
                    pe.wait_ge(yT_ready, past(b * MT + k + 1))
                    for half in range(2):
                        mm = nc.tensor.matmul(ps_h[:, half, :], yT[:, k, :], w[:, k, half * 512:(half + 1) * 512],
                                              start=(k == 0), stop=(k == MT - 1))
                return mm

            def step(b, first, last):
                pe.wait_ge(h_ready, past(b))
                multiply(b, EARLY).then_inc(early_used, 1)
                if not first:
                    turn_x(b - 1)
                if not last:
                    turn_y(b + 1, EARLY)
                multiply(b, LATE).then_inc(product, 1)
                if not last:
                    turn_y(b + 1, LATE)

            turn_y(0, EARLY + LATE)
            in_steps(pe, step)
            turn_x(NB - 1)

        @block.scalar
        def _(act):
            act.wait_ge(s_in, 32)

            def out_y(b, gs):
                for g in gs:
                    act.wait_ge(y_turned, past(b * NG + g + 1))
                    act.wait_ge(early_used if g in EARLY else product, past(b))
                    for j in range(GRP):
                        k = g * GRP + j
                        nc.scalar.activation(yT[:, k, :], ((ps_y, ps_y2)[g % 2])[:, j, :], ACT.Copy,
                                             scale=mw[:, k:k + 1]).then_inc(yT_ready, 1)

            def turned_out(b):
                act.wait_ge(xn_turned, past(b + 1))
                act.sem_inc(act_turn, 1)
                nc.scalar.activation(xnT[:, :, bass.ds(b * P, P)], ps_x[:], ACT.Copy).then_inc(xnT_ready, 1)

            def step(b, first, last):
                if not first:
                    turned_out(b - 1)
                if not last:
                    out_y(b + 1, EARLY)
                act.wait_ge(h_ready, past(b + 1))
                nc.scalar.activation(sq[:], h[:], ACT.Square, accum_out=ss[:]).then_inc(h_squared, 1)
                act.wait_ge(h_meaned, past(b + 1))
                nc.scalar.activation(rs[:], ss[:], ACT.Sqrt).then_inc(h_rooted, 1)
                if not last:
                    out_y(b + 1, LATE)

            act.wait_ge(meaned, past(2))
            nc.scalar.activation(osq[:], osq[:], ACT.Sqrt).then_inc(rooted, 1)
            nc.scalar.activation(ysq[:], ysq[:], ACT.Sqrt).then_inc(rooted, 1)
            out_y(0, EARLY + LATE)
            in_steps(act, step)
            turned_out(NB - 1)

        @block.gpsimd
        def _(pool):
            def copy_y(b):
                pool.wait_ge(y_turned, past(b * NG))
                pool.sem_inc(pool_turn, 1)
                nc.gpsimd.tensor_tensor(ys[:, D:MIX].rearrange("p (h d) -> p h d", h=HEADS),
                                        Y[:, bass.ds(b, 1), D:MIX].rearrange("p o (h d) -> p (o h) d", h=HEADS),
                                        osq[:, bass.ds(b, 1), :].rearrange("p o h -> p (o h)").unsqueeze(2)
                                        .to_broadcast([P, HEADS, P]), ALU.mult).then_inc(ys_copied, 1)

            def step(b, first, last):
                if not last:
                    copy_y(b + 1)
                pool.wait_ge(h_ready, past(b + 1))
                pool.sem_inc(pool_turn, 1)
                nc.gpsimd.tensor_copy(Y[:, bass.ds(b, 1), 0:D].rearrange("p o d -> p (o d)"), h[:])
                pool.wait_ge(xn_ready, past(b + 1))
                pool.wait_ge(ys_copied, past(b + 1))
                pool.sem_inc(pool_turn, 1)
                nc.gpsimd.tensor_copy(Y[:, bass.ds(b, 1), D:MIX].rearrange("p o d -> p (o d)"), xn[:]).then_inc(kept, 1)

            pool.wait_ge(inverse, past(2))
            copy_y(0)
            in_steps(pool, step)

        @block.vector
        def _(dve):
            def scale_y(b):
                dve.wait_ge(y_turned, past(b * NG))
                dve.sem_inc(dve_turn, 1)
                nc.vector.tensor_copy(ry[:], ysq[:, bass.ds(b, 1)]).then_inc(root_taken, 1)
                dve.wait_ge(root_taken, past(b + 1))
                nc.vector.tensor_scalar(ys[:, 0:D], Y[:, bass.ds(b, 1), 0:D].rearrange("p o d -> p (o d)"),
                                        ry[:], None, ALU.mult).then_inc(ys_scaled, 1)

            def step(b, first, last):
                if not last:
                    scale_y(b + 1)
                dve.wait_ge(x_in, (b + 1) * 16)
                dve.wait_ge(kept, past(b))
                dve.wait_ge(product, past(b + 1))
                nc.vector.tensor_tensor(h[:], ps_h[:].rearrange("p a c -> p (a c)"), xr[:], ALU.add).then_inc(h_ready, 1)
                dve.wait_ge(h_squared, past(b + 1))
                nc.vector.tensor_scalar(ss[:], ss[:], 1.0 / D, EPS, ALU.mult, ALU.add).then_inc(h_meaned, 1)
                dve.wait_ge(h_rooted, past(b + 1))
                nc.vector.reciprocal(rs[:], rs[:]).then_inc(h_inverse, 1)
                dve.wait_ge(h_inverse, past(b + 1))
                dve.wait_ge(xn_turned, past(b))
                nc.vector.scalar_tensor_tensor(out=xn[:], in0=h[:], scalar=rs[:], in1=fw[:],
                                               op0=ALU.mult, op1=ALU.mult).then_inc(xn_ready, 1)

            nc.vector.tensor_scalar(osq[:], osq[:], 1.0 / P, EPS, ALU.mult, ALU.add).then_inc(meaned, 1)
            nc.vector.tensor_scalar(ysq[:], ysq[:], 1.0 / D, EPS, ALU.mult, ALU.add).then_inc(meaned, 1)
            dve.wait_ge(rooted, past(2))
            nc.vector.reciprocal(osq[:], osq[:]).then_inc(inverse, 1)
            nc.vector.reciprocal(ysq[:], ysq[:]).then_inc(inverse, 1)
            dve.wait_ge(inverse, past(2))
            scale_y(0)
            in_steps(dve, step)
            dve.wait_ge(kept, past(NB))


def peer(nc, w_query, keys, table, fin_w, C, Y, xnT, wq, wq_in, out):
    with ExitStack() as ctx:
        def sb(name, shape, dt=F32):
            return ctx.enter_context(nc.sbuf_tensor("peer_" + name, shape, dt))

        primed = []

        def plain_sem(name):
            return ctx.enter_context(nc.semaphore("peer_" + name))

        def sem(name):
            primed.append(plain_sem(name))
            return primed[-1]

        def psum(name, shape):
            return ctx.enter_context(nc.psum_tensor("peer_" + name, shape, F32))

        ring = sb("ring", [P, RING, 2 * D])
        kT = sb("kT", [P, PH * 2 * KEYS])
        qs = sb("qs", [P, 2, P])
        sc = sb("sc", [P, 2, KEYS])
        sc2 = sb("sc2", [P, 2, KEYS])
        top = sb("top", [P, 2, TOPK])
        ix = sb("ix", [P, 2, TOPK], U32)
        ixf = sb("ixf", [P, 2, TOPK])
        cand = sb("cand", [P, NCAND])
        cand2 = sb("cand2", [P, NCAND])
        expert = sb("expert", [P, NCAND])
        best = sb("best", [P, TOPK])
        place = sb("place", [P, TOPK], U32)
        placef = sb("placef", [P, TOPK])
        count_u = sb("count_u", [P, NCAND], U32)
        count = sb("count", [P, NCAND])
        hit = sb("hit", [P, TOPK, NCAND])
        chosen = sb("chosen", [P, TOPK])
        neg = sb("neg", [P, 1])
        gx = sb("gx", [P, TOPK])
        gsum = sb("gsum", [P, 1])
        index = sb("index", [P, NB, TOPK], U32)
        gate = sb("gate", [P, NB, TOPK])
        index_even = sb("index_even", [P, TOPK], U32)
        index_odd = sb("index_odd", [P, TOPK], U32)
        gate_now = sb("gate_now", [P, TOPK])
        junk = sb("junk", [P, D])
        dots = sb("dots", [P, TOPK])
        act_out = sb("act_out", [P, BATCH])
        hid = sb("hid", [P, BATCH])
        diag = sb("diag", [P, RING, P])
        fw = sb("fw", [P, D])
        result = sb("result", [P, D])
        fss = sb("fss", [P, 1])
        frs = sb("frs", [P, 1])

        ps_q = psum("ps_q", [P, 2, 256])
        ps_s = psum("ps_s", [P, 2, 256])
        ps_o = psum("ps_o", [P, 2, 512])

        got = [plain_sem(f"got{s}") for s in range(RING)]
        counted = sem("counted")
        q_made, q_out, scores_made, scores_out, picked = (sem("q_made"), sem("q_out"), sem("scores_made"),
                                                          sem("scores_out"), sem("picked"))
        best_ready, gates_ready, routed = sem("best_ready"), sem("gates_ready"), sem("routed")
        index_taken, gate_taken = sem("index_taken"), sem("gate_taken")
        free_slots = plain_sem("free_slots")
        dot_ready, act_own, diag_ready, activated = sem("dot_ready"), sem("act_own"), sem("diag_ready"), sem("activated")
        added = sem("added")
        k_in, fw_in, written = plain_sem("k_in"), plain_sem("fw_in"), plain_sem("written")
        f_squared, f_meaned, f_rooted, f_inverse, f_normed = (sem("f_squared"), sem("f_meaned"), sem("f_rooted"),
                                                              sem("f_inverse"), sem("f_normed"))
        od = out.rearrange("o (b p) d -> p (o b) d", p=P)
        dve_own, dve_turn, act_turn, pool_turn = sem("dve_own"), sem("dve_turn"), sem("act_turn"), sem("pool_turn")
        block = ctx.enter_context(nc.Block())

        KEYS_PART, PAIRS_PART, EXPERTS_PART = range(3)
        ALL = (KEYS_PART, PAIRS_PART, EXPERTS_PART)

        def loops(eng, route_pass, gather_pass):
            def same_head(h, first, finish):
                with eng.Fori(first, NB - LAG) as b:
                    n = h * NB + b
                    gather_pass(n, b, lambda part=ALL: route_pass(n + LAG, h, b + LAG, n, part), finish)

            with eng.Fori(0, LAG) as b:
                route_pass(b, 0, b, None, ALL)
            with eng.Fori(0, PH - 1) as h:
                same_head(h, 0, False)
                with eng.Fori(0, LAG) as b:
                    n = h * NB + (NB - LAG) + b
                    gather_pass(n, b + (NB - LAG), lambda part=ALL: route_pass(n + LAG, h + 1, b, n, part), False)
            n = (PH - 1) * NB
            gather_pass(n, 0, lambda part=ALL: route_pass(n + LAG, PH - 1, LAG, n, part), False)
            same_head(PH - 1, 1, True)
            with eng.Fori(0, LAG) as b:
                gather_pass(b + (PH * NB - LAG), b + (NB - LAG), None, True)

        @block.sync
        def _(sp):
            prime(sp, primed)
            sp.dma_start(kT[:], keys).then_inc(k_in, 16)
            sp.dma_start(fw[:], fin_w).then_inc(fw_in, 16)
            sp.sem_inc(written, 16)
            with sp.Fori(1, PH) as h:
                sp.wait_ge(q_made, past(h * NB))
                sp.dma_start(wq[:], w_query[bass.ds(h, 1)].rearrange("o p k c -> p (o k) c")).then_inc(wq_in, 16)
            with sp.Fori(0, NB) as b:
                sp.wait_ge(f_normed, past(b + 1))
                sp.dma_start(od[:, bass.ds(b, 1), :].rearrange("p o d -> p (o d)"), result[:]).then_inc(written, 16)
            sp.wait_ge(written, (NB + 1) * 16)

        @block.gpsimd
        def _(pool):
            nc.gpsimd.iota(count_u[:], pattern=[[1, NCAND]], base=0, channel_multiplier=0).then_inc(counted, 1)
            pool.sem_inc(free_slots, RING)

            def gather(n, b, index_now):
                pool.wait_ge(routed, past(n + 1))
                pool.sem_inc(pool_turn, 1)
                nc.gpsimd.tensor_copy(index_now[:], index[:, bass.ds(b, 1), :].rearrange("p o k -> p (o k)")
                                      ).then_inc(index_taken, 1)
                pool.wait_ge(index_taken, past(n + 1))
                for k in range(TOPK):
                    pool.wait_ge(free_slots, n * TOPK + k + 1)
                    pool.sem_inc(pool_turn, 1)
                    pool.indirect_dma_start(ring[:, k % RING, :], None, table,
                                            bass.IndirectOffsetOnAxis(ap=index_now[:, k:k + 1], axis=0)
                                            ).then_inc(got[k % RING], 16)

            with pool.Fori(0, PH) as h:
                with pool.Fori(0, NB // 2) as pair:
                    gather(h * NB + pair * 2, pair * 2, index_even)
                    gather(h * NB + pair * 2 + 1, pair * 2 + 1, index_odd)

        @block.tensor
        def _(pe):
            def query(n, h, b):
                pe.wait_ge(wq_in, (h + 1) * 16)
                pe.wait_ge(q_out, past(n))
                for p in range(2):
                    for k in range(KT):
                        mm = nc.tensor.matmul(ps_q[:, p, 0:P], wq[:, k, p * P:(p + 1) * P],
                                              xnT[:, k, bass.ds(b * P, P)], start=(k == 0), stop=(k == KT - 1))
                mm.then_inc(q_made, 1)

            def score(n, h):
                pe.wait_ge(k_in, 16)
                pe.wait_ge(q_out, past(n + 1))
                pe.wait_ge(scores_out, past(n))
                for p in range(2):
                    mm = nc.tensor.matmul(ps_s[:, p, 0:P], qs[:, p, :], kT[:, bass.ds((h * 2 + p) * KEYS, KEYS)],
                                          start=True, stop=True)
                mm.then_inc(scores_made, 1)

            def route(n, h, b, last, part):
                query(n, h, b)
                score(n, h)

            def gather(n, b, route_next, finish_last):
                if route_next:
                    route_next()
                pe.wait_ge(added, past(n))
                for k in range(TOPK):
                    pe.wait_ge(diag_ready, past(n * TOPK + k + 1))
                    for half in range(2):
                        mm = nc.tensor.matmul(ps_o[:, half, :], diag[:, k % RING, :],
                                              ring[:, k % RING, D + half * 512:D + (half + 1) * 512],
                                              start=(k == 0), stop=(k == TOPK - 1))
                    mm.then_inc(free_slots, 1)

            loops(pe, route, gather)

        @block.scalar
        def _(act):
            def scores(n):
                act.wait_ge(q_made, past(n + 1))
                act.wait_ge(scores_made, past(n))
                nc.scalar.activation(qs[:], ps_q[:, :, 0:P], ACT.Copy).then_inc(q_out, 1)
                act.wait_ge(scores_made, past(n + 1))
                act.wait_ge(picked, past(n))
                nc.scalar.activation(sc[:], ps_s[:, :, 0:KEYS], ACT.Copy).then_inc(scores_out, 1)

            def gates(n):
                act.wait_ge(best_ready, past(n + 1))
                nc.scalar.activation(gx[:], best[:], ACT.Exp, bias=neg[:], accum_out=gsum[:]).then_inc(gates_ready, 1)

            def route(n, h, b, last, part):
                scores(n)
                gates(n)

            def finish(b):
                act.wait_ge(added, past((PH - 1) * NB + b + 1))
                act.wait_ge(written, (b + 1) * 16)
                act.sem_inc(act_turn, 1)
                nc.scalar.activation(result[:], Y[:, bass.ds(b, 1), 0:D].rearrange("p o d -> p (o d)"), ACT.Square,
                                     accum_out=fss[:]).then_inc(f_squared, 1)
                act.wait_ge(f_meaned, past(b + 1))
                nc.scalar.activation(frs[:], fss[:], ACT.Sqrt).then_inc(f_rooted, 1)

            def gather(n, b, route_next, finish_last):
                if route_next:
                    scores(n + LAG)
                own = Own(act, act_own, TOPK)
                own.at(n)
                act.wait_ge(routed, past(n + 1))
                act.sem_inc(act_turn, 1)
                nc.scalar.activation(gate_now[:], gate[:, bass.ds(b, 1), :].rearrange("p o k -> p (o k)"),
                                     ACT.Copy).then_inc(gate_taken, 1)
                act.wait_ge(gate_taken, past(n + 1))
                for q in range(TOPK // BATCH):
                    act.wait_ge(dot_ready, past(n * TOPK + (q + 1) * BATCH))
                    nc.scalar.activation(act_out[:], dots[:, q * BATCH:(q + 1) * BATCH], ACT.Gelu).then_inc(activated, 1)
                    act.wait_ge(activated, past(n * (TOPK // BATCH) + q + 1))
                    for j in range(BATCH):
                        k = q * BATCH + j
                        own.step(nc.scalar.activation(hid[:, j:j + 1], act_out[:, j:j + 1], ACT.Copy,
                                                      scale=gate_now[:, k:k + 1]))
                    own.wait()
                    for j in range(BATCH):
                        k = q * BATCH + j
                        act.wait_ge(free_slots, n * TOPK + k + 1)
                        ins = nc.scalar.activation(diag[:, k % RING, :], C["ident"][:], ACT.Copy, scale=hid[:, j:j + 1])
                        ins.then_inc(diag_ready, 1)
                    if finish_last and q == TOPK // BATCH // 2 - 1:
                        finish(b - 1)
                own.check()
                if route_next:
                    gates(n + LAG)

            loops(act, route, gather)
            finish(NB - 1)

        @block.vector
        def _(dve):
            dve.wait_ge(counted, past(1))
            nc.vector.tensor_copy(count[:], count_u[:]).then_inc(counted, 1)
            dve.wait_ge(counted, past(2))

            ROUTE_STEPS = (9, 6, 4)

            def part_own(n, part):
                own = Own(dve, dve_own, sum(ROUTE_STEPS))
                own.at(n)
                own.n = sum(ROUTE_STEPS[:part])

                def hold():
                    own.wait()
                    dve.sem_inc(dve_turn, 1)

                def check():
                    assert own.n == sum(ROUTE_STEPS[:part + 1])

                return own, hold, check

            def route_keys(n):
                own, hold, check = part_own(n, KEYS_PART)
                dve.wait_ge(scores_out, past(n + 1))
                dve.sem_inc(dve_turn, 1)
                for p in range(2):
                    own.step(nc.vector.max(top[:, p, 0:8], sc[:, p, :]))
                hold()
                for p in range(2):
                    nc.vector.max_index(ix[:, p, 0:8], top[:, p, 0:8], sc[:, p, :])
                    own.step(nc.vector.match_replace(sc2[:, p, :], top[:, p, 0:8], sc[:, p, :], LOW))
                hold()
                dve.sem_inc(picked, 1)
                for p in range(2):
                    own.step(nc.vector.max(top[:, p, 8:16], sc2[:, p, :]))
                hold()
                for p in range(2):
                    ins = nc.vector.max_index(ix[:, p, 8:16], top[:, p, 8:16], sc2[:, p, :])
                own.done(ins)
                own.done(nc.vector.tensor_copy(ixf[:], ix[:]))
                own.done(nc.vector.tensor_scalar(ixf[:, 0, :], ixf[:, 0, :], float(KEYS), None, ALU.mult))
                check()

            def route_pairs(n):
                own, hold, check = part_own(n, PAIRS_PART)
                at = 0
                for i in range(TOPK // 2):
                    m = ROWS_OF[i]
                    nc.vector.tensor_scalar(cand[:, at:at + m], top[:, 1, 0:m], top[:, 0, i:i + 1], None, ALU.add)
                    nc.vector.tensor_scalar(expert[:, at:at + m], ixf[:, 1, 0:m], ixf[:, 0, i:i + 1], None, ALU.add)
                    at += m
                nc.vector.tensor_scalar(expert[:, at:], ixf[:, 0, 8:16], ixf[:, 1, 0:1], None, ALU.add)
                own.step(nc.vector.tensor_scalar(cand[:, at:], top[:, 0, 8:16], top[:, 1, 0:1], None, ALU.add))
                hold()
                own.step(nc.vector.max(best[:, 0:8], cand[:]))
                hold()
                nc.vector.max_index(place[:, 0:8], best[:, 0:8], cand[:])
                own.step(nc.vector.match_replace(cand2[:], best[:, 0:8], cand[:], LOW))
                hold()
                own.step(nc.vector.max(best[:, 8:16], cand2[:]))
                nc.vector.tensor_scalar(neg[:], best[:, 0:1], -1.0, None, ALU.mult).then_inc(best_ready, 1)
                hold()
                own.done(nc.vector.max_index(place[:, 8:16], best[:, 8:16], cand2[:]))
                own.done(nc.vector.tensor_copy(placef[:], place[:]))
                check()

            def route_experts(n, b, last):
                own, hold, check = part_own(n, EXPERTS_PART)
                own.done(nc.vector.tensor_tensor(hit[:], count[:].unsqueeze(1).to_broadcast([P, TOPK, NCAND]),
                                                 placef[:].unsqueeze(2).to_broadcast([P, TOPK, NCAND]), ALU.is_equal))
                own.done(nc.vector.tensor_tensor(hit[:], hit[:], expert[:].unsqueeze(1).to_broadcast([P, TOPK, NCAND]),
                                                 ALU.mult))
                own.step(nc.vector.tensor_reduce(chosen[:], hit[:], AX.X, ALU.add))
                if last is not None:
                    dve.wait_ge(index_taken, past(last + 1))
                    dve.wait_ge(gate_taken, past(last + 1))
                hold()
                nc.vector.tensor_copy(index[:, bass.ds(b, 1), :].rearrange("p o k -> p (o k)"), chosen[:])
                dve.wait_ge(gates_ready, past(n + 1))
                own.done(nc.vector.reciprocal(gsum[:], gsum[:]))
                nc.vector.tensor_scalar(gate[:, bass.ds(b, 1), :].rearrange("p o k -> p (o k)"), gx[:], gsum[:], None,
                                        ALU.mult).then_inc(routed, 1)
                check()

            def route(n, h, b, last, part):
                if part in (ALL, KEYS_PART):
                    route_keys(n)
                if part in (ALL, PAIRS_PART):
                    route_pairs(n)
                if part in (ALL, EXPERTS_PART):
                    route_experts(n, b, last)

            def finish(b):
                dve.wait_ge(f_squared, past(b + 1))
                nc.vector.tensor_scalar(fss[:], fss[:], 1.0 / D, EPS, ALU.mult, ALU.add).then_inc(f_meaned, 1)
                dve.wait_ge(f_rooted, past(b + 1))
                nc.vector.reciprocal(frs[:], frs[:]).then_inc(f_inverse, 1)
                dve.wait_ge(f_inverse, past(b + 1))
                dve.sem_inc(dve_turn, 1)
                nc.vector.scalar_tensor_tensor(out=result[:], in0=Y[:, bass.ds(b, 1), 0:D].rearrange("p o d -> p (o d)"),
                                               scalar=frs[:], in1=fw[:], op0=ALU.mult, op1=ALU.mult).then_inc(f_normed, 1)

            def gather(n, b, route_next, finish_last):
                for k in range(TOPK):
                    s = k % RING
                    if finish_last and k == TOPK * 3 // 4:
                        finish(b - 1)
                    if route_next and k == TOPK // 4:
                        route_next(KEYS_PART)
                    if route_next and k == TOPK // 2:
                        route_next(PAIRS_PART)
                    dve.wait_ge(got[s], (n * 2 + k // RING + 1) * 16)
                    dve.wait_ge(dot_ready, past(n * TOPK + k))
                    if k % BATCH == 0:
                        dve.wait_ge(diag_ready, past(n * TOPK))
                    nc.vector.scalar_tensor_tensor(
                        out=junk[:], in0=ring[:, s, 0:D], scalar=1.0,
                        in1=Y[:, bass.ds(b, 1), D:MIX].rearrange("p o d -> p (o d)"),
                        op0=ALU.mult, op1=ALU.mult, accum_out=dots[:, k:k + 1]).then_inc(dot_ready, 1)
                if route_next:
                    route_next(EXPERTS_PART)
                dve.wait_ge(free_slots, RING + (n + 1) * TOPK)
                hb = Y[:, bass.ds(b, 1), 0:D].rearrange("p o d -> p (o d)")
                nc.vector.tensor_tensor(hb, hb, ps_o[:].rearrange("p a c -> p (a c)"), ALU.add).then_inc(added, 1)

            dve.wait_ge(fw_in, 16)
            loops(dve, route, gather)
            finish(NB - 1)


def block_program(nc, x, ln_w, w_ssd, par, w_hg, lb_logits, w_out, mix_w, ffn_w, w_query, keys, table, fin_w, out):
    with ExitStack() as ctx:
        C = {n: ctx.enter_context(nc.sbuf_tensor(n, [P, P], F32)) for n in ("ident", "ones", "tri", "below")}
        hnT = ctx.enter_context(nc.sbuf_tensor("hnT", [P, KT, SEQ], F32))
        Y = ctx.enter_context(nc.sbuf_tensor("Y", [P, NB, MIX], F32))
        osq = ctx.enter_context(nc.sbuf_tensor("osq", [P, NB, HEADS], F32))
        ysq = ctx.enter_context(nc.sbuf_tensor("ysq", [P, NB], F32))
        with nc.sbuf_tensor("reset", [P, SEQ], F32) as reset, nc.sbuf_tensor("lmask", [P, LEVELS + 1, P], F32) as lmask:
            C["reset"], C["lmask"] = reset, lmask
            with nc.sbuf_tensor("w_group", [P, KT, SSD_COLS], F32) as w_group, ExitStack() as sems:
                group_in = [sems.enter_context(nc.semaphore(f"group_in{i}")) for i in range(len(SSD_PARTS))]
                input_norm(nc, x, ln_w, w_ssd, C, hnT, w_group, group_in)
                ssd(nc, w_group, group_in, w_ssd, par, w_hg, C, hnT, Y)
            hgrn(nc, w_hg, lb_logits, C, hnT, Y, osq, ysq)
        wq = ctx.enter_context(nc.sbuf_tensor("wq", [P, KT, 2 * P], F32))
        wq_in = ctx.enter_context(nc.semaphore("wq_in"))
        mix_out(nc, x, w_out, mix_w, ffn_w, w_query, C, Y, osq, ysq, hnT, wq, wq_in)
        peer(nc, w_query, keys, table, fin_w, C, Y, hnT, wq, wq_in, out)


def laid_out(inputs):
    import numpy as np

    def first(name):
        return np.asarray(inputs[name])[0]

    inner, bc = GROUPS * XW, GROUPS * P
    w = first("w_in").reshape(KT, P, -1).transpose(1, 0, 2)
    at_x, at_dt = inner, 2 * inner + 2 * bc
    at_q = at_dt + GROUPS * HPG
    conv = np.concatenate([first("conv_w"), first("conv_b")[None]], 0)
    w_ssd, par = [], []
    for g in range(GROUPS):
        ch = np.concatenate([np.arange(g * XW, (g + 1) * XW), inner + g * P + np.arange(P),
                             inner + bc + g * P + np.arange(P)])
        w_ssd.append(np.concatenate([w[:, :, at_x + ch], w[:, :, g * XW:(g + 1) * XW],
                                     w[:, :, at_dt + g * HPG:at_dt + (g + 1) * HPG]], 2))
        taps = conv[:, ch].reshape(TAPS + 1, CT, P).transpose(2, 1, 0).reshape(P, CT * (TAPS + 1))
        heads = [np.broadcast_to(first(n)[g * HPG:(g + 1) * HPG], (P, HPG)) for n in ("dt_bias", "a_log", "d_skip")]
        par.append(np.concatenate([taps, *heads], 1))
    w_hg = [np.concatenate([w[:, :, at_q + j * D + h * P:at_q + j * D + (h + 1) * P] for j in range(4)], 2)
            for h in range(HEADS)]
    return {
        "x": np.asarray(inputs["x"]),
        "ln_w": first("ln_mix_w").reshape(KT, P).T,
        "w_ssd": np.stack(w_ssd),
        "par": np.stack(par, 1),
        "w_hg": np.stack(w_hg),
        "lb_logits": np.asarray(inputs["lb_logits"]).reshape(2, HEADS, P).transpose(2, 0, 1),
        "w_out": first("w_out").reshape(MT, P, D).transpose(1, 0, 2),
        "mix_w": np.concatenate([first("ssd_norm_w"), first("hg_norm_w")]).reshape(MT, P).T,
        "ffn_w": np.broadcast_to(first("ln_ffn_w"), (P, D)),
        "w_query": first("w_query").reshape(KT, P, PH, 2 * P).transpose(2, 1, 0, 3),
        "keys": first("sub_keys").transpose(3, 0, 1, 2).reshape(P, PH * 2 * KEYS),
        "table": np.concatenate([first("u_table"), first("v_table")], 1),
        "fin_w": np.broadcast_to(np.asarray(inputs["ln_final_w"]), (P, D)),
    }


def kernel(**inputs):
    import numpy as np
    import concourse.bacc as bacc
    from concourse.bass_utils import run_bass_kernel_spmd

    nc = bacc.Bacc("TRN2", target_bir_lowering=False, num_devices=1)
    arrays = {n: np.ascontiguousarray(a) for n, a in laid_out(inputs).items()}
    args = {n: nc.dram_tensor("in_" + n, a.shape, mybir.dt.from_np(a.dtype), kind="ExternalInput").ap()
            for n, a in arrays.items()}
    out = nc.dram_tensor("out_0", [1, SEQ, D], F32, kind="ExternalOutput").ap()
    block_program(nc, out=out, **args)
    r = run_bass_kernel_spmd(nc, [{"in_" + n: a for n, a in arrays.items()}], core_ids=[0])
    return r.results[0]["out_0"]
```
